# Optimizing a Trainium2 kernel written in Bass

```python
import jax
import jax.numpy as jnp
from jax import lax
import numpy as np
import jax, jax.numpy as jnp

D_MODEL = 1024
BATCH = 1
SEQ = 256
DEPTH = 1

GRID_W = 64
CTX_LEN = 256

A_HEADS = 8
A_HEAD_DIM = 64
D_A = A_HEADS * A_HEAD_DIM
LORA_W = 64
LORA_A = 64
LORA_G = 128

B_HEADS = 8
B_HEAD_DIM = 64
D_B = B_HEADS * B_HEAD_DIM
WIN_H = 8
WIN_W = 16

N_EXPERTS = 16
N_GROUPS = 4
EXPERTS_PER_GROUP = N_EXPERTS // N_GROUPS
TOP_K = 2
D_EXPERT = 512

RMS_EPS = 1e-6
GN_EPS = 64e-5

IN_SPLITS = (D_A, D_A, D_A, 2 * LORA_W, 2 * LORA_A, LORA_G, D_B, D_B, D_B, D_MODEL, D_MODEL)
IN_COLS = sum(IN_SPLITS)
IN_OFFSETS = tuple(int(o) for o in np.cumsum(IN_SPLITS)[:-1])


def rms_norm(x, g):
    xf = x.astype(jnp.float32)
    y = xf * lax.rsqrt(jnp.mean(xf * xf, axis=-1, keepdims=True) + RMS_EPS)
    return (y * g.astype(jnp.float32)).astype(x.dtype)

def modulate(h, shift, scale):
    return h * (1.0 + scale) + shift

def split_cols(z):
    return jnp.split(z, IN_OFFSETS, axis=-1)

def rwkv_prep(z, w0, w_lora_b, a0, a_lora_b, k_k, k_a):
    f = jnp.float32
    k, v, lw, la = z[1].astype(f), z[2].astype(f), z[3].astype(f), z[4].astype(f)
    bsz, t = k.shape[:2]
    heads = lambda u: u.reshape(bsz, t, A_HEADS, A_HEAD_DIM)
    lw = jnp.tanh(lw).reshape(bsz, t, 2, LORA_W)
    wl = w0.astype(f) + jnp.einsum('btzr,zrc->btzc', lw, w_lora_b.astype(f))
    decay = jnp.exp(-jnp.exp(-jax.nn.softplus(-wl) - 0.5))
    la = la.reshape(bsz, t, 2, LORA_A)
    a = jax.nn.sigmoid(a0.astype(f) + jnp.einsum('btzr,zrc->btzc', la, a_lora_b.astype(f)))
    kk = heads(k * k_k.astype(f))
    kk = kk * lax.rsqrt(jnp.maximum(jnp.sum(kk * kk, axis=-1, keepdims=True), 1e-12))
    k_dir = k[:, :, None, :] * (1.0 + (a - 1.0) * k_a.astype(f))
    per_dir = [(heads(decay[:, :, d]), heads(k_dir[:, :, d]), heads(a[:, :, d])) for d in range(2)]
    return heads(k), heads(v), kk, per_dir

def rwkv_scan(s0, r, decay, k, v, kk, a, reverse, emit):
    def step(s, inp):
        w_t, k_t, v_t, kk_t, a_t = inp[:5]
        s_kk = jnp.einsum('bhvk,bhk->bhv', s, kk_t)
        s = (s * w_t[:, :, None, :]
             - s_kk[..., None] * (kk_t * a_t)[:, :, None, :]
             + v_t[..., None] * k_t[:, :, None, :])
        y = jnp.einsum('bhvk,bhk->bhv', s, inp[5]) if emit else None
        return s, y
    seq = (decay, k, v, kk, a) + ((r,) if emit else ())
    xs = tuple(jnp.moveaxis(u, 1, 0) for u in seq)
    s_final, ys = lax.scan(step, s0, xs, reverse=reverse)
    return s_final, (jnp.moveaxis(ys, 0, 1) if emit else None)

def rwkv_out(y, r, k, v, lg, r_k, g_lora_b, ln_g, ln_b, out_dtype):
    f = jnp.float32
    bsz, t = y.shape[:2]
    mu = jnp.mean(y, axis=-1, keepdims=True)
    var = jnp.mean(jnp.square(y - mu), axis=-1, keepdims=True)
    yn = ((y - mu) * lax.rsqrt(var + GN_EPS)).reshape(bsz, t, D_A) * ln_g.astype(f) + ln_b.astype(f)
    bonus = (jnp.sum(r * k * r_k.astype(f), axis=-1, keepdims=True) * v).reshape(bsz, t, D_A)
    g = jax.nn.sigmoid(lg.astype(f)) @ g_lora_b.astype(f)
    return ((yn + bonus) * g).astype(out_dtype)

def rwkv_mixer(z_c, z_x, w0, w_lora_b, a0, a_lora_b, g_lora_b, k_k, k_a, r_k, ln_g, ln_b, emit_ctx):
    f = jnp.float32
    k_c, v_c, kk_c, dir_c = rwkv_prep(z_c, w0, w_lora_b, a0, a_lora_b, k_k, k_a)
    k_x, v_x, kk_x, dir_x = rwkv_prep(z_x, w0, w_lora_b, a0, a_lora_b, k_k, k_a)
    bsz, seq = z_x[0].shape[:2]
    r_x = z_x[0].astype(f).reshape(bsz, seq, A_HEADS, A_HEAD_DIM)
    r_c = z_c[0].astype(f).reshape(bsz, z_c[0].shape[1], A_HEADS, A_HEAD_DIM) if emit_ctx else None
    y_x, y_c = 0.0, 0.0
    for d in range(2):
        rev = d == 1
        s0 = jnp.zeros((bsz, A_HEADS, A_HEAD_DIM, A_HEAD_DIM), f)
        w_c, kd_c, a_c = dir_c[d]
        s_c, yc_d = rwkv_scan(s0, r_c, w_c, kd_c, v_c, kk_c, a_c, rev, emit_ctx)
        w_x, kd_x, a_x = dir_x[d]
        _, yx_d = rwkv_scan(s_c, r_x, w_x, kd_x, v_x, kk_x, a_x, rev, True)
        y_x = y_x + yx_d
        if emit_ctx:
            y_c = y_c + yc_d
    out_x = rwkv_out(y_x, r_x, k_x, v_x, z_x[5], r_k, g_lora_b, ln_g, ln_b, z_x[0].dtype)
    out_c = rwkv_out(y_c, r_c, k_c, v_c, z_c[5], r_k, g_lora_b, ln_g, ln_b, z_c[0].dtype) if emit_ctx else None
    return out_c, out_x

def na_mixer(z_c, z_x, q_g, k_g, rpb, need_ctx):
    f = jnp.float32
    scale = B_HEAD_DIM ** -0.5

    def heads(u):
        bsz, t = u.shape[:2]
        return u.reshape(bsz, t, B_HEADS, B_HEAD_DIM).transpose(0, 2, 1, 3)

    k_c, v_c = rms_norm(heads(z_c[7]), k_g), heads(z_c[8])
    q_x = rms_norm(heads(z_x[6]), q_g) * scale
    k_x, v_x = rms_norm(heads(z_x[7]), k_g), heads(z_x[8])
    bsz, _, seq, _ = q_x.shape
    rows = seq // GRID_W
    kh = min(WIN_H, rows)
    kw = WIN_W
    grid = lambda u: u.reshape(bsz, B_HEADS, rows, GRID_W, B_HEAD_DIM)
    q_grid, k_grid, v_grid = grid(q_x), grid(k_x), grid(v_x)

    i = jnp.arange(rows)
    key_rows = jnp.clip(i - kh // 2, 0, rows - kh)[:, None] + jnp.arange(kh)[None, :]
    k_blk = k_grid[:, :, key_rows]
    v_blk = v_grid[:, :, key_rows]
    s_lat = jnp.einsum('bhiqd,bhiakd->bhiqak', q_grid, k_blk).astype(f)

    j = jnp.arange(GRID_W)
    col_start = jnp.clip(j - kw // 2, 0, GRID_W - kw)
    in_win = (j[None, :] >= col_start[:, None]) & (j[None, :] < col_start[:, None] + kw)
    d_row = key_rows - i[:, None] + (WIN_H - 1)
    d_col = jnp.clip(j[None, :] - j[:, None], -(WIN_W - 1), WIN_W - 1) + (WIN_W - 1)
    bias = rpb[:, d_row[:, None, :, None], d_col[None, :, None, :]].astype(f)
    s_lat = jnp.where(in_win[:, None, :], s_lat + bias[None], -jnp.inf)

    s_ctx = jnp.einsum('bhiqd,bhcd->bhiqc', q_grid, k_c).astype(f)
    n_lat = kh * GRID_W
    logits = jnp.concatenate([s_lat.reshape(bsz, B_HEADS, rows, GRID_W, n_lat), s_ctx], axis=-1)
    p = jax.nn.softmax(logits, axis=-1).astype(v_x.dtype)
    p_lat = p[..., :n_lat].reshape(bsz, B_HEADS, rows, GRID_W, kh, GRID_W)
    o = (jnp.einsum('bhiqak,bhiakd->bhiqd', p_lat, v_blk)
         + jnp.einsum('bhiqc,bhcd->bhiqd', p[..., n_lat:], v_c))
    y_x = o.transpose(0, 2, 3, 1, 4).reshape(bsz, seq, D_B)

    y_c = None
    if need_ctx:
        q_c = rms_norm(heads(z_c[6]), q_g) * scale
        p_c = jax.nn.softmax(jnp.einsum('bhqd,bhkd->bhqk', q_c, k_c).astype(f), axis=-1).astype(v_c.dtype)
        y_c = jnp.einsum('bhqk,bhkd->bhqd', p_c, v_c).transpose(0, 2, 1, 3).reshape(bsz, -1, D_B)
    return y_c, y_x

def branch_merge(gate_a, gate_b, y_a, y_b, proj_a, proj_b, w_out):
    merged = jax.nn.sigmoid(gate_a) * (y_a @ proj_a) + jax.nn.sigmoid(gate_b) * (y_b @ proj_b)
    return merged @ w_out

def moe(h, router_w, router_bias, w1, w3, w2):
    f = jnp.float32
    shp = h.shape
    t = h.reshape(-1, shp[-1])
    n = t.shape[0]
    scores = jax.nn.sigmoid(t.astype(f) @ router_w.astype(f))
    sel = scores + router_bias.astype(f)
    grp_score = lax.top_k(sel.reshape(n, N_GROUPS, EXPERTS_PER_GROUP), TOP_K)[0].sum(-1)
    best = jnp.argmax(grp_score, axis=-1)
    in_group = (jnp.arange(N_EXPERTS) // EXPERTS_PER_GROUP)[None, :] == best[:, None]
    _, top_idx = lax.top_k(jnp.where(in_group, sel, -jnp.inf), TOP_K)
    top_s = jnp.take_along_axis(scores, top_idx, axis=-1)
    wts = top_s / jnp.sum(top_s, axis=-1, keepdims=True)
    gate = jnp.sum(jax.nn.one_hot(top_idx, N_EXPERTS, dtype=f) * wts[..., None], axis=1).astype(t.dtype)
    out = jnp.zeros_like(t)
    for e in range(N_EXPERTS):
        hid = jax.nn.silu(t @ w1[e]) * (t @ w3[e])
        out = out + gate[:, e:e + 1] * (hid @ w2[e])
    return out.reshape(shp)

def first_inputs(seed: int = 0) -> dict:
    key = jax.random.key(seed)
    ks = iter(jax.random.split(key, 40))
    D = D_MODEL

    def nrm(shape, s):
        return jax.random.normal(next(ks), shape, jnp.float32) * s

    inp = {}
    inp['x'] = nrm((BATCH, SEQ, D), 1.0)
    inp['c'] = nrm((BATCH, D), 1.0)
    inp['ctx'] = nrm((BATCH, CTX_LEN, D), 1.0)
    inp['c_ctx'] = nrm((D,), 1.0)
    inp['mod_w'] = nrm((DEPTH, D, 6 * D), 0.5 * D ** -0.5)
    inp['mod_b'] = nrm((DEPTH, 6 * D), 0.02)
    inp['norm1_g'] = 1.0 + nrm((DEPTH, D), 0.05)
    inp['norm2_g'] = 1.0 + nrm((DEPTH, D), 0.05)
    inp['w_in'] = nrm((DEPTH, D, IN_COLS), D ** -0.5)
    inp['rw_w0'] = jax.random.uniform(next(ks), (DEPTH, 2, D_A), jnp.float32, -6.0, 1.0)
    inp['rw_w_lora_b'] = nrm((DEPTH, 2, LORA_W, D_A), 0.5 * LORA_W ** -0.5)
    inp['rw_a0'] = nrm((DEPTH, 2, D_A), 0.5)
    inp['rw_a_lora_b'] = nrm((DEPTH, 2, LORA_A, D_A), 0.5 * LORA_A ** -0.5)
    inp['rw_g_lora_b'] = nrm((DEPTH, LORA_G, D_A), LORA_G ** -0.5)
    inp['rw_k_k'] = 0.85 + nrm((DEPTH, D_A), 0.05)
    inp['rw_k_a'] = 1.0 + nrm((DEPTH, D_A), 0.05)
    inp['rw_r_k'] = nrm((DEPTH, A_HEADS, A_HEAD_DIM), 0.1)
    inp['rw_ln_g'] = 1.0 + nrm((DEPTH, D_A), 0.05)
    inp['rw_ln_b'] = nrm((DEPTH, D_A), 0.02)
    inp['na_q_g'] = 1.0 + nrm((DEPTH, B_HEAD_DIM), 0.1)
    inp['na_k_g'] = 1.0 + nrm((DEPTH, B_HEAD_DIM), 0.1)
    inp['na_rpb'] = nrm((DEPTH, B_HEADS, 2 * WIN_H - 1, 2 * WIN_W - 1), 0.5)
    inp['proj_a'] = nrm((DEPTH, D_A, D), D_A ** -0.5)
    inp['proj_b'] = nrm((DEPTH, D_B, D), D_B ** -0.5)
    inp['w_out'] = nrm((DEPTH, D, D), D ** -0.5)
    inp['router_w'] = nrm((D, N_EXPERTS), D ** -0.5)
    inp['router_bias'] = nrm((N_EXPERTS,), 0.01)
    inp['moe_w1'] = nrm((DEPTH, N_EXPERTS, D, D_EXPERT), D ** -0.5)
    inp['moe_w3'] = nrm((DEPTH, N_EXPERTS, D, D_EXPERT), D ** -0.5)
    inp['moe_w2'] = nrm((DEPTH, N_EXPERTS, D_EXPERT, D), D_EXPERT ** -0.5)
    return inp

def first_block(x, c, ctx, c_ctx, mod_w, mod_b, norm1_g, norm2_g, w_in,
              rw_w0, rw_w_lora_b, rw_a0, rw_a_lora_b, rw_g_lora_b, rw_k_k, rw_k_a, rw_r_k,
              rw_ln_g, rw_ln_b, na_q_g, na_k_g, na_rpb, proj_a, proj_b, w_out,
              router_w, router_bias, moe_w1, moe_w3, moe_w2):
    for l in range(DEPTH):
        last = l == DEPTH - 1
        m_x = [m[:, None, :] for m in jnp.split(jax.nn.silu(c) @ mod_w[l] + mod_b[l], 6, axis=-1)]
        m_c = jnp.split(jax.nn.silu(c_ctx) @ mod_w[l] + mod_b[l], 6, axis=-1)

        h_x = modulate(rms_norm(x, norm1_g[l]), m_x[0], m_x[1])
        h_c = modulate(rms_norm(ctx, norm1_g[l]), m_c[0], m_c[1])
        z_x = split_cols(h_x @ w_in[l])
        z_c = split_cols(h_c @ w_in[l])
        ya_c, ya_x = rwkv_mixer(z_c, z_x, rw_w0[l], rw_w_lora_b[l], rw_a0[l], rw_a_lora_b[l],
                                rw_g_lora_b[l], rw_k_k[l], rw_k_a[l], rw_r_k[l], rw_ln_g[l], rw_ln_b[l],
                                emit_ctx=not last)
        yb_c, yb_x = na_mixer(z_c, z_x, na_q_g[l], na_k_g[l], na_rpb[l], need_ctx=not last)
        x = x + m_x[2] * branch_merge(z_x[9], z_x[10], ya_x, yb_x, proj_a[l], proj_b[l], w_out[l])

        h2_x = modulate(rms_norm(x, norm2_g[l]), m_x[3], m_x[4])
        x = x + m_x[5] * moe(h2_x, router_w, router_bias, moe_w1[l], moe_w3[l], moe_w2[l])

        if not last:
            ctx = ctx + m_c[2] * branch_merge(z_c[9], z_c[10], ya_c, yb_c, proj_a[l], proj_b[l], w_out[l])
            h2_c = modulate(rms_norm(ctx, norm2_g[l]), m_c[3], m_c[4])
            ctx = ctx + m_c[5] * moe(h2_c, router_w, router_bias, moe_w1[l], moe_w3[l], moe_w2[l])
    return x


DEPTH_2 = 2

HEAD_DIM = 64
POOL_WIDTH = D_MODEL // 4
POOL_WINDOWS = (2, 4, 8, 16)
N_POOL_GROUPS = len(POOL_WINDOWS)
POOL_GC = POOL_WIDTH // N_POOL_GROUPS
ATTN_WIDTH = D_MODEL - POOL_WIDTH
N_ATTN_HEADS = ATTN_WIDTH // HEAD_DIM
DIL_PATTERNS = ((128, 1), (512, 4), (2048, 16))
HEADS_PER_PATTERN = N_ATTN_HEADS // len(DIL_PATTERNS)
ROT_DIM = HEAD_DIM // 4
ROPE_THETA = 500000.0
BLK = 128
D_FF = 4 * D_MODEL
PLE_DIM = 256
EPS = 1e-6


def rmsnorm(x, g):
    xf = x.astype(jnp.float32)
    y = xf * lax.rsqrt(jnp.mean(xf * xf, axis=-1, keepdims=True) + EPS)
    return (y * g.astype(jnp.float32)).astype(x.dtype)

def rotary_tables(positions, dtype):
    inv_freq = ROPE_THETA ** (-jnp.arange(0, ROT_DIM, 2, dtype=jnp.float32) / ROT_DIM)
    ang = positions.astype(jnp.float32)[..., None] * inv_freq
    return jnp.cos(ang)[:, :, None, :].astype(dtype), jnp.sin(ang)[:, :, None, :].astype(dtype)

def apply_partial_rotary(x, cos, sin):
    half = ROT_DIM // 2
    x1 = x[..., :half]
    x2 = x[..., half:ROT_DIM]
    rot = jnp.concatenate([x1 * cos - x2 * sin, x2 * cos + x1 * sin], axis=-1)
    return jnp.concatenate([rot, x[..., ROT_DIM:]], axis=-1)

def pool_mixer(u, w, scale):
    B, S, _ = u.shape
    ug = u.reshape(B, S, N_POOL_GROUPS, POOL_GC).astype(jnp.float32)
    c = lax.cumsum(ug, axis=1)
    c0 = jnp.pad(c, ((0, 0), (1, 0), (0, 0), (0, 0)))
    t = jnp.arange(S, dtype=jnp.int32)
    win = jnp.array(POOL_WINDOWS, dtype=jnp.int32)
    lo = jnp.maximum(t[:, None] + 1 - win[None, :], 0)
    c_lo = jnp.take_along_axis(c0, lo[None, :, :, None], axis=1)
    cnt = (t[:, None] + 1 - lo).astype(jnp.float32)
    y = ((c - c_lo) / cnt[None, :, :, None] - ug).astype(u.dtype)
    y = jnp.einsum('bsgc,gcd->bsgd', y, w).reshape(B, S, POOL_WIDTH)
    return y * scale

def dilated_window_attention(q, k, v, window, dil):
    B, S, H, Dh = q.shape
    steps = window // dil
    L = -(-S // (dil * BLK)) * BLK
    pad = L * dil - S
    nb = L // BLK

    def to_strided(a):
        a = jnp.pad(a, ((0, 0), (0, pad), (0, 0), (0, 0)))
        a = a.reshape(B, L, dil, H, Dh).transpose(0, 2, 1, 3, 4)
        return a.reshape(B, dil, nb, BLK, H, Dh)

    def with_prev(a):
        prev = jnp.pad(a[:, :, :-1], ((0, 0), (0, 0), (1, 0), (0, 0), (0, 0), (0, 0)))
        return jnp.concatenate([prev, a], axis=3)

    qs = to_strided(q)
    kb = with_prev(to_strided(k))
    vb = with_prev(to_strided(v))
    s = jnp.einsum('brnqhd,brnkhd->brnhqk', qs, kb,
                   preferred_element_type=jnp.float32) * (HEAD_DIM ** -0.5)
    qi = jnp.arange(nb)[:, None] * BLK + jnp.arange(BLK)[None, :]
    ki = jnp.arange(nb)[:, None] * BLK - BLK + jnp.arange(2 * BLK)[None, :]
    dist = qi[:, :, None] - ki[:, None, :]
    valid = (dist >= 0) & (dist <= steps) & (ki[:, None, :] >= 0)
    s = jnp.where(valid[None, None, :, None], s, -jnp.inf)
    m = jnp.max(s, axis=-1, keepdims=True)
    e = jnp.exp(s - m)
    l = jnp.sum(e, axis=-1, keepdims=True)
    o = jnp.einsum('brnhqk,brnkhd->brnqhd', e / l, vb.astype(jnp.float32))
    lse = (m + jnp.log(l))[..., 0]
    o = o.reshape(B, dil, L, H, Dh).transpose(0, 2, 1, 3, 4).reshape(B, L * dil, H, Dh)[:, :S]
    lse = lse.transpose(0, 1, 2, 4, 3).reshape(B, dil, L, H).transpose(0, 2, 1, 3)
    lse = lse.reshape(B, L * dil, H)[:, :S]
    return o, lse

def dilated_mixer(q, k, v):
    outs, lses = [], []
    for g, (window, dil) in enumerate(DIL_PATTERNS):
        sl = slice(g * HEADS_PER_PATTERN, (g + 1) * HEADS_PER_PATTERN)
        o, lse = dilated_window_attention(q[:, :, sl], k[:, :, sl], v[:, :, sl], window, dil)
        outs.append(o)
        lses.append(lse)
    wts = jax.nn.softmax(jnp.stack(lses, axis=0), axis=0)
    o = jnp.concatenate([outs[g] * wts[g][..., None] for g in range(len(DIL_PATTERNS))], axis=2)
    B, S = q.shape[0], q.shape[1]
    return o.reshape(B, S, ATTN_WIDTH).astype(q.dtype)

def second_inputs(seed: int = 0) -> dict:
    key = jax.random.key(seed)
    ks = jax.random.split(key, 16)
    f32 = jnp.float32
    n_in = POOL_WIDTH + 3 * ATTN_WIDTH
    return {
        "x": jax.random.normal(ks[0], (BATCH, SEQ, D_MODEL), f32),
        "p": jax.random.normal(ks[1], (DEPTH_2, BATCH, SEQ, PLE_DIM), f32),
        "positions": jnp.broadcast_to(jnp.arange(SEQ, dtype=jnp.int32), (BATCH, SEQ)),
        "norm1": 1.0 + 0.02 * jax.random.normal(ks[2], (DEPTH_2, D_MODEL), f32),
        "w_in": jax.random.normal(ks[3], (DEPTH_2, D_MODEL, n_in), f32) * D_MODEL ** -0.5,
        "pool_w": jax.random.normal(ks[4], (DEPTH_2, N_POOL_GROUPS, POOL_GC, POOL_GC), f32) * POOL_GC ** -0.5,
        "pool_scale": 1.0 + 0.02 * jax.random.normal(ks[5], (DEPTH_2, POOL_WIDTH), f32),
        "w_out": jax.random.normal(ks[6], (DEPTH_2, POOL_WIDTH + ATTN_WIDTH, D_MODEL), f32) * (POOL_WIDTH + ATTN_WIDTH) ** -0.5,
        "norm2": 1.0 + 0.02 * jax.random.normal(ks[7], (DEPTH_2, D_MODEL), f32),
        "w_up": jax.random.normal(ks[8], (DEPTH_2, D_MODEL, D_FF), f32) * D_MODEL ** -0.5,
        "w_down": jax.random.normal(ks[9], (DEPTH_2, D_FF, D_MODEL), f32) * D_FF ** -0.5,
        "norm3": 1.0 + 0.02 * jax.random.normal(ks[10], (DEPTH_2, D_MODEL), f32),
        "w_gate": jax.random.normal(ks[11], (DEPTH_2, D_MODEL, D_MODEL), f32) * D_MODEL ** -0.5,
        "w_ple": jax.random.normal(ks[12], (DEPTH_2, PLE_DIM, D_MODEL), f32) * PLE_DIM ** -0.5,
        "final_norm": 1.0 + 0.02 * jax.random.normal(ks[13], (D_MODEL,), f32),
    }

def second_block(x, p, positions, norm1, w_in, pool_w, pool_scale, w_out, norm2, w_up, w_down,
              norm3, w_gate, w_ple, final_norm):
    B, S, _ = x.shape
    cos, sin = rotary_tables(positions, x.dtype)
    h = x
    for i in range(DEPTH_2):
        hn = rmsnorm(h, norm1[i])
        z = hn @ w_in[i]
        u = z[..., :POOL_WIDTH]
        q, k, v = jnp.split(z[..., POOL_WIDTH:], 3, axis=-1)
        q = apply_partial_rotary(q.reshape(B, S, N_ATTN_HEADS, HEAD_DIM), cos, sin)
        k = apply_partial_rotary(k.reshape(B, S, N_ATTN_HEADS, HEAD_DIM), cos, sin)
        v = v.reshape(B, S, N_ATTN_HEADS, HEAD_DIM)
        pool_out = pool_mixer(u, pool_w[i], pool_scale[i])
        attn_out = dilated_mixer(q, k, v)
        h = h + jnp.concatenate([pool_out, attn_out], axis=-1) @ w_out[i]
        hn = rmsnorm(h, norm2[i])
        h = h + jnp.square(jax.nn.relu(hn @ w_up[i])) @ w_down[i]
        gate = jax.nn.sigmoid(rmsnorm(h, norm3[i]) @ w_gate[i])
        h = h + gate * (p[i] @ w_ple[i])
    return rmsnorm(h, final_norm)


def setup_inputs(seed=0):
    out = dict(first_inputs(seed))
    for name, value in second_inputs(seed + 1).items():
        if name != "x":
            out[name + "_2"] = value
    return out


def reference(
    x, c, ctx, c_ctx, mod_w, mod_b, norm1_g, norm2_g, w_in, rw_w0, rw_w_lora_b, rw_a0,
    rw_a_lora_b, rw_g_lora_b, rw_k_k, rw_k_a, rw_r_k, rw_ln_g, rw_ln_b, na_q_g, na_k_g, na_rpb,
    proj_a, proj_b, w_out, router_w, router_bias, moe_w1, moe_w3, moe_w2, p_2, positions_2,
    norm1_2, w_in_2, pool_w_2, pool_scale_2, w_out_2, norm2_2, w_up_2, w_down_2, norm3_2,
    w_gate_2, w_ple_2, final_norm_2,
):
    x = first_block(
        x, c, ctx, c_ctx, mod_w, mod_b, norm1_g, norm2_g, w_in, rw_w0, rw_w_lora_b, rw_a0,
        rw_a_lora_b, rw_g_lora_b, rw_k_k, rw_k_a, rw_r_k, rw_ln_g, rw_ln_b, na_q_g, na_k_g,
        na_rpb, proj_a, proj_b, w_out, router_w, router_bias, moe_w1, moe_w3, moe_w2,
    )
    return second_block(
        x, p_2, positions_2, norm1_2, w_in_2, pool_w_2, pool_scale_2, w_out_2, norm2_2, w_up_2,
        w_down_2, norm3_2, w_gate_2, w_ple_2, final_norm_2,
    )


_drawn_inputs = setup_inputs


def setup_inputs(seed=0):
    import zlib

    import numpy as np

    out = dict(_drawn_inputs(seed))
    spreads = {}
    factors = {'rw_w_lora_b': 5.422,
     'rw_k_k': 2.828,
     'rw_k_a': 3.783,
     'rw_ln_g': 3.91,
     'rw_ln_b': 7.392,
     'na_q_g': 8.0,
     'na_k_g': 8.0,
     'na_rpb': 3.584,
     'norm1_2': 5.631,
     'pool_scale_2': 5.9,
     'norm2_2': 8.029,
     'norm3_2': 200.0,
     'final_norm_2': 21.448,
     'p_2': 4.937,
     'w_gate_2': 7.021,
     'w_ple_2': 4.935}
    for name, (base, spread) in spreads.items():
        noise = np.random.default_rng([zlib.crc32(name.encode()), seed]).standard_normal(out[name].shape)
        drawn = base * np.exp(spread * noise) if base else spread * noise
        out[name] = jnp.asarray(drawn.astype(out[name].dtype))
    for name, factor in factors.items():
        out[name] = (out[name] * factor).astype(out[name].dtype)
    return out
```

```python
from contextlib import ExitStack

import concourse.bass as bass
from concourse import mybir

F32 = mybir.dt.float32
F32R = mybir.dt.float32r
I32 = mybir.dt.int32
ALU = mybir.AluOpType
ACT = mybir.ActivationFunctionType
AX = mybir.AxisListType.X

P = 128
KB = 1024


def two_block_kernel(nc, a, out):
    T, D = a["x"].shape[1], a["x"].shape[2]
    KT = D // P
    NT = T // P
    DA = a["rw_w0"].shape[2]
    HD = 64
    H = DA // HD
    PW = 512
    E = a["router_w"].shape[1]
    L2 = a["norm1_2"].shape[0]
    EPS = 1e-6
    NEG = -1e30

    ctx = ExitStack()
    base = (nc.sbuf_base + 63) // 64 * 64

    def sb(name, shape, dt, offset):
        return nc.alloc_sbuf_tensor_at(name, shape, dt, offset=offset)

    class Region:

        def __init__(self, start, size):
            self.at, self.end = start, start + size

        def take(self, name, shape, dt=F32):
            size = 4
            for s in shape[1:]:
                size *= s
            t = sb(name, shape, dt, self.at)
            self.at += (size + 31) // 32 * 32
            assert self.at <= self.end, (name, self.at - self.end)
            return t

    def sem(name):
        return ctx.enter_context(nc.semaphore(name))

    def mod_bc(ap, shape):
        return ap.to_broadcast(shape)

    ring = Region(base, 96 * KB)
    RAW = [ring.take(f"raw{i}", [P, 4096]) for i in range(2)]
    WH = [None, None]
    WL = [None, None]
    for i in range(2):
        WH[i] = ring.take(f"w_high{i}", [P, 4096], F32R)
        WL[i] = ring.take(f"w_low{i}", [P, 4096], F32R)
    slot0_off = base + 32 * KB
    act_off = ring.at
    acts = Region(act_off, 32 * KB)
    actH = acts.take("act_high", [P, KT, 2 * T], F32R)
    actL = acts.take("act_low", [P, KT, 2 * T], F32R)
    keep = Region(acts.end, 14 * KB)
    xres = keep.take("xres", [P, NT, D])
    ident = keep.take("ident", [P, P])
    flip = keep.take("flip", [P, P])
    ones = keep.take("ones", [P, P])
    stat = keep.take("stat", [P, 256])
    free_off = keep.end
    FREE = nc.sbuf_usable_end - free_off

    mrow = nc.dram_tensor("mrow", (8, PW), F32, kind="Internal").ap()
    gates_d = nc.dram_tensor("gates_d", (2 * KT, P, T), F32, kind="Internal").ap()

    psum = ctx.enter_context(nc.psum_tensor("psum", [P, 8, 512], F32))

    front = Region(free_off, FREE)
    z_k = front.take("z_k", [P, 2 * NT, DA])
    z_v = front.take("z_v", [P, 2 * NT, DA])
    z_r = front.take("z_r", [P, NT, DA])
    z_lwT = front.take("z_lwT", [P, 2 * T])
    z_laT = front.take("z_laT", [P, 2 * T])
    z_lgT = front.take("z_lgT", [P, T])
    after_front = front.at
    modw = [front.take(f"modw{i}", [P, KT, PW]) for i in range(2)]
    after_modw = front.at
    early = Region(free_off, after_front - free_off)
    ctx_in = early.take("ctx_in", [P, NT, D])
    mbc = early.take("mbc", [P, 4, D])
    tail = Region(after_modw, free_off + FREE - after_modw)
    cc = tail.take("cc", [P, 2, KT])
    ccs = tail.take("ccs", [P, 2, KT])
    macc = tail.take("macc", [P, 2, PW])
    macc_c = Region(slot0_off + 32 * KB, 4 * KB).take("macc_c", [P, 2, PW])
    g1 = Region(slot0_off + 36 * KB, 4 * KB).take("g1", [P, D])
    hbuf = Region(slot0_off + 40 * KB, 8 * KB).take("hbuf", [P, 2, D])
    junk = Region(slot0_off + 48 * KB, 4 * KB).take("junk", [P, D])
    modb = tail.take("modb", [12, PW])
    mstage = tail.take("mstage", [1, PW])
    gstage = Region(acts.end, 8 * KB).take("gstage", [P, 2, 2, 2 * P])

    s_const = sem("const_ready")
    s_small = sem("small_in")
    s_modw = [sem("modw_in0"), sem("modw_in1")]
    s_ccs = sem("silu_ready")
    s_sig = sem("sigmoid_c")
    s_macc = sem("macc_ready")
    s_mps = sem("mod_psum")
    s_mev = sem("mod_evac")
    s_mrow = sem("mrow_out")
    s_ssq = sem("ssq_ready")
    s_var = sem("var_ready")
    s_sqrt = sem("sqrt_ready")
    s_h = sem("h_ready")
    s_hT = sem("hT_psum")
    s_hH = sem("hT_high")
    s_hL = sem("hT_low")
    s_raw = [sem("raw_in0"), sem("raw_in1")]
    s_wh = sem("w_high_ready")
    s_wl = sem("w_low_ready")
    s_wdone = sem("w_used")
    s_unit = sem("win_unit")
    s_uev = sem("win_evac")
    s_gst = [sem("gates_out0"), sem("gates_out1")]

    def full_panel(w, col, width=PW):
        return w[:, col:col + width].rearrange("(k p) n -> p k n", p=P)

    def load_panel(sp, n, par, src, elems=4096):
        if not isinstance(n, int) or n >= 2:
            sp.wait_ge(s_wl, n - 1)
        dst = RAW[par][:, 0:elems]
        if len(src.shape) == 3:
            dst = dst.rearrange("p (k n) -> p k n", n=src.shape[2])
        sp.dma_start(dst, src).then_inc(s_raw[par], 16)

    def panel_arrivals(n):
        return (n // 2) * 16 + 16

    def split_high(act, n, par, arrived, elems=4096):
        act.wait_ge(s_raw[par], arrived)
        if not isinstance(n, int) or n >= 2:
            act.wait_ge(s_wdone, n - 1)
        act.activation(WH[par][:, 0:elems], RAW[par][:, 0:elems], ACT.Copy).then_inc(s_wh, 1)

    def split_low(dve, n, par, elems=4096):
        dve.wait_ge(s_wh, n + 1)
        dve.tensor_tensor(WL[par][:, 0:elems], RAW[par][:, 0:elems],
                          WH[par][:, 0:elems].bitcast(F32), ALU.subtract).then_inc(s_wl, 1)

    def three_pass(pe, o, aH, aL, wH, wL, start, stop):
        pe.matmul(o, aH, wH, start=start, stop=False)
        pe.matmul(o, aH, wL, start=False, stop=False)
        return pe.matmul(o, aL, wH, start=False, stop=stop)

    r0, k0, v0 = 0, DA, 2 * DA
    l0 = 3 * DA
    q0, kb0, vb0 = l0 + 3 * P, l0 + 3 * P + DA, l0 + 3 * P + 2 * DA
    g0 = l0 + 3 * P + 3 * DA
    W_IN = [(k0, PW, "k"), (v0, PW, "v"), (r0, PW, "r"), (l0, 3 * P, "lora")]
    W_IN += [(g0 + PW * i, PW, f"gate{i}") for i in range(4)]
    W_IN += [(q0, PW, "q"), (kb0, PW, "kb"), (vb0, PW, "vb")]
    UNITS = {"k": 4, "v": 4, "kb": 4, "vb": 4, "r": 2, "q": 2, "lora": 3}
    NU_T = 2 * 2 * NT
    RB = 6
    unit0 = []
    u = NU_T
    for _, _, what in W_IN:
        unit0.append(u)
        u += UNITS.get(what, 2)
    NU = u
    N_MOD = 12

    att_in = Region(after_front, free_off + FREE - after_front)
    z_q = att_in.take("z_q", [P, NT, DA])
    z_kb = att_in.take("z_kb", [P, 2 * NT, DA])
    z_vb = att_in.take("z_vb", [P, 2 * NT, DA])

    def mod_load(sp, m):
        if m >= 2:
            sp.wait_ge(s_macc, m - 1)
        sp.dma_start(modw[m % 2][:, :, :],
                     a["mod_w"][0][:, PW * m:PW * (m + 1)].rearrange("(p k) n -> p k n", p=P)
                     ).then_inc(s_modw[m % 2], 16)

    def mod_sum(dve, m):
        dve.wait_ge(s_modw[m % 2], 16 * (m // 2 + 1))
        if m >= 2:
            dve.wait_ge(s_mps, m - 1)
        w = modw[m % 2]
        sides = [(0, macc)] + ([(1, macc_c)] if m < 4 else [])
        for side, acc in sides:
            dve.tensor_scalar(acc[:, m % 2, :], w[:, 0, :], ccs[:, side, 0:1], None, ALU.mult)
        for k in range(1, KT):
            dve.drain()
            for side, acc in sides:
                i = dve.scalar_tensor_tensor(out=acc[:, m % 2, :], in0=w[:, k, :],
                                             scalar=ccs[:, side, k:k + 1], in1=acc[:, m % 2, :],
                                             op0=ALU.mult, op1=ALU.add)
        i.then_inc(s_macc, 1)

    def mod_reduce(pe, m):
        pe.wait_ge(s_macc, m + 1)
        if m >= 1:
            pe.wait_ge(s_mev, m)
        for side, acc in [(0, macc)] + ([(1, macc_c)] if m < 4 else []):
            pe.matmul(psum[:, 6 + side, :], ones[:, :], acc[:, m % 2, :], start=True, stop=False)
            i = pe.matmul(psum[:, 6 + side, :], mod_bc(ident[0:N_MOD, m:m + 1], [N_MOD, P]), modb[:, :],
                          start=False, stop=True)
        i.then_inc(s_mps, 1)

    def mod_evac(act, m):
        act.wait_ge(s_mps, m + 1)
        if m < 4:
            dst = slice(PW * (m % 2), PW * (m % 2 + 1))
            act.activation(mbc[:, m // 2, dst], psum[:, 6, :], ACT.Copy)
            act.activation(mbc[:, 2 + m // 2, dst], psum[:, 7, :], ACT.Copy).then_inc(s_mev, 1)
        else:
            if m > 4:
                act.wait_ge(s_mrow, 16 * (m - 4))
            act.activation(mstage[:, :], psum[0:1, 6, :], ACT.Copy).then_inc(s_mev, 1)

    def mod_store(q, m):
        q.wait_ge(s_mev, m + 1)
        q.dma_start(mrow[m - 4:m - 3, :], mstage[:, :]).then_inc(s_mrow, 16)

    def token_tile(t):
        return xres[:, t, :] if t < NT else ctx_in[:, t - NT, :]

    def front_pool(pool):
        pool.memset(ident[:, :], 0.0)
        pool.memset(ones[:, :], 1.0)
        pool.drain()
        pool.affine_select(out=ident[:, :], in_=ident[:, :], compare_op=ALU.not_equal, fill=1.0,
                           base=0, pattern=[[-1, P]], channel_multiplier=1)
        pool.memset(flip[:, :], 0.0)
        pool.drain()
        for half in range(2):
            cs = slice(64 * half, 64 * half + 64)
            pool.affine_select(out=flip[:, cs], in_=flip[:, cs], compare_op=ALU.not_equal, fill=1.0,
                               base=-63 - 64 * half, pattern=[[1, 64]], channel_multiplier=1)
        pool.drain().then_inc(s_const, 1)
        for dst, src in [(cc[:, 0, :], a["c"].rearrange("o (p k) -> (o p) k", p=P)),
                         (cc[:, 1, :], a["c_ctx"].rearrange("(p k) -> p k", p=P)),
                         (modb[:, :], a["mod_b"][0].rearrange("(m n) -> m n", n=PW)),
                         (g1[:, :], a["norm1_g"][0].partition_broadcast(P)),
                         (xres[:, :, :], a["x"][0].rearrange("(t p) d -> p t d", p=P)),
                         (ctx_in[:, :, :], a["ctx"][0].rearrange("(t p) d -> p t d", p=P))]:
            pool.dma_start(dst, src).then_inc(s_small, 16)
        for m in range(4, N_MOD):
            mod_store(pool, m)
        pool.wait_ge(s_mrow, 16 * (N_MOD - 4))

    def front_sync(sp):
        for m in range(6):
            mod_load(sp, m)
            if m >= 2 and m < 4:
                load_panel(sp, m - 2, m % 2, full_panel(a["w_in"][0], W_IN[m - 2][0]))
        for n, (col, width, what) in enumerate(W_IN):
            if n >= 2:
                load_panel(sp, n, n % 2, full_panel(a["w_in"][0], col, width), KT * width)
            if n + 4 >= 6 and n + 4 < N_MOD:
                mod_load(sp, n + 4)

    def front_vector(dve):
        dve.wait_ge(s_small, 96)
        dve.wait_ge(s_sig, 1)
        dve.tensor_tensor(ccs[:, :, :], cc[:, :, :], ccs[:, :, :], ALU.mult)
        dve.drain()
        dve.wait_ge(s_ssq, 1)
        dve.tensor_scalar(stat[:, 4:8], stat[:, 0:4], 1.0 / D, EPS, ALU.mult, ALU.add).then_inc(s_var, 1)
        for m in range(4):
            mod_sum(dve, m)
        dve.wait_ge(s_sqrt, 1)
        dve.reciprocal(stat[:, 12:16], stat[:, 8:12])
        dve.wait_ge(s_mev, 4)
        for side in range(2):
            dve.scalar_tensor_tensor(out=mbc[:, 2 * side + 1, :], in0=mbc[:, 2 * side + 1, :], scalar=1.0,
                                     in1=g1[:, :], op0=ALU.add, op1=ALU.mult)
        dve.drain()
        for t in range(2 * NT):
            if t >= 2:
                dve.wait_ge(s_hT, 2 * (t - 1))
            dve.scalar_tensor_tensor(out=hbuf[:, t % 2, :], in0=token_tile(t), scalar=stat[:, 12 + t:13 + t],
                                     in1=mbc[:, 2 * (t // NT) + 1, :], op0=ALU.mult, op1=ALU.mult)
            dve.drain()
            dve.tensor_tensor(hbuf[:, t % 2, :], hbuf[:, t % 2, :], mbc[:, 2 * (t // NT), :],
                              ALU.add).then_inc(s_h, 1)
            if t >= 1:
                front_low(dve, t - 1)
        front_low(dve, 2 * NT - 1)
        for n in range(len(W_IN)):
            if n < 2:
                dve.wait_ge(s_hT, NU_T)
            split_low(dve, n, n % 2, KT * W_IN[n][1])
            if n + 4 < N_MOD:
                mod_sum(dve, n + 4)

    def hT_dst(dst, u):
        t, half = u // 2, u % 2
        return dst[:, 4 * half:4 * half + 4, P * t:P * (t + 1)]

    def front_low(dve, t):
        for u in (2 * t, 2 * t + 1):
            dve.wait_ge(s_hH, u + 1)
            dve.tensor_tensor(hT_dst(actL, u), psum[:, u % RB, :].rearrange("p (k n) -> p k n", n=P),
                              hT_dst(actH, u).bitcast(F32), ALU.subtract).then_inc(s_hL, 1)

    def front_scalar(act):
        act.wait_ge(s_small, 96)
        act.activation(ccs[:, :, :], cc[:, :, :], ACT.Sigmoid).then_inc(s_sig, 1)
        for t in range(2 * NT):
            i = act.activation(junk[:, :], token_tile(t), ACT.Square, accum_out=stat[:, t:t + 1])
            act.drain()
        act.drain().then_inc(s_ssq, 1)
        act.wait_ge(s_var, 1)
        act.activation(stat[:, 8:12], stat[:, 4:8], ACT.Sqrt).then_inc(s_sqrt, 1)
        for m in range(4):
            mod_evac(act, m)
        for u in range(NU_T):
            act.wait_ge(s_hT, u + 1)
            act.activation(hT_dst(actH, u), psum[:, u % RB, :].rearrange("p (k n) -> p k n", n=P),
                           ACT.Copy).then_inc(s_hH, 1)
        split_high(act, 0, 0, 16, KT * W_IN[0][1])
        for n, (col, width, what) in enumerate(W_IN):
            if n + 1 < len(W_IN):
                split_high(act, n + 1, (n + 1) % 2, panel_arrivals(n + 1), KT * W_IN[n + 1][1])
            if n + 4 < N_MOD:
                mod_evac(act, n + 4)
            for j in range(UNITS.get(what, 2)):
                u = unit0[n] + j
                act.wait_ge(s_unit, u - NU_T + 1)
                src = psum[:, u % RB, :]
                if what == "lora":
                    if j == 2:
                        act.activation(z_lgT[:, :], src[:, 0:T], ACT.Sigmoid).then_inc(s_uev, 1)
                    elif j == 1:
                        act.activation(z_laT[:, :], src, ACT.Copy).then_inc(s_uev, 1)
                    else:
                        act.activation(z_lwT[:, :], src, ACT.Tanh).then_inc(s_uev, 1)
                elif what.startswith("gate"):
                    g = 2 * int(what[4:]) + j
                    if g >= 2:
                        act.wait_ge(s_gst[g % 2], 16 * (g // 2))
                    act.activation(gstage[:, g % 2, :, :], src.rearrange("p (c t) -> p c t", c=2),
                                   ACT.Sigmoid).then_inc(s_uev, 1)
                    act.wait_ge(s_uev, u - NU_T + 1)
                    act.dma_start(gates_d[2 * g:2 * g + 2].rearrange("c p t -> p c t"),
                                  gstage[:, g % 2, :, :]).then_inc(s_gst[g % 2], 16)
                else:
                    if what == "q" and j == 0:
                        act.wait_ge(s_macc, N_MOD)
                    dst = {"k": z_k, "v": z_v, "r": z_r, "q": z_q, "kb": z_kb, "vb": z_vb}[what]
                    act.activation(dst[:, j, :], src, ACT.Copy).then_inc(s_uev, 1)

        for i in range(2):
            act.wait_ge(s_gst[i], 64)

    def wait_bank(pe, u):
        if u - RB < 0:
            return
        if u - RB < NU_T:
            pe.wait_ge(s_hL, u - RB + 1)
        else:
            pe.wait_ge(s_uev, u - RB - NU_T + 1)

    def front_tensor(pe):
        pe.wait_ge(s_const, 1)
        pe.wait_ge(s_small, 96)
        for m in range(4):
            mod_reduce(pe, m)
        for u in range(NU_T):
            t, half = u // 2, u % 2
            pe.wait_ge(s_h, t + 1)
            wait_bank(pe, u)
            for j in range(4):
                c = 4 * half + j
                i = pe.transpose(psum[:, u % RB, P * j:P * (j + 1)], hbuf[:, t % 2, P * c:P * (c + 1)],
                                 ident[:, :])
            i.then_inc(s_hT, 1)
        pe.wait_ge(s_hL, NU_T)
        for n, (col, width, what) in enumerate(W_IN):
            pe.wait_ge(s_wl, n + 1)
            wh = WH[n % 2][:, 0:KT * width].rearrange("p (k n) -> p k n", k=KT)
            wl = WL[n % 2][:, 0:KT * width].rearrange("p (k n) -> p k n", k=KT)
            for j in range(UNITS.get(what, 2)):
                u = unit0[n] + j
                wait_bank(pe, u)
                bank = psum[:, u % RB, :]
                if what == "lora" or what.startswith("gate"):
                    toks = 2 * T if what == "lora" and j < 2 else T
                    chunks = [j] if what == "lora" else [2 * j, 2 * j + 1]
                    for ci, c in enumerate(chunks):
                        o = bank[:, T * ci:T * ci + toks]
                        for k in range(KT):
                            cs = slice(P * c, P * (c + 1))
                            i = three_pass(pe, o, wh[:, k, cs], wl[:, k, cs], actH[:, k, 0:toks],
                                           actL[:, k, 0:toks], k == 0, k == KT - 1)
                else:
                    for k in range(KT):
                        ts = slice(P * j, P * (j + 1))
                        i = three_pass(pe, bank, actH[:, k, ts], actL[:, k, ts], wh[:, k, :], wl[:, k, :],
                                       k == 0, k == KT - 1)
                i.then_inc(s_unit, 1)
            pe.drain().then_inc(s_wdone, 1)
            if n + 4 < N_MOD:
                mod_reduce(pe, n + 4)

    NW = NU - NU_T
    BW = PW // 2
    attw = Region(act_off, 32 * KB)
    qT = attw.take("qT", [P, H // 2, T])
    kT = attw.take("kT", [P, H // 2, 2 * T])
    logit = attw.take("logit", [P, 2, BW])
    prob = attw.take("prob", [P, 2, 2 * T])
    probT = attw.take("probT", [P, 2, 4, P])
    sq = attw.take("sq", [P, 2 * T])
    qg = attw.take("qg", [P, 2, HD])
    rtab = attw.take("rtab", [15 * H, P])
    attf = Region(att_in.at, free_off + FREE - att_in.at)
    bias = attf.take("bias", [P, NT, H, BW])
    yb = attf.take("yb", [P, NT, DA])
    rtab_d = nc.dram_tensor("rtab_d", (15 * H, P), F32, kind="Internal").ap()
    qk_ss = stat[:, 16:64]
    qk_rs = stat[:, 64:112]
    lsum = stat[:, 112:144].rearrange("p (s i) -> p s i", s=2)
    nmax = stat[:, 144:160]
    mx = stat[:, 160:192].rearrange("p (s i) -> p s i", s=2)

    s_qg = sem("qk_gains_in")
    s_rt = sem("rpb_in")
    s_rz = sem("rpb_zeroed")
    s_rtd = sem("rpb_table_out")
    s_bias = sem("bias_in")
    s_mask = sem("bias_masked")
    s_qss = sem("qk_squares")
    s_qsq = sem("qk_sqrt")
    s_qn = sem("qk_normed")
    s_qT = sem("qkT_psum")
    s_qTe = sem("qkT_ready")
    s_S = sem("logits")
    s_lg = sem("logits_biased")
    s_ex = sem("exp_done")
    s_pT = sem("probT_psum")
    s_pTe = sem("probT_ready")
    s_pv = sem("pv_done")
    s_yb = sem("yb_ready")

    def att_pool(pool):
        pool.wait_ge(s_macc, N_MOD)
        pool.wait_ge(s_mps, N_MOD)
        pool.wait_ge(s_unit, NW)
        pool.dma_start(qg[:, 0, :], a["na_q_g"][0].partition_broadcast(P)).then_inc(s_qg, 16)
        pool.dma_start(qg[:, 1, :], a["na_k_g"][0].partition_broadcast(P)).then_inc(s_qg, 16)
        pool.memset(rtab[:, :], 0.0).then_inc(s_rz, 1)
        pool.wait_ge(s_rz, 1)
        pool.dma_start(rtab[:, 48:48 + 31], a["na_rpb"][0].rearrange("h r c -> (h r) c")).then_inc(s_rt, 16)
        pool.wait_ge(s_rt, 16)
        pool.dma_start(rtab_d, rtab[:, :]).then_inc(s_rtd, 16)
        pool.wait_ge(s_rtd, 16)
        for i in range(4):
            for h in range(H):
                src = bass.AP(rtab_d.tensor, (h * 15 + 7 - i) * P, [[1, 64], [P, 4], [1, 64]])
                pool.dma_start(bias[64 * (i % 2):64 * (i % 2) + 64, i // 2, h, :]
                               .rearrange("p (a k) -> p a k", a=4), src).then_inc(s_bias, 16)
        pool.wait_ge(s_bias, 16 * 4 * H)
        for half in range(2):
            b = bias[64 * half:64 * half + 64, :, :, :].rearrange("p t h (a k) -> p (t h a) k", a=4)
            pool.affine_select(out=b[:, :, 0:48], in_=b[:, :, 0:48], compare_op=ALU.is_ge, fill=NEG,
                               base=8 - 63, pattern=[[0, 64], [1, 48]], channel_multiplier=1)
            pool.drain()
            pool.affine_select(out=b[:, :, 16:64], in_=b[:, :, 16:64], compare_op=ALU.is_ge, fill=NEG,
                               base=63 + 7 - 16, pattern=[[0, 64], [-1, 48]], channel_multiplier=-1
                               ).then_inc(s_mask, 1)

    def heads(ap):
        return ap.rearrange("p t (h d) -> p (t h) d", d=HD)

    def bc(ap, n):
        return ap.unsqueeze(2).to_broadcast([ap.shape[0], ap.shape[1], n])

    def att_vector(dve):
        dve.wait_ge(s_uev, NW)
        dve.wait_ge(s_unit, NW)
        parts = [(z_q, t, t) for t in range(NT)] + [(z_kb, t, NT + t) for t in range(2 * NT)]
        for z, t, c in parts:
            dve.tensor_tensor(sq[:, :], z[:, t, :], z[:, t, :], ALU.mult)
            dve.drain()
            i = dve.tensor_reduce(qk_ss[:, H * c:H * c + H], sq[:, :].rearrange("p (h d) -> p h d", d=HD),
                                  AX, ALU.add)
            dve.drain()
        dve.tensor_scalar(qk_ss, qk_ss, 1.0 / HD, EPS, ALU.mult, ALU.add).then_inc(s_qss, 1)
        dve.wait_ge(s_qsq, 1)
        dve.reciprocal(qk_rs, qk_rs)
        dve.wait_ge(s_qg, 32)
        dve.tensor_scalar(qg[:, 0, :], qg[:, 0, :], HD ** -0.5, None, ALU.mult)
        dve.drain()
        for z, t, c in parts:
            zt = z[:, t, :].rearrange("p (h d) -> p h d", d=HD)
            dve.tensor_tensor(zt, zt, bc(qk_rs[:, H * c:H * c + H], HD), ALU.mult)
            dve.drain()
            g = qg[:, 0 if c < NT else 1, :].unsqueeze(1).to_broadcast([P, H, HD])
            dve.tensor_tensor(zt, zt, g, ALU.mult).then_inc(s_qn, 1)
        for i in range(NT * H + 1):
            if i < NT * H:
                t, h = i // H, i % H
                dve.wait_ge(s_S, i + 1)
                if i == 0:
                    dve.wait_ge(s_mask, 2)
                dve.tensor_tensor_reduce(out=logit[:, i % 2, :], in0=psum[:, i % 2, 0:BW],
                                         in1=bias[:, t, h, :], scale=1.0, scalar=NEG, op0=ALU.add,
                                         op1=ALU.max, accum_out=mx[:, 0, i:i + 1])
                dve.tensor_reduce(mx[:, 1, i:i + 1], psum[:, i % 2, BW:2 * BW], AX, ALU.max)
                dve.drain()
                dve.tensor_scalar(nmax[:, i:i + 1], mx[:, 0, i:i + 1], mx[:, 1, i:i + 1], -1.0, ALU.max,
                                  ALU.mult).then_inc(s_lg, 1)
            if i >= 1:
                j = i - 1
                dve.wait_ge(s_pT, j + 1)
                if j >= 2:
                    dve.wait_ge(s_pv, j - 1)
                dve.tensor_copy(probT[:, j % 2, :, :],
                                psum[:, 2 + j % 2, :].rearrange("p (c n) -> p c n", c=4)).then_inc(s_pTe, 1)
        dve.wait_ge(s_ex, NT * H)
        dve.tensor_tensor(lsum[:, 0, :], lsum[:, 0, :], lsum[:, 1, :], ALU.add)
        dve.drain()
        dve.reciprocal(lsum[:, 0, :], lsum[:, 0, :])
        dve.wait_ge(s_pv, NT * H)
        dve.drain()
        for t in range(NT):
            dve.tensor_tensor(yb[:, t, :].rearrange("p (h d) -> p h d", d=HD),
                              psum[:, 4 + t, :].rearrange("p (h d) -> p h d", d=HD),
                              bc(lsum[:, 0, H * t:H * t + H], HD), ALU.mult).then_inc(s_yb, 1)

    def att_scalar(act):
        act.wait_ge(s_qss, 1)
        act.activation(qk_rs, qk_ss, ACT.Sqrt).then_inc(s_qsq, 1)
        for b in range(3 * NT):
            act.wait_ge(s_qT, b + 1)
            dst = qT[:, :, P * b:P * b + P] if b < NT else kT[:, :, P * (b - NT):P * (b - NT) + P]
            act.activation(dst, psum[:, b, :].rearrange("p (c n) -> p c n", c=4), ACT.Copy).then_inc(s_qTe, 1)
        for i in range(NT * H):
            act.wait_ge(s_lg, i + 1)
            if i >= 2:
                act.wait_ge(s_pT, i - 1)
            act.activation(prob[:, i % 2, 0:BW], logit[:, i % 2, :], ACT.Exp, bias=nmax[:, i:i + 1],
                           accum_out=lsum[:, 0, i:i + 1])
            act.activation(prob[:, i % 2, BW:2 * BW], psum[:, i % 2, BW:2 * BW], ACT.Exp,
                           bias=nmax[:, i:i + 1], accum_out=lsum[:, 1, i:i + 1])
            act.drain().then_inc(s_ex, 1)

    def att_tensor(pe):
        for b in range(3 * NT):
            pe.wait_ge(s_qn, b + 1)
            z, t = (z_q, b) if b < NT else (z_kb, b - NT)
            for j in range(4):
                i = pe.matmul(psum[:, b, P * j:P * (j + 1)], z[:, t, P * j:P * (j + 1)],
                              (flip if b < NT else ident)[:, :], start=True, stop=True)
            i.then_inc(s_qT, 1)
        for i in range(NT * H + 2):
            if i < NT * H:
                t, h = i // H, i % H
                if i == 0:
                    pe.wait_ge(s_qTe, 3 * NT)
                if i >= 2:
                    pe.wait_ge(s_ex, i - 1)
                hs = slice(64 * (h % 2), 64 * (h % 2) + 64)
                pe.matmul(psum[:, i % 2, :], qT[hs, h // 2, P * t:P * (t + 1)], kT[hs, h // 2, :],
                          start=True, stop=True).then_inc(s_S, 1)
            if 1 <= i <= NT * H:
                j = i - 1
                pe.wait_ge(s_ex, j + 1)
                if j >= 2:
                    pe.wait_ge(s_pTe, j - 1)
                for c in range(4):
                    ins = pe.transpose(psum[:, 2 + j % 2, P * c:P * (c + 1)], prob[:, j % 2, P * c:P * (c + 1)],
                                       ident[:, :])
                ins.then_inc(s_pT, 1)
            if i >= 2:
                j = i - 2
                t, h = j // H, j % H
                pe.wait_ge(s_pTe, j + 1)
                for c in range(4):
                    ins = pe.matmul(psum[:, 4 + t, HD * h:HD * (h + 1)], probT[:, j % 2, c, :],
                                    z_vb[:, c, HD * h:HD * (h + 1)], start=(c == 0), stop=(c == 3))
                ins.then_inc(s_pv, 1)

    STEPS = [(0, 2), (1, 3), (0, 3), (1, 2), (0, 0), (1, 1), (0, 1), (1, 0)]
    NS = len(STEPS)
    LV = 7
    C0 = float(2.718281828459045 ** -0.5)

    rk = Region(slot0_off, 32 * KB)
    maskF = rk.take("maskF", [P, LV, P])
    maskR = rk.take("maskR", [P, LV, P])
    tri2 = rk.take("tri2", [P, 2, 2, P])
    cumT = rk.take("cumT", [P, 2, P])
    colm = rk.take("colm", [P, 2, 2])
    w0b = rk.take("w0b", [P, 2, DA])
    a0b = rk.take("a0b", [P, 2, DA])
    kkb = rk.take("kkb", [P, DA])
    kab = rk.take("kab", [P, DA])
    wlb = rk.take("wlb", [P, DA])
    alb = rk.take("alb", [P, DA])
    xr = Region(acts.end, 8 * KB)
    glb = xr.take("glb", [P, DA])
    rkb = xr.take("rkb", [P, DA])
    lngb = xr.take("lngb", [P, DA])
    lnbb = xr.take("lnbb", [P, DA])

    rf = Region(after_front, 36 * KB)
    ew = rf.take("ew", [P, DA])
    ea = rf.take("ea", [P, DA])
    kkn = rf.take("kkn", [P, DA])
    Ktk = rf.take("Ktk", [P, DA])
    Rtk = rf.take("Rtk", [P, DA])
    epos = rf.take("epos", [P, DA])
    kdir = rf.take("kdir", [P, DA])
    Kb = rf.take("Kb", [P, 2, DA])
    Bb = rf.take("Bb", [P, 2, DA])
    KRT = rf.take("KRT", [P, H // 2, 2, P])
    KbT = rf.take("KbT", [P, H // 2, P])
    BbT = rf.take("BbT", [P, H // 2, P])
    CD = rf.take("CD", [P, 2, 2, P])
    Mst = rf.take("Mst", [P, 2, H // 2, HD])
    Mp = rf.take("Mp", [P, 2, H // 2, HD])
    ra = Region(act_off, 32 * KB)
    AtE = ra.take("AtE", [P, H, 2, P])
    Tm = ra.take("Tm", [P, H, P])
    Tt = ra.take("Tt", [P, H, P])
    Atm = ra.take("Atm", [P, H, P])
    M1s = ra.take("M1s", [P, H, P])
    Xs = ra.take("Xs", [P, DA])
    yacc = ra.take("yacc", [P, NT, DA])
    nU = ra.take("nU", [P, DA])
    Yps = rk.take("Yps", [P, DA])
    idx = Region(act_off, 4 * KB)
    ixor = idx.take("ixor", [P, P], I32)
    ixp = idx.take("ixp", [P, P], I32)
    ixs = idx.take("ixs", [P, P], I32)
    krs = stat[:, 192:224]
    facs = stat[:, 224:240].rearrange("p (s c) -> p s c", s=2)
    kq = stat[:, 0:32]
    gst = stat[:, 32:64]

    HO = [h for par in range(2) for h in range(par, H, 2)]

    R = {name: sem("rk_" + name) for name in (
        "iota", "masks", "tri", "vec", "krs", "kk", "p1", "e1", "a1", "p2", "e3", "a2", "ks",
        "tr", "trE", "gram", "gev", "Ap", "T0", "Tt0", "xyh", "xy", "xyE", "mp", "atm", "m1", "m1e",
        "y", "upd", "U", "nU", "EU", "yf", "dM", "Mu", "gmm", "gss", "gsq", "done")}

    def tr_before(s):
        return 3 * s if s <= 4 else 12 + 4 * (s - 4)

    def is_x(s):
        return s >= 4

    def rwkv_pool(pool):
        pool.wait_ge(s_pv, NT * H)
        pool.wait_ge(s_yb, NT)
        pool.wait_ge(s_gst[0], 64)
        pool.wait_ge(s_gst[1], 64)
        pool.iota(ixp[:, :], pattern=[[0, P]], base=0, channel_multiplier=1)
        pool.iota(ixor[:, :], pattern=[[1, P]], base=0, channel_multiplier=0)
        pool.drain().then_inc(R["iota"], 1)
        for d in range(2):
            for dst, src in [(w0b[:, d, :], a["rw_w0"][0, d].partition_broadcast(P)),
                             (a0b[:, d, :], a["rw_a0"][0, d].partition_broadcast(P))]:
                pool.dma_start(dst, src).then_inc(R["vec"], 16)
        for dst, src in [(kkb[:, :], a["rw_k_k"][0].partition_broadcast(P)),
                         (kab[:, :], a["rw_k_a"][0].partition_broadcast(P)),
                         (wlb[:, :], a["rw_w_lora_b"][0].rearrange("z r c -> (z r) c")),
                         (alb[:, :], a["rw_a_lora_b"][0].rearrange("z r c -> (z r) c")),
                         (glb[:, :], a["rw_g_lora_b"][0]),
                         (rkb[:, :], a["rw_r_k"][0].rearrange("h d -> (h d)").partition_broadcast(P)),
                         (lngb[:, :], a["rw_ln_g"][0].partition_broadcast(P)),
                         (lnbb[:, :], a["rw_ln_b"][0].partition_broadcast(P))]:
            pool.dma_start(dst, src).then_inc(R["vec"], 16)
        pool.memset(tri2[:, :, :, :], 1.0)
        pool.memset(cumT[:, :, :], 1.0)
        pool.memset(colm[:, :, :], 0.0)
        pool.drain()
        for d, sgn in ((0, 1), (1, -1)):
            for incl in range(2):
                pool.affine_select(out=tri2[:, d, incl, :], in_=tri2[:, d, incl, :], compare_op=ALU.is_ge,
                                   fill=0.0, base=incl - 1, pattern=[[sgn, P]], channel_multiplier=-sgn)
                pool.drain()
            pool.affine_select(out=cumT[:, d, :], in_=cumT[:, d, :], compare_op=ALU.is_ge,
                               fill=0.0, base=0, pattern=[[sgn, P]], channel_multiplier=-sgn)
        pool.drain()
        pool.memset(colm[0:64, 0, 0:1], 1.0)
        pool.drain()
        pool.memset(colm[64:128, 0, 1:2], 1.0)
        pool.drain()
        pool.memset(colm[64:128, 1, 0:1], 1.0)
        pool.drain()
        pool.memset(colm[0:64, 1, 1:2], 1.0)
        pool.drain()
        for d in range(2):
            half = slice(0, 64) if d == 0 else slice(64, 128)
            pool.tensor_scalar(cumT[half, d, :], cumT[half, d, :], -1.0, None, ALU.add)
            pool.drain()
        pool.drain().then_inc(R["tri"], 1)
        pool.wait_ge(R["krs"], 1)
        pool.wait_ge(R["masks"], 1)
        kk_pool(pool, 0)
        for s in range(NS):
            d, tt = STEPS[s]
            mk = maskF if d == 0 else maskR
            for g in range(2):
                hs = slice(4 * g, 4 * g + 4)
                pool.wait_ge(R["gev"], 8 * s + 4 * g + 4)
                if s > 0:
                    pool.wait_ge(R["U"], s)
                pool.tensor_tensor(Atm[:, hs, :], AtE[:, hs, 0, :], mb(mk[:, 0, :]), ALU.mult)
                pool.drain()
                pool.tensor_tensor(Tt[:, hs, :], mb(ident[:, :]), Atm[:, hs, :], ALU.subtract)
                pool.drain().then_inc(R["Tt0"], 1)
            for l in range(1, LV):
                for g in range(2):
                    hs = slice(4 * g, 4 * g + 4)
                    if l > 1:
                        pool.wait_ge(R["m1"], 12 * s + 2 * (l - 2) + g + 1)
                    pool.tensor_tensor(Atm[:, hs, :], AtE[:, hs, 0, :], mb(mk[:, l, :]), ALU.mult
                                       ).then_inc(R["atm"], 1)
            if s + 1 < NS:
                kk_pool(pool, s + 1)

    def kk_pool(pool, s):
        tt = STEPS[s][1]
        if s > 0:
            pool.wait_ge(R["ks"], s)
        pool.tensor_tensor(kkn[:, :], z_k[:, tt, :], kkb[:, :], ALU.mult)
        pool.drain()
        pool.tensor_tensor(kkn[:, :].rearrange("p (h d) -> p h d", d=HD),
                           kkn[:, :].rearrange("p (h d) -> p h d", d=HD),
                           bc(krs[:, H * tt:H * tt + H], HD), ALU.mult).then_inc(R["kk"], 1)

    def mb(m):
        return m.unsqueeze(1).to_broadcast([P, 4, P])

    def hv(ap):
        return ap.rearrange("p (h d) -> p h d", d=HD)

    def prep_vector(dve, s, part):
        d, tt = STEPS[s]
        if part == 1:
            dve.wait_ge(R["p1"], s + 1)
            if s > 0:
                dve.wait_ge(R["p2"], s)
            dve.tensor_tensor(ew[:, :], psum[:, 6, :], w0b[:, d, :], ALU.add)
            dve.tensor_tensor(ea[:, :], psum[:, 7, :], a0b[:, d, :], ALU.add)
            dve.drain().then_inc(R["e1"], 1)
        elif part == 3:
            dve.wait_ge(R["p2"], s + 1)
            if s > 0:
                dve.wait_ge(R["tr"], tr_before(s))
            dve.tensor_tensor(Ktk[:, :], psum[:, 6, :], ew[:, :], ALU.subtract)
            dve.wait_ge(R["a1"], s + 1)
            dve.scalar_tensor_tensor(out=kdir[:, :], in0=ea[:, :], scalar=-1.0, in1=kab[:, :],
                                     op0=ALU.add, op1=ALU.mult)
            dve.drain().then_inc(R["e3"], 1)
        elif part == 4:
            dve.scalar_tensor_tensor(out=kdir[:, :], in0=kdir[:, :], scalar=1.0, in1=z_k[:, tt, :],
                                     op0=ALU.add, op1=ALU.mult)
            dve.wait_ge(R["kk"], s + 1)
            dve.tensor_tensor(ea[:, :], ea[:, :], kkn[:, :], ALU.mult)
            dve.drain()
        elif part == 5:
            dve.wait_ge(R["a2"], s + 1)
            if s >= 2:
                dve.wait_ge(R["dM"], s - 1)
            dve.tensor_tensor(Kb[:, s % 2, :], kdir[:, :], epos[:, :], ALU.mult)
            dve.tensor_tensor(Bb[:, s % 2, :], ea[:, :], epos[:, :], ALU.mult)
        elif part == 6:
            dve.tensor_tensor(Ktk[:, :], Ktk[:, :], kkn[:, :], ALU.mult)
            if is_x(s):
                dve.tensor_tensor(Rtk[:, :], Rtk[:, :], z_r[:, tt, :], ALU.mult)
            dve.drain().then_inc(R["ks"], 1)

    def rwkv_vector(dve):
        split_low(dve, len(W_IN), 1)
        dve.wait_ge(R["iota"], 1)
        dve.tensor_tensor(ixor[:, :], ixor[:, :], ixp[:, :], ALU.bitwise_xor)
        dve.wait_ge(R["tri"], 1)
        dve.drain()
        for l in range(LV):
            dve.tensor_scalar(ixs[:, :], ixor[:, :], l, None, ALU.logical_shift_right)
            dve.drain()
            dve.tensor_scalar(maskF[:, l, :], ixs[:, :], 1, None, ALU.is_equal)
            dve.drain()
            dve.tensor_tensor(maskR[:, l, :], maskF[:, l, :], tri2[:, 1, 0, :], ALU.mult)
            dve.drain()
            dve.tensor_tensor(maskF[:, l, :], maskF[:, l, :], tri2[:, 0, 0, :], ALU.mult)
            dve.drain()
        dve.drain().then_inc(R["masks"], 1)
        dve.wait_ge(R["vec"], 16 * 12)
        for tt in range(2 * NT):
            dve.tensor_tensor(ew[:, :], z_k[:, tt, :], kkb[:, :], ALU.mult)
            dve.drain()
            dve.tensor_tensor(ea[:, :], ew[:, :], ew[:, :], ALU.mult)
            dve.drain()
            dve.tensor_reduce(kq[:, H * tt:H * tt + H], hv(ea[:, :]), AX, ALU.add)
            dve.drain()
        dve.tensor_scalar(kq, kq, 1e-12, None, ALU.max).then_inc(s_qss, 1)
        dve.wait_ge(s_qsq, 2)
        dve.reciprocal(krs, krs).then_inc(R["krs"], 1)
        for part in (1, 3, 4, 5, 6):
            prep_vector(dve, 0, part)
        for s in range(NS):
            d, tt = STEPS[s]
            mk = maskR if d == 0 else maskF
            if s >= 2:
                dve.tensor_tensor(Mp[:, d, :, :], Mst[:, d, :, :],
                                  bc(facs[:, s % 2, 0:8:2], HD), ALU.mult).then_inc(R["mp"], 1)
            for h in range(H):
                dve.wait_ge(R["gram"], H * s + h + 1)
                if h == 0 and s > 0:
                    dve.wait_ge(R["atm"], 12 * s)
                    dve.wait_ge(R["EU"], s)
                n = 2 if is_x(s) else 1
                m = tri2[:, d, 0:n, :]
                pb = psum[:, 4 + h % 2, :].rearrange("p (s c n) -> p s c n", s=2, c=2)
                dve.tensor_tensor(AtE[:, h, 0:n, :], pb[:, 0, 0:n, :], m, ALU.mult)
                if s > 0 or h >= 2:
                    dve.wait_ge(R["xyh"], H * s + h - 1)
                dve.tensor_tensor(CD[:, h % 2, 0:n, :], pb[:, 1, 0:n, :], m, ALU.mult)
                dve.drain().then_inc(R["gev"], 1)
            for g in range(2):
                hs = slice(4 * g, 4 * g + 4)
                dve.wait_ge(R["Ap"], 2 * s + g + 1)
                if s > 0 and g == 0:
                    dve.wait_ge(R["y"], 12 * s)
                dve.tensor_tensor(Tm[:, hs, :], psum[:, g, :].rearrange("p (h n) -> p h n", n=P),
                                  mb(mk[:, 0, :]), ALU.mult)
                dve.drain()
                dve.tensor_tensor(Tm[:, hs, :], mb(ident[:, :]), Tm[:, hs, :], ALU.subtract
                                  ).then_inc(R["T0"], 1)
            for l in range(1, LV):
                for g in range(2):
                    hs = slice(4 * g, 4 * g + 4)
                    dve.wait_ge(R["y"], 12 * s + 2 * (l - 1) + g + 1)
                    if l < LV - 1:
                        dve.tensor_tensor(Tm[:, hs, :], Tm[:, hs, :],
                                          psum[:, g, :].rearrange("p (h n) -> p h n", n=P), ALU.subtract)
                    dve.tensor_tensor(Tt[:, hs, :], Tt[:, hs, :],
                                      psum[:, 2 + g, :].rearrange("p (h n) -> p h n", n=P), ALU.subtract)
                    dve.drain().then_inc(R["upd"], 1)
                if s + 1 < NS:
                    prep_vector(dve, s + 1, l)
            if is_x(s):
                dve.wait_ge(R["EU"], s + 1)
                first = s < 6
                dst = yacc[:, tt, :] if first else Yps[:, :]
                dve.tensor_tensor(dst, Yps[:, :], psum[:, 5, :], ALU.add)
                if not first:
                    dve.drain()
                    dve.tensor_tensor(yacc[:, tt, :], yacc[:, tt, :], Yps[:, :], ALU.add)
                dve.drain().then_inc(R["yf"], 1)
            if s < NS - 2:
                dve.wait_ge(R["dM"], s + 1)
                src = psum[:, 0, 0:4 * HD].rearrange("p (c v) -> p c v", c=4)
                fl = bc(facs[:, s % 2, 1:8:2], HD)
                if s < 2:
                    dve.tensor_tensor(Mst[:, d, :, :], src, fl, ALU.mult)
                else:
                    dve.tensor_tensor(Mst[:, d, :, :], Mp[:, d, :, :], src, ALU.add)
                    dve.drain()
                    dve.tensor_tensor(Mst[:, d, :, :], Mst[:, d, :, :], fl, ALU.mult)
                dve.drain().then_inc(R["Mu"], 1)
        for t in range(NT):
            dve.tensor_reduce(gst[:, H * t:H * t + H], hv(yacc[:, t, :]), AX, ALU.add)
            dve.tensor_tensor(kdir[:, :], z_r[:, t, :], z_k[:, t, :], ALU.mult)
            dve.drain()
            dve.tensor_scalar(gst[:, H * t:H * t + H], gst[:, H * t:H * t + H], 1.0 / HD, None, ALU.mult)
            dve.tensor_tensor(kdir[:, :], kdir[:, :], rkb[:, :], ALU.mult)
            dve.drain()
            dve.tensor_tensor(hv(yacc[:, t, :]), hv(yacc[:, t, :]), bc(gst[:, H * t:H * t + H], HD),
                              ALU.subtract)
            dve.tensor_reduce(krs[:, H * t:H * t + H], hv(kdir[:, :]), AX, ALU.add)
            dve.drain()
            dve.tensor_tensor(ew[:, :], yacc[:, t, :], yacc[:, t, :], ALU.mult)
            dve.drain()
            dve.tensor_reduce(gst[:, 16 + H * t:16 + H * t + H], hv(ew[:, :]), AX, ALU.add)
            dve.drain()
        dve.tensor_scalar(gst[:, 16:32], gst[:, 16:32], 1.0 / HD, 64e-5, ALU.mult, ALU.add
                          ).then_inc(R["gss"], 1)
        dve.wait_ge(R["gsq"], 1)
        dve.reciprocal(gst[:, 16:32], gst[:, 16:32])
        dve.drain()
        for t in range(NT):
            dve.tensor_tensor(hv(yacc[:, t, :]), hv(yacc[:, t, :]), bc(gst[:, 16 + H * t:16 + H * t + H], HD),
                              ALU.mult)
            dve.tensor_tensor(hv(kdir[:, :]), hv(z_v[:, t, :]), bc(krs[:, H * t:H * t + H], HD), ALU.mult)
            dve.drain()
            dve.tensor_tensor(yacc[:, t, :], yacc[:, t, :], lngb[:, :], ALU.mult)
            dve.tensor_tensor(kdir[:, :], kdir[:, :], lnbb[:, :], ALU.add)
            dve.drain()
            dve.tensor_tensor(yacc[:, t, :], yacc[:, t, :], kdir[:, :], ALU.add)
            dve.wait_ge(R["gmm"], 1)
            dve.drain()
            dve.tensor_tensor(yacc[:, t, :], yacc[:, t, :], psum[:, 6 + t, :], ALU.mult)
            dve.drain()
        dve.drain().then_inc(R["done"], 1)

    def prep_scalar(act, s, part):
        if part == 1:
            act.wait_ge(R["e1"], s + 1)
            act.activation(ew[:, :], ew[:, :], ACT.Sigmoid)
            act.activation(ea[:, :], ea[:, :], ACT.Sigmoid)
            act.drain().then_inc(R["a1"], 1)
        else:
            act.wait_ge(R["e3"], s + 1)
            act.wait_ge(R["p2"], s + 1)
            if s > 0:
                act.wait_ge(R["ks"], s)
                act.wait_ge(R["tr"], tr_before(s))
            act.activation(Ktk[:, :], Ktk[:, :], ACT.Exp, scale=-C0)
            act.activation(epos[:, :], psum[:, 6, :], ACT.Exp, scale=C0)
            if is_x(s):
                act.activation(Rtk[:, :], psum[:, 6, :], ACT.Exp, scale=-C0)
            if s >= 2 and s - 2 < NS - 2:
                act.wait_ge(R["Mu"], s - 1)
            act.activation(facs[:, s % 2, :], psum[:, 7, 0:8], ACT.Exp, scale=-C0)
            act.drain().then_inc(R["a2"], 1)

    def rwkv_scalar(act):
        split_high(act, len(W_IN), 1, panel_arrivals(len(W_IN)))
        act.wait_ge(s_qss, 2)
        act.activation(krs, kq, ACT.Sqrt).then_inc(s_qsq, 1)
        prep_scalar(act, 0, 1)
        prep_scalar(act, 0, 2)
        for s in range(NS):
            d, tt = STEPS[s]
            names = [(KRT[:, :, 0, :], 0), (KbT[:, :, :], 2), (BbT[:, :, :], 3)]
            if is_x(s):
                names.append((KRT[:, :, 1, :], 1))
            if s > 0:
                act.wait_ge(R["xy"], s)
            for j, (dst, b) in enumerate(names):
                act.wait_ge(R["tr"], tr_before(s) + j + 1)
                act.activation(dst, psum[:, b, :].rearrange("p (c n) -> p c n", c=4), ACT.Copy
                               ).then_inc(R["trE"], 1)
            act.wait_ge(R["xy"], s + 1)
            if s > 0:
                act.wait_ge(R["U"], s)
            act.activation(Xs[:, :], psum[:, 2, :], ACT.Copy)
            if is_x(s):
                if s > 4:
                    act.wait_ge(R["yf"], s - 4)
                act.activation(Yps[:, :], psum[:, 3, :], ACT.Copy)
            act.drain().then_inc(R["xyE"], 1)
            for l in range(1, LV):
                for g in range(2):
                    i = 12 * s + 2 * (l - 1) + g
                    act.wait_ge(R["m1"], i + 1)
                    if i >= 2:
                        act.wait_ge(R["y"], i - 1)
                    act.activation(M1s[:, 4 * g:4 * g + 4, :], psum[:, 4 + g, :].rearrange("p (h n) -> p h n", n=P),
                                   ACT.Copy).then_inc(R["m1e"], 1)
                if s + 1 < NS and l == 1:
                    prep_scalar(act, s + 1, 1)
                if s + 1 < NS and l == 4:
                    prep_scalar(act, s + 1, 2)
            act.wait_ge(R["U"], s + 1)
            if s > 0:
                act.wait_ge(R["EU"], s)
                act.wait_ge(R["dM"], min(s, NS - 2))
            act.activation(nU[:, :], psum[:, 4, :], ACT.Copy, scale=-1.0).then_inc(R["nU"], 1)
        act.wait_ge(R["gss"], 1)
        act.activation(gst[:, 16:32], gst[:, 16:32], ACT.Sqrt).then_inc(R["gsq"], 1)

    def prep_tensor(pe, s, part):
        d, tt = STEPS[s]
        ts = slice(P * tt, P * (tt + 1))
        ds = slice(64 * d, 64 * d + 64)
        if part == 1:
            if s > 0:
                pe.wait_ge(R["a2"], s)
            pe.matmul(psum[:, 6, :], z_lwT[ds, ts], wlb[ds, :], start=True, stop=True)
            pe.matmul(psum[:, 7, :], z_laT[ds, ts], alb[ds, :], start=True, stop=True).then_inc(R["p1"], 1)
        else:
            pe.wait_ge(R["a1"], s + 1)
            pe.matmul(psum[:, 6, :], cumT[:, d, :], ew[:, :], start=True, stop=True)
            for c in range(4):
                i = pe.matmul(psum[:, 7, 2 * c:2 * c + 2], ew[:, P * c:P * (c + 1)], colm[:, d, :],
                              start=True, stop=True)
            i.then_inc(R["p2"], 1)

    def rwkv_tensor(pe):
        pe.wait_ge(R["vec"], 16 * 12)
        pe.wait_ge(R["tri"], 1)
        prep_tensor(pe, 0, 1)
        prep_tensor(pe, 0, 2)
        for s in range(NS):
            d, tt = STEPS[s]
            pe.wait_ge(R["ks"], s + 1)
            if s > 0:
                pe.wait_ge(R["upd"], 12 * s)
                pe.wait_ge(R["Mu"], min(s, NS - 2))
                pe.wait_ge(R["xyE"], s)
            names = [(Ktk[:, :], 0), (Kb[:, s % 2, :], 2), (Bb[:, s % 2, :], 3)]
            if is_x(s):
                names.append((Rtk[:, :], 1))
            for src, b in names:
                for c in range(4):
                    i = pe.transpose(psum[:, b, P * c:P * (c + 1)], src[:, P * c:P * (c + 1)], ident[:, :])
                i.then_inc(R["tr"], 1)
            if s > 0:
                pe.wait_ge(R["nU"], s)
                if s > 4:
                    pe.wait_ge(R["yf"], s - 4)
            pe.wait_ge(R["trE"], tr_before(s + 1))
            if s >= 2:
                pe.wait_ge(R["mp"], s - 1)
            n = 2 if is_x(s) else 1

            def xy(i_h):
                h = HO[i_h]
                hs, c = slice(64 * (h % 2), 64 * (h % 2) + 64), h // 2
                vs = slice(HD * h, HD * (h + 1))
                pe.wait_ge(R["gev"], H * s + i_h + 1)
                if i_h == H // 2:
                    pe.wait_ge(R["xyh"], H * s + i_h)
                for q in range(n):
                    o = psum[:, 2 + q, vs]
                    if s >= 2:
                        pe.matmul(o, KRT[hs, c, q, :], Mp[hs, d, c, :], start=True, stop=False)
                    i = pe.matmul(o, CD[:, i_h % 2, q, :], z_v[:, tt, vs], start=(s < 2), stop=True)
                i.then_inc(R["xyh"], 1)

            for i_h, h in enumerate(HO):
                hs, c = slice(64 * (h % 2), 64 * (h % 2) + 64), h // 2
                if i_h >= 2:
                    pe.wait_ge(R["gev"], H * s + i_h - 1)
                b = psum[:, 4 + i_h % 2, :].rearrange("p (s n) -> p s n", s=2)
                rhs = KRT[hs, c, 0:n, :].rearrange("p c n -> p (c n)")
                pe.matmul(b[:, 0, 0:P * n], BbT[hs, c, :], rhs, start=True, stop=True)
                pe.matmul(b[:, 1, 0:P * n], KbT[hs, c, :], rhs, start=True, stop=True).then_inc(R["gram"], 1)
                i = pe.matmul(psum[:, i_h // 4, P * (i_h % 4):P * (i_h % 4 + 1)], KRT[hs, c, 0, :], BbT[hs, c, :],
                              start=True, stop=True)
                if i_h % 4 == 3:
                    i.then_inc(R["Ap"], 1)
                if i_h >= 1:
                    xy(i_h - 1)
            xy(H - 1)
            pe.drain().then_inc(R["xy"], 1)
            if s + 1 < NS:
                prep_tensor(pe, s + 1, 1)
            for l in range(1, LV):
                for g in range(2):
                    i0 = 12 * s + 2 * (l - 1) + g
                    pe.wait_ge(R["atm"], i0 + 1)
                    if l == 1:
                        pe.wait_ge(R["T0"], 2 * s + g + 1)
                        pe.wait_ge(R["Tt0"], 2 * s + g + 1)
                    else:
                        pe.wait_ge(R["upd"], i0 - 1)
                    for h in range(4 * g, 4 * g + 4):
                        i = pe.matmul(psum[:, 4 + g, P * (h % 4):P * (h % 4 + 1)], Atm[:, h, :], Tm[:, h, :],
                                      start=True, stop=True)
                    i.then_inc(R["m1"], 1)
                for g in range(2):
                    i0 = 12 * s + 2 * (l - 1) + g
                    pe.wait_ge(R["m1e"], i0 + 1)
                    if l == 1:
                        pe.wait_ge(R["xyE"], s + 1)
                    for h in range(4 * g, 4 * g + 4):
                        cs = slice(P * (h % 4), P * (h % 4 + 1))
                        if l < LV - 1:
                            pe.matmul(psum[:, g, cs], Tt[:, h, :], M1s[:, h, :], start=True, stop=True)
                        i = pe.matmul(psum[:, 2 + g, cs], M1s[:, h, :], Tt[:, h, :], start=True, stop=True)
                    i.then_inc(R["y"], 1)
                if s + 1 < NS and l == 2:
                    prep_tensor(pe, s + 1, 2)
            pe.wait_ge(R["upd"], 12 * (s + 1))
            for i_h, h in enumerate(HO):
                vs = slice(HD * h, HD * (h + 1))
                i = pe.matmul(psum[:, 4, vs], Tt[:, i_h, :], Xs[:, vs], start=True, stop=True)
            i.then_inc(R["U"], 1)
            pe.wait_ge(R["nU"], s + 1)
            if is_x(s):
                for i_h, h in enumerate(HO):
                    vs = slice(HD * h, HD * (h + 1))
                    pe.matmul(psum[:, 5, vs], AtE[:, i_h, 1, :], nU[:, vs], start=True, stop=True)
            pe.drain().then_inc(R["EU"], 1)
            if s < NS - 2:
                for h in HO:
                    hs, c = slice(64 * (h % 2), 64 * (h % 2) + 64), h // 2
                    vs = slice(HD * h, HD * (h + 1))
                    o = psum[hs, 0, HD * c:HD * (c + 1)]
                    pe.matmul(o, Kb[:, s % 2, vs], z_v[:, tt, vs], start=True, stop=False)
                    i = pe.matmul(o, Bb[:, s % 2, vs], nU[:, vs], start=False, stop=True)
                i.then_inc(R["dM"], 1)
        pe.wait_ge(R["a2"], NS)
        for t in range(NT):
            i = pe.matmul(psum[:, 6 + t, :], z_lgT[:, P * t:P * (t + 1)], glb[:, :], start=True, stop=True)
        i.then_inc(R["gmm"], 1)

    class Seq:

        def __init__(self, c, *terms):
            self.c, self.terms = c, terms

        def v(self, off=0, mul=1):
            x = (self.c + off) * mul
            for reg, k in self.terms:
                x = reg * (k * mul) + x
            return x

        def plus(self, off):
            return Seq(self.c + off, *self.terms)

        def par(self):
            return self.c % 2

        def arrivals(self):
            x = (self.c // 2) * 16 + 16
            for reg, k in self.terms:
                x = reg * (k * 8) + x
            return x

    def sp_panel(sp, n, src):
        sp.wait_ge(s_wl, n.v(-1))
        size = src.shape[-1] * src.shape[-2]
        dst = RAW[n.par()][:, 0:size].rearrange("p (k n) -> p k n", n=src.shape[-1])
        sp.dma_start(dst, src).then_inc(s_raw[n.par()], 16)

    def act_panel(act, n, elems=4096):
        act.wait_ge(s_raw[n.par()], n.arrivals())
        act.wait_ge(s_wdone, n.v(-1))
        act.activation(WH[n.par()][:, 0:elems], RAW[n.par()][:, 0:elems], ACT.Copy).then_inc(s_wh, 1)

    def dve_panel(dve, n, elems=4096):
        dve.wait_ge(s_wh, n.v(1))
        dve.tensor_tensor(WL[n.par()][:, 0:elems], RAW[n.par()][:, 0:elems],
                          WH[n.par()][:, 0:elems].bitcast(F32), ALU.subtract).then_inc(s_wl, 1)

    def pe_panel(pe, n, k):
        pe.wait_ge(s_wl, n.v(1))
        return tuple(w[n.par()][:, :].rearrange("p (k n) -> p k n", k=k) for w in (WH, WL))

    NP0 = len(W_IN)
    act2H = Region(act_off, 8 * KB).take("act2_high", [P, KT, T], F32R)
    act2L = Region(act_off + 16 * KB, 8 * KB).take("act2_low", [P, KT, T], F32R)
    gap1 = act_off + 8 * KB
    gap2 = act_off + 24 * KB
    me = Region(free_off, 25 * KB)
    pg = me.take("pg", [P, KT, T])
    msum = me.take("msum", [P, KT, T])
    mg2 = me.take("mg2", [P, D])
    sh2 = me.take("sh2", [P, D])
    me2 = Region(after_front, 36 * KB)
    yTH = me2.take("yT_high", [P, 2, H // 2, T], F32R)
    yTL = me2.take("yT_low", [P, 2, H // 2, T], F32R)
    gt = me2.take("gates", [P, 2, KT, T])
    sc2 = me2.take("sc2", [P, D])
    n2g = Region(free_off, 4 * KB).take("n2g", [P, D])
    mg5 = Region(free_off + 4 * KB, 4 * KB).take("mg5", [P, D])
    htok = Region(free_off + 8 * KB, 8 * KB).take("htok", [P, NT, D])
    mo = Region(after_front, FREE - (after_front - free_off))
    accm = mo.take("accm", [P, NT, D])
    sg = mo.take("sg", [P, 4, T])
    hidf = mo.take("hidf", [P, 4, T])
    hidH = mo.take("hid_high", [P, 4, T], F32R)
    hidL = mo.take("hid_low", [P, 4, T], F32R)
    rwf = mo.take("rwf", [P, KT, E])
    rwH = mo.take("rw_high", [P, KT, E], F32R)
    rwL = mo.take("rw_low", [P, KT, E], F32R)
    rbias = mo.take("rbias", [P, E])
    junk2 = Region(gap1, 4 * KB).take("junk2", [P, D])
    rt_off = gap1 + 4 * KB
    rtr = Region(rt_off, 4 * KB)
    NG = 4
    GE = E // NG
    sco = rtr.take("sco", [P, NT, E])
    sel = rtr.take("sel", [P, NT, E])
    pair = rtr.take("pair", [P, NT * NG, 6])
    gs4 = rtr.take("gs4", [P, NT, NG])
    gmask = rtr.take("gmask", [P, NT, NG])
    rank4 = rtr.take("rank4", [P, NT, NG])
    rank16 = rtr.take("rank16", [P, NT, E])
    tmpr = rtr.take("tmpr", [P, NT, E])
    oh = rtr.take("oh", [P, 2, NT, E])
    mx1 = rtr.take("mx1", [P, NT])
    gate = rtr.take("gate", [P, NT, E])
    n2st = stat[:, 64:80]

    M = {name: sem("mg_" + name) for name in (
        "x_in", "gt_in", "vec_in", "yT", "yH", "yL", "pa", "pb", "ga", "gb", "mH", "mL", "wo", "x1", "v2_in",
        "rw_in", "rH", "rL", "logit", "sig", 
        "rank", "g", "silu", "u", "hid", "hH2", "hL2", "o", "acc", "x2")}

    def merge_sync(sp):
        load_panel(sp, NP0, 1, a["proj_a"][0].rearrange("(k p) n -> p k n", p=P))
        load_panel(sp, NP0 + 1, 0, a["proj_b"][0].rearrange("(k p) n -> p k n", p=P))
        for c in range(2):
            load_panel(sp, NP0 + 2 + c, (NP0 + c) % 2, full_panel(a["w_out"][0], PW * c))

    def merge_pool(pool):
        pool.wait_ge(R["done"], 1)
        pool.dma_start(xres[:, :, :], a["x"][0].rearrange("(t p) d -> p t d", p=P)).then_inc(M["x_in"], 16)
        for c in range(2):
            pool.dma_start(gt[:, c, :, :], gates_d[KT * c:KT * (c + 1)].rearrange("c p t -> p c t")
                           ).then_inc(M["gt_in"], 16)
        rows = mrow.rearrange("(v h) n -> v (h n)", h=2)
        for dst, v in ((mg2, 0), (sh2, 1), (sc2, 2)):
            pool.dma_start(dst[:, :], rows[v].partition_broadcast(P)).then_inc(M["vec_in"], 16)
        pool.wait_ge(M["yT"], 4)
        pool.iota(rank4[:, :, :], pattern=[[0, NT], [-1, NG]], base=NG, channel_multiplier=0,
                  allow_small_or_imprecise_dtypes=True)
        pool.iota(rank16[:, :, :], pattern=[[0, NT], [-1, E]], base=E, channel_multiplier=0,
                  allow_small_or_imprecise_dtypes=True).then_inc(M["rank"], 1)
        pool.wait_ge(M["mH"], 4)
        pool.wait_ge(M["mL"], 4)
        pool.dma_start(n2g[:, :], a["norm2_g"][0].partition_broadcast(P)).then_inc(M["v2_in"], 16)
        pool.dma_start(mg5[:, :], rows[3].partition_broadcast(P)).then_inc(M["v2_in"], 16)
        pool.dma_start(rwf[:, :, :], a["router_w"].rearrange("(k p) e -> p k e", p=P)).then_inc(M["rw_in"], 16)
        pool.dma_start(rbias[:, :], a["router_bias"].partition_broadcast(P)).then_inc(M["rw_in"], 16)

    def bank3(b, n=P):
        return psum[:, b, :].rearrange("p (c n) -> p c n", n=n)

    def merge_scalar(act):
        act.wait_ge(R["done"], 1)
        for j in range(4):
            act.wait_ge(M["yT"], j + 1)
            act.activation(yTH[:, j // 2, :, P * (j % 2):P * (j % 2 + 1)], bank3(j), ACT.Copy
                           ).then_inc(M["yH"], 1)
        act_panel(act, Seq(NP0 + 1))
        act_panel(act, Seq(NP0 + 2))
        for b in range(4):
            act.wait_ge(M["gb"], b + 1)
            act.activation(act2H[:, 2 * b:2 * b + 2, :], msum[:, 2 * b:2 * b + 2, :], ACT.Copy
                           ).then_inc(M["mH"], 1)
        act_panel(act, Seq(NP0 + 3))
        act_panel(act, Seq(NP0 + 4))

    def merge_vector(dve):
        for j in range(4):
            dve.wait_ge(M["yH"], j + 1)
            ts = slice(P * (j % 2), P * (j % 2 + 1))
            dve.tensor_tensor(yTL[:, j // 2, :, ts], bank3(j), yTH[:, j // 2, :, ts].bitcast(F32),
                              ALU.subtract).then_inc(M["yL"], 1)
        dve_panel(dve, Seq(NP0 + 1))
        dve.wait_ge(M["gt_in"], 32)
        for b in range(4):
            dve.wait_ge(M["pa"], b + 1)
            dve.tensor_tensor(pg[:, 2 * b:2 * b + 2, :], bank3(4 + b, T), gt[:, 0, 2 * b:2 * b + 2, :],
                              ALU.mult).then_inc(M["ga"], 1)
        dve_panel(dve, Seq(NP0 + 2))
        for b in range(4):
            dve.wait_ge(M["pb"], b + 1)
            cs = slice(2 * b, 2 * b + 2)
            dve.tensor_tensor(msum[:, cs, :], bank3(b, T), gt[:, 1, cs, :], ALU.mult)
            dve.drain()
            dve.tensor_tensor(msum[:, cs, :], msum[:, cs, :], pg[:, cs, :], ALU.add).then_inc(M["gb"], 1)
            dve.wait_ge(M["mH"], b + 1)
            dve.tensor_tensor(act2L[:, cs, :], msum[:, cs, :], act2H[:, cs, :].bitcast(F32), ALU.subtract
                              ).then_inc(M["mL"], 1)
        dve_panel(dve, Seq(NP0 + 3))
        dve_panel(dve, Seq(NP0 + 4))
        dve.wait_ge(M["x_in"], 16)
        dve.wait_ge(M["vec_in"], 48)
        for c in range(2):
            cs = slice(PW * c, PW * (c + 1))
            for t in range(NT):
                dve.wait_ge(M["wo"], NT * c + t + 1)
                b = psum[:, 4 + 2 * c + t, :]
                dve.tensor_tensor(junk2[:, cs], b, mg2[:, cs], ALU.mult)
                dve.drain()
                dve.tensor_tensor(xres[:, t, cs], xres[:, t, cs], junk2[:, cs], ALU.add)
                dve.drain().then_inc(M["x1"], 1)

    def merge_tensor(pe):
        pe.wait_ge(R["done"], 1)
        for j in range(4):
            src = yacc[:, j, :] if j < 2 else yb[:, j - 2, :]
            for c in range(4):
                i = pe.matmul(psum[:, j, P * c:P * (c + 1)], src[:, P * c:P * (c + 1)],
                              (ident if j < 2 else flip)[:, :], start=True, stop=True)
            i.then_inc(M["yT"], 1)
        for side in range(2):
            wh, wl = pe_panel(pe, Seq(NP0 + side), 4)
            if side == 0:
                pe.wait_ge(M["yL"], 4)
            for c in range(KT):
                b = (4 if side == 0 else 0) + c // 2
                for k in range(4):
                    i = three_pass(pe, psum[:, b, T * (c % 2):T * (c % 2 + 1)], wh[:, k, P * c:P * (c + 1)],
                                   wl[:, k, P * c:P * (c + 1)], yTH[:, side, k, :], yTL[:, side, k, :],
                                   k == 0, k == 3)
                if c % 2 == 1:
                    i.then_inc(M["pa" if side == 0 else "pb"], 1)
            pe.drain().then_inc(s_wdone, 1)
        pe.wait_ge(M["mL"], 4)
        pe.wait_ge(M["ga"], 4)
        for c in range(2):
            wh, wl = pe_panel(pe, Seq(NP0 + 2 + c), KT)
            for t in range(NT):
                i = token_major(pe, psum[:, 4 + 2 * c + t, :], act2H, act2L, wh, wl, t, KT)
                i.then_inc(M["wo"], 1)
            pe.drain().then_inc(s_wdone, 1)

    def token_major(pe, o, xH, xL, wh, wl, t, kt, cols=slice(None), start=True, stop=True):
        ts = slice(P * t, P * (t + 1))
        for k in range(kt):
            i = three_pass(pe, o, xH[:, k, ts], xL[:, k, ts], wh[:, k, cols], wl[:, k, cols],
                           start and k == 0, stop and k == kt - 1)
        return i

    def feature_major(pe, o, xH, xL, wh, wl, c, kt):
        cs = slice(P * c, P * (c + 1))
        for k in range(kt):
            i = three_pass(pe, o, wh[:, k, cs], wl[:, k, cs], xH[:, k, :], xL[:, k, :], k == 0, k == kt - 1)
        return i

    NM = NP0 + 4

    def route_scalar(act):
        act.wait_ge(M["x1"], 2 * NT)
        for t in range(NT):
            act.activation(htok[:, t, :], xres[:, t, :], ACT.Square, accum_out=n2st[:, t:t + 1])
        act.drain().then_inc(s_ssq, 1)
        act.wait_ge(s_var, 2)
        act.activation(n2st[:, 4:6], n2st[:, 2:4], ACT.Sqrt).then_inc(s_sqrt, 1)
        act.wait_ge(M["rw_in"], 32)
        act.activation(rwH[:, :, :], rwf[:, :, :], ACT.Copy).then_inc(M["rH"], 1)
        for j in range(4):
            act.wait_ge(s_hT, NU_T + j + 1)
            act.activation(hdst(act2H, j), bank3(j), ACT.Copy).then_inc(s_hH, 1)
        act.wait_ge(M["logit"], 1)
        act.activation(sco[:, :, :], psum[:, 4, 0:NT * E].rearrange("p (t e) -> p t e", t=NT), ACT.Sigmoid
                       ).then_inc(M["sig"], 1)

    def hdst(x, j):
        return x[:, 4 * (j % 2):4 * (j % 2) + 4, P * (j // 2):P * (j // 2 + 1)]

    def route_vector(dve):
        dve.wait_ge(s_ssq, 2)
        dve.tensor_scalar(n2st[:, 2:4], n2st[:, 0:2], 1.0 / D, EPS, ALU.mult, ALU.add).then_inc(s_var, 1)
        dve.wait_ge(M["v2_in"], 32)
        dve.scalar_tensor_tensor(out=sc2[:, :], in0=sc2[:, :], scalar=1.0, in1=n2g[:, :], op0=ALU.add,
                                 op1=ALU.mult)
        dve.wait_ge(s_sqrt, 2)
        dve.reciprocal(n2st[:, 6:8], n2st[:, 4:6])
        dve.drain()
        for t in range(NT):
            dve.scalar_tensor_tensor(out=htok[:, t, :], in0=xres[:, t, :], scalar=n2st[:, 6 + t:7 + t],
                                     in1=sc2[:, :], op0=ALU.mult, op1=ALU.mult)
            dve.drain()
            dve.tensor_tensor(htok[:, t, :], htok[:, t, :], sh2[:, :], ALU.add).then_inc(s_h, 1)
        dve.wait_ge(M["rH"], 1)
        dve.tensor_tensor(rwL[:, :, :], rwf[:, :, :], rwH[:, :, :].bitcast(F32), ALU.subtract
                          ).then_inc(M["rL"], 1)
        for j in range(4):
            dve.wait_ge(s_hH, NU_T + j + 1)
            dve.tensor_tensor(hdst(act2L, j), bank3(j), hdst(act2H, j).bitcast(F32), ALU.subtract
                              ).then_inc(s_hL, 1)
        dve.memset(accm[:, :, :], 0.0).then_inc(M["acc"], 1)
        dve.wait_ge(M["sig"], 1)
        dve.wait_ge(M["rank"], 1)
        step = lambda i: dve.drain()
        step(dve.tensor_tensor(sel[:, :, :], sco[:, :, :], rbias[:, :].unsqueeze(1).to_broadcast([P, NT, E]),
                               ALU.add))
        s4 = sel[:, :, :].rearrange("p t (g e) -> p (t g) e", e=GE)
        dve.tensor_tensor(pair[:, :, 0:3], s4[:, :, 0:3], s4[:, :, 1:4], ALU.add)
        dve.tensor_tensor(pair[:, :, 3:5], s4[:, :, 0:2], s4[:, :, 2:4], ALU.add)
        step(dve.tensor_tensor(pair[:, :, 5:6], s4[:, :, 0:1], s4[:, :, 3:4], ALU.add))
        step(dve.tensor_reduce(gs4[:, :, :].rearrange("p t g -> p (t g)"), pair[:, :, :], AX, ALU.max))

        def first_max(mask, vals, ranks, n):
            tmp = tmpr[:, :, 0:n]
            step(dve.tensor_reduce(mx1[:, :], vals, AX, ALU.max))
            step(dve.tensor_tensor(tmp, vals, bc(mx1[:, :], n), ALU.is_equal))
            step(dve.tensor_tensor(tmp, tmp, ranks, ALU.mult))
            step(dve.tensor_reduce(mx1[:, :], tmp, AX, ALU.max))
            step(dve.tensor_tensor(mask, ranks, bc(mx1[:, :], n), ALU.is_equal))

        first_max(gmask[:, :, :], gs4[:, :, :], rank4[:, :, :], NG)
        g16 = gmask[:, :, :].rearrange("p t g -> p (t g)")
        s16 = s4
        step(dve.tensor_tensor(s16, s16, bc(g16, GE), ALU.mult))
        step(dve.tensor_scalar(g16, g16, -NEG, NEG, ALU.mult, ALU.add))
        step(dve.tensor_tensor(s16, s16, bc(g16, GE), ALU.add))
        first_max(oh[:, 0, :, :], sel[:, :, :], rank16[:, :, :], E)
        step(dve.scalar_tensor_tensor(out=sel[:, :, :].rearrange("p t e -> p (t e)"),
                                      in0=oh[:, 0, :, :].rearrange("p t e -> p (t e)"), scalar=4 * NEG,
                                      in1=sel[:, :, :].rearrange("p t e -> p (t e)"),
                                      op0=ALU.mult, op1=ALU.add))
        first_max(oh[:, 1, :, :], sel[:, :, :], rank16[:, :, :], E)
        step(dve.tensor_tensor(gate[:, :, :], oh[:, 0, :, :], oh[:, 1, :, :], ALU.add))
        step(dve.tensor_tensor(gate[:, :, :], gate[:, :, :], sco[:, :, :], ALU.mult))
        step(dve.tensor_reduce(mx1[:, :], gate[:, :, :], AX, ALU.add))
        step(dve.reciprocal(mx1[:, :], mx1[:, :]))
        step(dve.tensor_tensor(gate[:, :, :], gate[:, :, :], bc(mx1[:, :], E), ALU.mult))

    def route_tensor(pe):
        for j in range(4):
            t, half = j // 2, j % 2
            pe.wait_ge(s_h, NU_T // 2 + t + 1)
            for c in range(4):
                i = pe.transpose(psum[:, j, P * c:P * (c + 1)],
                                 htok[:, t, P * (4 * half + c):P * (4 * half + c + 1)], ident[:, :])
            i.then_inc(s_hT, 1)
        pe.wait_ge(s_hL, NU_T + 4)
        pe.wait_ge(M["rL"], 1)
        for t in range(NT):
            i = token_major(pe, psum[:, 4, E * t:E * (t + 1)], act2H, act2L, rwH, rwL, t, KT)
        i.then_inc(M["logit"], 1)


    PLW = 256
    WINS = (2, 4, 8, 16)
    AW = D - PLW
    H2 = AW // HD
    DIL = (1, 4, 16)
    STEPS_BACK = 128
    ZW = PLW + 3 * AW
    RH = HD // 4 // 2
    c2 = Region(free_off + 51 * KB + 512, FREE - 51 * KB - 512)
    band = c2.take("band", [P, 4, NT, T])
    cmask = c2.take("cmask", [P, 3, 3 * P])
    cs_t = c2.take("cs_t", [P, 2, NT, RH])
    invf = c2.take("invf", [P, RH])
    posi = c2.take("posi", [P, NT], I32)
    posf = c2.take("posf", [P, NT])
    ang = c2.take("ang", [P, NT, RH])
    kint = c2.take("kint", [P, NT, RH], I32)
    kflt = c2.take("kflt", [P, NT, RH])
    g2r = Region(gap2, 8 * KB)
    cnt = g2r.take("cnt", [P, 4, T])
    dint = g2r.take("dint", [P, 3 * P], I32)
    dand = g2r.take("dand", [P, 3 * P], I32)

    C = {name: sem("c2_" + name) for name in ("iota", "vec", "done", "sin", "pos_in", "ang")}

    def const2_pool(pool):
        pool.wait_ge(M["logit"], 1)
        pool.wait_ge(s_hL, NU_T + 4)
        pool.iota(cnt[:, :, :], pattern=[[0, 4], [1, T]], base=1, channel_multiplier=0,
                  allow_small_or_imprecise_dtypes=True)
        pool.iota(dint[:, 0:P], pattern=[[-1, P]], base=2 * T, channel_multiplier=1)
        pool.iota(dint[:, P:3 * P], pattern=[[-1, 2 * P]], base=2 * T + P, channel_multiplier=1)
        for i in range(RH):
            pool.memset(invf[:, i:i + 1], float(500000.0 ** (-2.0 * i / (2 * RH))))
        pool.drain().then_inc(C["iota"], 1)
        for t in range(NT):
            pool.dma_start(posi[:, t:t + 1], a["positions_2"][0, P * t:P * (t + 1)].unsqueeze(1)
                           ).then_inc(C["pos_in"], 16)
        pool.wait_ge(C["vec"], 1)
        for g, w in enumerate(WINS):
            for st in range(NT):
                b = band[:, g, st, :]
                pool.tensor_copy(b, cnt[:, g, :])
                pool.drain()
                pool.affine_select(out=b, in_=b, compare_op=ALU.is_ge, fill=0.0, base=-P * st,
                                   pattern=[[1, T]], channel_multiplier=-1)
                pool.drain()
                pool.affine_select(out=b, in_=b, compare_op=ALU.is_ge, fill=0.0, base=P * st + w - 1,
                                   pattern=[[-1, T]], channel_multiplier=1)
                pool.drain()
                pool.tensor_tensor(b[:, P * st:P * (st + 1)], b[:, P * st:P * (st + 1)], ident[:, :],
                                   ALU.subtract)
        for g in range(3):
            for t, k in ((0, slice(0, P)), (1, slice(P, 3 * P))):
                m = cmask[:, g, k]
                n = P * (t + 1)
                pool.affine_select(out=m, in_=m, compare_op=ALU.is_ge, fill=NEG, base=P * t,
                                   pattern=[[-1, n]], channel_multiplier=1)
                pool.drain()
                pool.affine_select(out=m, in_=m, compare_op=ALU.is_ge, fill=NEG,
                                   base=STEPS_BACK * DIL[g] - P * t, pattern=[[1, n]], channel_multiplier=-1)
                pool.drain()
        pool.drain().then_inc(C["done"], 1)

    def const2_vector(dve):
        dve.wait_ge(C["iota"], 1)
        for g, w in enumerate(WINS):
            dve.tensor_scalar(cnt[:, g, :], cnt[:, g, :], float(w), None, ALU.min)
        dve.drain()
        dve.reciprocal(cnt[:, :, :], cnt[:, :, :])
        for g in range(3):
            dve.drain()
            dve.tensor_scalar(dand[:, :], dint[:, :], DIL[g] - 1, None, ALU.bitwise_and)
            dve.drain()
            dve.tensor_scalar(cmask[:, g, :], dand[:, :], 0, None, ALU.is_equal)
            dve.drain()
            dve.tensor_scalar(cmask[:, g, :], cmask[:, g, :], -NEG, NEG, ALU.mult, ALU.add)
        dve.drain().then_inc(C["vec"], 1)
        dve.wait_ge(C["pos_in"], 32)
        dve.tensor_copy(posf[:, :], posi[:, :])
        dve.drain()
        for t in range(NT):
            dve.tensor_scalar(ang[:, t, :], invf[:, :], posf[:, t:t + 1], None, ALU.mult)
        dve.drain()
        dve.tensor_scalar(kint[:, :, :], ang[:, :, :], 0.15915494309189535, None, ALU.mult)
        dve.drain()
        dve.tensor_copy(kflt[:, :, :], kint[:, :, :])
        dve.drain()
        af = ang[:, :, :].rearrange("p t r -> p (t r)")
        kf = kflt[:, :, :].rearrange("p t r -> p (t r)")
        for part in (6.28125, 0.0019350051879882812, 3.019915981956753e-07):
            dve.scalar_tensor_tensor(out=af, in0=kf, scalar=-part, in1=af, op0=ALU.mult, op1=ALU.add)
            dve.drain()
        dve.tensor_scalar(af, af, 3.1415925, -3.1415925, ALU.min, ALU.max)
        dve.drain().then_inc(C["ang"], 1)
        dve.wait_ge(C["sin"], 1)
        dve.tensor_tensor(cs_t[:, 0, :, :], cs_t[:, 0, :, :], cs_t[:, 0, :, :], ALU.mult)
        dve.drain()
        dve.tensor_scalar(cs_t[:, 0, :, :], cs_t[:, 0, :, :], -2.0, 1.0, ALU.mult, ALU.add)

    def const2_scalar(act):
        act.wait_ge(C["ang"], 1)
        act.activation(cs_t[:, 0, :, :], ang[:, :, :], ACT.Sin, scale=0.5)
        act.activation(cs_t[:, 1, :, :], ang[:, :, :], ACT.Sin)
        act.drain().then_inc(C["sin"], 1)

    class Expert:

        def __init__(self, c, i=None):
            self.c, self.i = c, i

        def count(self, mul, off):
            return Seq(self.c * mul + off, *([(self.i, 2 * mul)] if self.i is not None else []))

        def index(self):
            return self.c if self.i is None else self.i * 2 + self.c

    def expert_loop(eng, body):
        with eng.Fori(0, (E - 2) // 2) as i:
            for c in range(2):
                body(eng, Expert(c, i), False)
        body(eng, Expert(E - 2), False)
        body(eng, Expert(E - 1), True)

    def moe_src(name, e, kt):
        w = a[name][0]
        idx = e.index()
        w = w[idx] if isinstance(idx, int) else w[bass.ds(idx, 1)].rearrange("a k n -> (a k) n")
        return w.rearrange("(k p) n -> p k n", p=P)

    def moe_sync_body(sp, e, last):
        sp_panel(sp, e.count(3, NM + 1), moe_src("moe_w3", e, KT))
        if not last:
            sp_panel(sp, e.count(3, NM + 2), moe_src("moe_w1", Expert(e.c + 1, e.i), KT))
        sp_panel(sp, e.count(3, NM + (2 if last else 3)), moe_src("moe_w2", e, 4))

    def moe_sync(sp):
        sp_panel(sp, Seq(NM), moe_src("moe_w1", Expert(0), KT))
        expert_loop(sp, moe_sync_body)

    def moe_scalar_body(act, e, last):
        act.wait_ge(M["g"], e.count(1, 1).v())
        act.activation(sg[:, :, :], psum[:, 0:2, :].rearrange("p b (c n) -> p (b c) n", n=T), ACT.Silu
                       ).then_inc(M["silu"], 1)
        act_panel(act, e.count(3, NM + 2))
        act.wait_ge(M["hid"], e.count(1, 1).v())
        act.activation(hidH[:, :, :], hidf[:, :, :], ACT.Copy).then_inc(M["hH2"], 1)
        if not last:
            act_panel(act, e.count(3, NM + 3))
            act_panel(act, e.count(3, NM + 4))

    def moe_scalar(act):
        act_panel(act, Seq(NM + 1))
        expert_loop(act, moe_scalar_body)

    def moe_vector_acc(dve, e):
        dve.wait_ge(M["o"], e.count(1, 1).v())
        for t in range(NT):
            g = (gate[:, t, e.c:e.c + 1] if e.i is None else gate[:, t, bass.ds(e.i * 2 + e.c, 1)])
            dve.scalar_tensor_tensor(out=accm[:, t, :],
                                     in0=psum[:, 4 + 2 * t:6 + 2 * t, :].rearrange("p b n -> p (b n)"),
                                     scalar=g, in1=accm[:, t, :], op0=ALU.mult, op1=ALU.add)
        dve.drain().then_inc(M["acc"], 1)

    def moe_vector_body(dve, e, last):
        dve_panel(dve, e.count(3, NM + 2))
        dve.wait_ge(M["u"], e.count(1, 1).v())
        dve.wait_ge(M["silu"], e.count(1, 1).v())
        dve.tensor_tensor(hidf[:, :, :], psum[:, 2:4, :].rearrange("p b (c n) -> p (b c) n", n=T),
                          sg[:, :, :], ALU.mult).then_inc(M["hid"], 1)
        if not last:
            dve_panel(dve, e.count(3, NM + 3))
        dve.wait_ge(M["hH2"], e.count(1, 1).v())
        dve.tensor_tensor(hidL[:, :, :], hidf[:, :, :], hidH[:, :, :].bitcast(F32), ALU.subtract
                          ).then_inc(M["hL2"], 1)
        if not last:
            dve_panel(dve, e.count(3, NM + 4))
        moe_vector_acc(dve, e)

    def moe_vector(dve):
        dve_panel(dve, Seq(NM + 1))
        expert_loop(dve, moe_vector_body)
        dve.wait_ge(M["v2_in"], 32)
        for t in range(NT):
            dve.tensor_tensor(accm[:, t, :], accm[:, t, :], mg5[:, :], ALU.mult)
            dve.drain()
            dve.tensor_tensor(xres[:, t, :], xres[:, t, :], accm[:, t, :], ALU.add)
        dve.drain().then_inc(M["x2"], 1)

    def moe_w1(pe, n, e_next):
        wh, wl = pe_panel(pe, n, KT)
        for c in range(4):
            i = feature_major(pe, psum[:, c // 2, T * (c % 2):T * (c % 2 + 1)], act2H, act2L, wh, wl, c, KT)
        i.then_inc(M["g"], 1)
        pe.drain().then_inc(s_wdone, 1)

    def moe_tensor_body(pe, e, last):
        wh, wl = pe_panel(pe, e.count(3, NM + 1), KT)
        for c in range(4):
            i = feature_major(pe, psum[:, 2 + c // 2, T * (c % 2):T * (c % 2 + 1)], act2H, act2L, wh, wl, c, KT)
        i.then_inc(M["u"], 1)
        pe.drain().then_inc(s_wdone, 1)
        if not last:
            pe.wait_ge(M["silu"], e.count(1, 1).v())
            moe_w1(pe, e.count(3, NM + 2), e)
        wh, wl = pe_panel(pe, e.count(3, NM + (2 if last else 3)), 4)
        pe.wait_ge(M["hL2"], e.count(1, 1).v())
        pe.wait_ge(M["acc"], e.count(1, 1).v())
        for t in range(NT):
            for half in range(2):
                i = token_major(pe, psum[:, 4 + 2 * t + half, :], hidH, hidL, wh, wl, t, 4,
                                slice(PW * half, PW * (half + 1)))
        i.then_inc(M["o"], 1)
        pe.drain().then_inc(s_wdone, 1)

    def moe_tensor(pe):
        moe_w1(pe, Seq(NM), None)
        expert_loop(pe, moe_tensor_body)

    NB = NM + 3 * E
    FF = a["w_up_2"].shape[2]
    NQ = FF // PW
    NW2 = ZW // PW
    J_OUT = NW2
    J_UP0 = J_OUT + 2
    J_GATE = J_UP0 + 2 * NQ
    J_PLE = J_GATE + 2
    LP = J_PLE + 1
    assert LP % 2 == 0 and NQ % 2 == 0
    z2 = Region(free_off, 20 * KB).take("z2", [P, NT, ZW])
    n3b = Region(free_off + 4 * KB, 4 * KB).take("n3b", [P, D])
    n2b = Region(free_off + 14 * KB, 4 * KB).take("n2b", [P, D])
    v2 = Region(free_off + 20 * KB, 5 * KB)
    n1b = v2.take("n1b", [P, D])
    pw = v2.take("pw", [P, 2, HD])
    psc = v2.take("psc", [P, 2])
    r1 = Region(free_off + 25 * KB, 24 * KB)
    qT2 = r1.take("qT2", [P, H2 // 2, T])
    kT2 = r1.take("kT2", [P, H2 // 2, T])
    logit2 = r1.take("logit2", [P, 2, 2 * T])
    prob2 = r1.take("prob2", [P, 2, 2 * T])
    probT2 = r1.take("probT2", [P, 2, 4, P])
    r2 = Region(free_off + 25 * KB, 24 * KB)
    rel = r2.take("rel", [P, 4, T])
    sqf = r2.take("sqf", [P, 4, T])
    fH = r2.take("ff_high", [P, 4, T], F32R)
    fL = r2.take("ff_low", [P, 4, T], F32R)
    sg2 = r2.take("sg2", [P, NT, D])
    htok2 = Region(gap1, 8 * KB).take("htok2", [P, NT, D])
    g2 = Region(gap2, 8 * KB)
    ptok = g2.take("ptok", [P, NT, PLW])
    pTH = g2.take("pT_high", [P, 2, T], F32R)
    pTL = g2.take("pT_low", [P, 2, T], F32R)
    yT2 = g2.take("yT2", [P, 2, T])
    negm = stat[:, 0:24]
    mcol = stat[:, 24:48]
    l2 = stat[:, 48:72]
    lse = stat[:, 72:96]
    mx3 = stat[:, 96:104]
    e3 = stat[:, 104:128]
    sw = stat[:, 128:136]
    fac = stat[:, 136:160]
    n3st = stat[:, 160:176]

    B = {name: sem("b2_" + name) for name in (
        "n1_in", "n2_in", "n3_in", "pw_in", "p_in", "nf_in", 
        "z", "ze", "pT", "pH", "pL", "py", "pyE", "pf", "pfE", "rot", 
        "ln", "fmax", "fexp", "ao", "cT", "cH", "cL", "o", "oe", "up", "rel", "sq", "fH",
        "fL", "dn", "ffe", "gt", "gs", "pl", "x3", "outh", "store")}

    def lay(d, k, c):
        return Seq(c, (d, k)).v()

    def row(name, d):
        return a[name][bass.ds(d, 1)].rearrange("a n -> (a n)").partition_broadcast(P)

    def layer_sync(sp):
        with sp.Fori(0, L2) as d:
            def src(name, rows=slice(None), cols=slice(None)):
                w = a[name][bass.ds(d, 1)].rearrange("a k n -> (a k) n")
                return w[rows, cols].rearrange("(k p) n -> p k n", p=P)

            def panel(j, s, *terms):
                sp_panel(sp, Seq(NB + j, (d, LP), *terms), s)

            for j in range(NW2):
                panel(j, src("w_in_2", cols=slice(PW * j, PW * (j + 1))))
            for j in range(2):
                panel(J_OUT + j, src("w_out_2", cols=slice(PW * j, PW * (j + 1))))

            def up(j, q, *terms):
                panel(j, src("w_up_2", cols=bass.ds(q * PW, PW)), *terms)

            def down(j, q, *terms):
                panel(j, src("w_down_2", rows=bass.ds(q * PW, PW)), *terms)

            up(J_UP0, 0)
            sp.wait_ge(B["cL"], lay(d, 4, 4))
            sp.dma_start(n2b[:, :], row("norm2_2", d)).then_inc(B["n2_in"], 16)
            sp.dma_start(n3b[:, :], row("norm3_2", d)).then_inc(B["n3_in"], 16)
            up(J_UP0 + 1, 1)
            down(J_UP0 + 2, 0)
            with sp.Fori(0, (NQ - 2) // 2) as i:
                for c in range(2):
                    up(J_UP0 + 3 + 2 * c, i * 2 + (2 + c), (i, 4))
                    down(J_UP0 + 4 + 2 * c, i * 2 + (1 + c), (i, 4))
            down(J_GATE - 1, NQ - 1)
            for j in range(2):
                panel(J_GATE + j, src("w_gate_2", cols=slice(PW * j, PW * (j + 1))))
            panel(J_PLE, src("w_ple_2"))
        sp.wait_ge(B["outh"], 1)
        sp.dma_start(out[0].rearrange("(t p) d -> p t d", p=P), htok2[:, :, :]).then_inc(B["store"], 16)
        sp.wait_ge(B["store"], 16)

    def layer_pool(pool):
        pool.wait_ge(M["x2"], 1)
        with pool.Fori(0, L2) as d:
            pool.dma_start(n1b[:, :], row("norm1_2", d)).then_inc(B["n1_in"], 16)
            for par in range(2):
                hs = slice(64 * par, 64 * par + 64)
                w = a["pool_w_2"][bass.ds(d, 1)].rearrange("a (h g) c n -> g c (a h) n", g=2)
                s = a["pool_scale_2"][bass.ds(d, 1)].rearrange("a (h g c n) -> g c (a h) n", g=2, h=2, n=1)
                pool.dma_start(pw[hs, :, :], w[par]).then_inc(B["pw_in"], 16)
                for c in range(2):
                    pool.dma_start(psc[hs, c:c + 1], s[par, :, c, :]).then_inc(B["pw_in"], 16)
            pool.dma_start(ptok[:, :, :], a["p_2"][bass.ds(d, 1)].rearrange("a o (t p) n -> p (a o t) n", p=P)
                           ).then_inc(B["p_in"], 16)
            pool.wait_ge(B["x3"], lay(d, 1, 1))
        pool.dma_start(n1b[:, :], a["final_norm_2"].partition_broadcast(P)).then_inc(B["nf_in"], 16)

    def norm_scalar(act, cnt1):
        for t in range(NT):
            act.activation(htok2[:, t, :], xres[:, t, :], ACT.Square, accum_out=n3st[:, t:t + 1])
        act.drain().then_inc(s_ssq, 1)
        act.wait_ge(s_var, 2 + cnt1)
        act.activation(n3st[:, 4:6], n3st[:, 2:4], ACT.Sqrt).then_inc(s_sqrt, 1)

    def norm_vector(dve, cnt1, gain):
        dve.wait_ge(s_ssq, 2 + cnt1)
        dve.tensor_scalar(n3st[:, 2:4], n3st[:, 0:2], 1.0 / D, EPS, ALU.mult, ALU.add).then_inc(s_var, 1)
        dve.wait_ge(s_sqrt, 2 + cnt1)
        dve.reciprocal(n3st[:, 6:8], n3st[:, 4:6])
        dve.drain()
        for t in range(NT):
            dve.scalar_tensor_tensor(out=htok2[:, t, :], in0=xres[:, t, :], scalar=n3st[:, 6 + t:7 + t],
                                     in1=gain[:, :], op0=ALU.mult, op1=ALU.mult).then_inc(s_h, 1)

    def split_scalar(act, d, k):
        for j in range(4):
            act.wait_ge(s_hT, lay(d, 12, NU_T + 4 + 4 * k + j + 1))
            act.activation(hdst(act2H, j), bank3(j), ACT.Copy).then_inc(s_hH, 1)

    def split_vector(dve, d, k):
        for j in range(4):
            dve.wait_ge(s_hH, lay(d, 12, NU_T + 4 + 4 * k + j + 1))
            dve.tensor_tensor(hdst(act2L, j), bank3(j), hdst(act2H, j).bitcast(F32), ALU.subtract
                              ).then_inc(s_hL, 1)

    def norm_tensor(pe, d, k):
        for j in range(4):
            t, half = j // 2, j % 2
            pe.wait_ge(s_h, lay(d, 6, NU_T // 2 + 2 + 2 * k + t + 1))
            for c in range(4):
                i = pe.transpose(psum[:, j, P * c:P * (c + 1)],
                                 htok2[:, t, P * (4 * half + c):P * (4 * half + c + 1)], ident[:, :])
            i.then_inc(s_hT, 1)
        pe.wait_ge(s_hL, lay(d, 12, NU_T + 4 + 4 * k + 4))

    def heads_of(w):
        t, g, par = w // 6, w % 6 // 2, w % 2
        return t, g, par, (4 * g + par, 4 * g + par + 2)

    def two(col, t, g, par):
        at = H2 * t + 4 * g + par
        return col[:, at:at + 3:2]

    def layer_scalar(act):
        act.wait_ge(M["x2"], 1)
        with act.Fori(0, L2) as d:
            def panel(j, *terms, elems=4096):
                act_panel(act, Seq(NB + j, (d, LP), *terms), elems)

            panel(0)
            norm_scalar(act, lay(d, 3, 1))
            split_scalar(act, d, 0)
            for j in range(NW2):
                panel(j + 1)
                for t in range(NT):
                    v = NT * j + t
                    act.wait_ge(B["z"], lay(d, 10, v + 1))
                    act.activation(z2[:, t, PW * j:PW * (j + 1)], psum[:, 4 + v % 4, :], ACT.Copy
                                   ).then_inc(B["ze"], 1)
            act.wait_ge(B["pT"], lay(d, 1, 1))
            act.activation(pTH[:, :, :], bank3(3, T), ACT.Copy).then_inc(B["pH"], 1)
            act.wait_ge(B["py"], lay(d, 1, 1))
            act.activation(yT2[:, :, :], bank3(0, T), ACT.Copy).then_inc(B["pyE"], 1)
            for b in range(6):
                act.wait_ge(s_qT, lay(d, 6, 3 * NT + b + 1))
                dst = (qT2 if b < 3 else kT2)[:, 2 * (b % 3):2 * (b % 3) + 2, :]
                act.activation(dst, bank3(2 + b, T), ACT.Copy).then_inc(s_qTe, 1)
            for w in range(12):
                t, g, par, hh = heads_of(w)
                act.wait_ge(s_lg, lay(d, 12, NT * H + w + 1))
                if w >= 2:
                    act.wait_ge(s_pT, lay(d, 12, NT * H + w - 1))
                n = P * (t + 1)
                for x, h in enumerate(hh):
                    c = H2 * t + h
                    act.activation(prob2[:, w % 2, n * x:n * (x + 1)], logit2[:, w % 2, n * x:n * (x + 1)],
                                   ACT.Exp, bias=negm[:, c:c + 1], accum_out=l2[:, c:c + 1])
                act.drain().then_inc(s_ex, 1)
            act.activation(lse, l2, ACT.Ln).then_inc(B["ln"], 1)
            act.wait_ge(B["fmax"], lay(d, 1, 1))
            act.activation(e3, e3, ACT.Exp).then_inc(B["fexp"], 1)
            act.wait_ge(B["pf"], lay(d, 1, 1))
            act.activation(act2H[:, 0:2, :], z2[:, :, 0:PLW], ACT.Copy).then_inc(B["cH"], 1)
            for b in range(3):
                act.wait_ge(B["cT"], lay(d, 3, b + 1))
                act.activation(act2H[:, 2 + 2 * b:4 + 2 * b, :], bank3(b, T), ACT.Copy).then_inc(B["cH"], 1)
            panel(J_OUT + 1)
            panel(J_UP0)
            act.wait_ge(B["oe"], lay(d, 4, 4))
            norm_scalar(act, lay(d, 3, 2))
            panel(J_UP0 + 1)
            split_scalar(act, d, 1)

            def relu(c, *terms):
                act.wait_ge(B["up"], Seq(c + 1, (d, NQ), *terms).v())
                b = 2 * (c % 2)
                act.activation(rel[:, :, :], psum[:, b:b + 2, :].rearrange("p b (c n) -> p (b c) n", n=T),
                               ACT.Relu).then_inc(B["rel"], 1)

            def high(c, *terms, first=False):
                act.wait_ge(B["sq"], Seq(c + 1, (d, NQ), *terms).v())
                if not first:
                    act.wait_ge(B["dn"], Seq(c, (d, NQ), *terms).v())
                act.activation(fH[:, :, :], sqf[:, :, :], ACT.Copy).then_inc(B["fH"], 1)

            relu(0)
            high(0, first=True)
            panel(J_UP0 + 2)
            relu(1)
            panel(J_UP0 + 3)
            with act.Fori(0, (NQ - 2) // 2) as i:
                for c in range(2):
                    high(1 + c, (i, 2))
                    panel(J_UP0 + 4 + 2 * c, (i, 4))
                    relu(2 + c, (i, 2))
                    panel(J_UP0 + 5 + 2 * c, (i, 4))
            high(NQ - 1)
            panel(J_GATE)
            act.wait_ge(B["ffe"], lay(d, 1, 1))
            norm_scalar(act, lay(d, 3, 3))
            split_scalar(act, d, 2)
            panel(J_GATE + 1)
            for c in range(2):
                for t in range(NT):
                    act.wait_ge(B["gt"], lay(d, 4, NT * c + t + 1))
                    act.activation(sg2[:, t, PW * c:PW * (c + 1)], psum[:, 2 * c + t, :], ACT.Sigmoid
                                   ).then_inc(B["gs"], 1)
                if c == 0:
                    panel(J_PLE, elems=PLW // P * D)
            act.wait_ge(B["x3"], lay(d, 1, 1))
        norm_scalar(act, 3 * L2 + 1)

    def layer_vector(dve):
        dve.wait_ge(C["done"], 1)
        with dve.Fori(0, L2) as d:
            def panel(j, *terms, elems=4096):
                dve_panel(dve, Seq(NB + j, (d, LP), *terms), elems)

            panel(0)
            dve.wait_ge(B["n1_in"], lay(d, 16, 16))
            norm_vector(dve, lay(d, 3, 1), n1b)
            split_vector(dve, d, 0)
            for j in range(NW2):
                panel(j + 1)
            dve.wait_ge(B["ze"], lay(d, 10, 10))
            dve.wait_ge(B["pH"], lay(d, 1, 1))
            dve.tensor_tensor(pTL[:, :, :], bank3(3, T), pTH[:, :, :].bitcast(F32), ALU.subtract
                              ).then_inc(B["pL"], 1)
            for t in range(NT):
                qk = z2[:, t, PLW:PLW + 2 * AW].rearrange("p (h d) -> p h d", d=HD)
                x1, x2 = qk[:, :, 0:RH], qk[:, :, RH:2 * RH]
                co, si = (cs_t[:, i, t, :].unsqueeze(1).to_broadcast([P, 2 * H2, RH]) for i in range(2))
                tmp = [htok2[:, t, 2 * H2 * RH * i:2 * H2 * RH * (i + 1)].rearrange("p (h r) -> p h r", r=RH)
                       for i in range(4)]
                dve.tensor_tensor(tmp[0], x1, co, ALU.mult)
                dve.tensor_tensor(tmp[1], x2, si, ALU.mult)
                dve.tensor_tensor(tmp[2], x2, co, ALU.mult)
                dve.tensor_tensor(tmp[3], x1, si, ALU.mult)
                dve.drain()
                dve.tensor_tensor(x1, tmp[0], tmp[1], ALU.subtract)
                dve.tensor_tensor(x2, tmp[2], tmp[3], ALU.add)
            dve.drain().then_inc(B["rot"], 1)
            dve.wait_ge(B["pfE"], lay(d, 1, 1))
            for c in range(2):
                dve.tensor_scalar(z2[:, c, 0:PLW], psum[:, 1, T * c:T * (c + 1)], psc[:, c:c + 1], None, ALU.mult)
            dve.drain().then_inc(B["pf"], 1)
            for w in range(13):
                if w < 12:
                    t, g, par, hh = heads_of(w)
                    n = P * (t + 1)
                    dve.wait_ge(s_S, lay(d, 12, NT * H + w + 1))
                    lg = logit2[:, w % 2, 0:2 * n].rearrange("p (h n) -> p h n", h=2)
                    k = slice(0, P) if t == 0 else slice(P, 3 * P)
                    dve.scalar_tensor_tensor(out=lg,
                                             in0=psum[:, w % 2, 0:2 * n].rearrange("p (h n) -> p h n", h=2),
                                             scalar=HD ** -0.5,
                                             in1=cmask[:, g, k].unsqueeze(1).to_broadcast([P, 2, n]),
                                             op0=ALU.mult, op1=ALU.add)
                    dve.drain()
                    dve.tensor_reduce(two(mcol, t, g, par), lg, AX, ALU.max)
                    dve.drain()
                    dve.tensor_scalar(two(negm, t, g, par), two(mcol, t, g, par), -1.0, None, ALU.mult)
                    dve.drain().then_inc(s_lg, 1)
                if w >= 1:
                    j = w - 1
                    n = P * (j // 6 + 1)
                    dve.wait_ge(s_pT, lay(d, 12, NT * H + j + 1))
                    if j >= 2:
                        dve.wait_ge(s_pv, lay(d, 12, NT * H + j - 1))
                    dve.tensor_copy(probT2[:, j % 2, 0:2 * n // P, :], bank3(2 + j % 2)[:, 0:2 * n // P, :]
                                    ).then_inc(s_pTe, 1)
            dve.wait_ge(B["ln"], lay(d, 1, 1))
            dve.tensor_tensor(lse, lse, mcol, ALU.add)
            dve.reciprocal(l2, l2)
            dve.drain()
            by_g = lambda x: x.rearrange("p (t g j) -> p t j g", t=NT, g=3)
            view = lambda x: x.rearrange("p (t j) -> p t j", t=NT)
            dve.tensor_reduce(view(mx3), by_g(lse), AX, ALU.max)
            dve.drain()
            for t in range(NT):
                dve.tensor_tensor(e3[:, H2 * t:H2 * (t + 1)].rearrange("p (g j) -> p g j", g=3),
                                  lse[:, H2 * t:H2 * (t + 1)].rearrange("p (g j) -> p g j", g=3),
                                  mx3[:, 4 * t:4 * t + 4].unsqueeze(1).to_broadcast([P, 3, 4]), ALU.subtract)
            dve.drain().then_inc(B["fmax"], 1)
            dve.wait_ge(B["fexp"], lay(d, 1, 1))
            dve.tensor_reduce(view(sw), by_g(e3), AX, ALU.add)
            dve.drain()
            dve.tensor_tensor(e3, e3, l2, ALU.mult)
            dve.drain()
            dve.reciprocal(sw, sw)
            dve.drain()
            for t in range(NT):
                dve.tensor_tensor(fac[:, H2 * t:H2 * (t + 1)].rearrange("p (g j) -> p g j", g=3),
                                  e3[:, H2 * t:H2 * (t + 1)].rearrange("p (g j) -> p g j", g=3),
                                  sw[:, 4 * t:4 * t + 4].unsqueeze(1).to_broadcast([P, 3, 4]), ALU.mult)
            dve.drain()
            dve.wait_ge(s_pv, lay(d, 12, NT * H + 12))
            for t in range(NT):
                ao = z2[:, t, PLW:PLW + AW].rearrange("p (h d) -> p h d", d=HD)
                dve.tensor_tensor(ao[:, 0:8, :], bank3(4 + 2 * t, HD), bc(fac[:, H2 * t:H2 * t + 8], HD), ALU.mult)
                dve.tensor_tensor(ao[:, 8:12, :], bank3(5 + 2 * t, HD)[:, 0:4, :],
                                  bc(fac[:, H2 * t + 8:H2 * t + 12], HD), ALU.mult)
            dve.drain().then_inc(B["ao"], 1)
            dve.wait_ge(B["cH"], lay(d, 4, 1))
            dve.tensor_tensor(act2L[:, 0:2, :], z2[:, :, 0:PLW], act2H[:, 0:2, :].bitcast(F32), ALU.subtract
                              ).then_inc(B["cL"], 1)
            for b in range(3):
                dve.wait_ge(B["cH"], lay(d, 4, b + 2))
                cs = slice(2 + 2 * b, 4 + 2 * b)
                dve.tensor_tensor(act2L[:, cs, :], bank3(b, T), act2H[:, cs, :].bitcast(F32), ALU.subtract
                                  ).then_inc(B["cL"], 1)
            panel(J_OUT + 1)
            for c in range(2):
                if c == 1:
                    panel(J_UP0)
                for t in range(NT):
                    dve.wait_ge(B["o"], lay(d, 4, NT * c + t + 1))
                    cs = slice(PW * c, PW * (c + 1))
                    dve.tensor_tensor(xres[:, t, cs], xres[:, t, cs], psum[:, 4 + 2 * c + t, :], ALU.add)
                    dve.drain().then_inc(B["oe"], 1)
            dve.wait_ge(B["n2_in"], lay(d, 16, 16))
            norm_vector(dve, lay(d, 3, 2), n2b)
            panel(J_UP0 + 1)
            split_vector(dve, d, 1)

            def square(c, *terms):
                dve.wait_ge(B["rel"], Seq(c + 1, (d, NQ), *terms).v())
                dve.tensor_tensor(sqf[:, :, :], rel[:, :, :], rel[:, :, :], ALU.mult).then_inc(B["sq"], 1)

            def low(c, *terms):
                dve.wait_ge(B["fH"], Seq(c + 1, (d, NQ), *terms).v())
                dve.tensor_tensor(fL[:, :, :], sqf[:, :, :], fH[:, :, :].bitcast(F32), ALU.subtract
                                  ).then_inc(B["fL"], 1)
                dve.drain()

            square(0)
            low(0)
            panel(J_UP0 + 2)
            square(1)
            panel(J_UP0 + 3)
            with dve.Fori(0, (NQ - 2) // 2) as i:
                for c in range(2):
                    low(1 + c, (i, 2))
                    panel(J_UP0 + 4 + 2 * c, (i, 4))
                    square(2 + c, (i, 2))
                    panel(J_UP0 + 5 + 2 * c, (i, 4))
            low(NQ - 1)
            panel(J_GATE)
            dve.wait_ge(B["dn"], lay(d, NQ, NQ))
            for t in range(NT):
                dve.tensor_tensor(xres[:, t, :], xres[:, t, :],
                                  psum[:, 4 + 2 * t:6 + 2 * t, :].rearrange("p b n -> p (b n)"), ALU.add)
            dve.drain().then_inc(B["ffe"], 1)
            dve.wait_ge(B["n3_in"], lay(d, 16, 16))
            norm_vector(dve, lay(d, 3, 3), n3b)
            split_vector(dve, d, 2)
            panel(J_GATE + 1)
            panel(J_PLE, elems=PLW // P * D)
            dve.wait_ge(B["gs"], lay(d, 4, 4))
            dve.wait_ge(B["pl"], lay(d, 1, 1))
            for t in range(NT):
                dve.tensor_tensor(sg2[:, t, :], psum[:, 4 + 2 * t:6 + 2 * t, :].rearrange("p b n -> p (b n)"),
                                  sg2[:, t, :], ALU.mult)
            dve.drain()
            for t in range(NT):
                dve.tensor_tensor(xres[:, t, :], xres[:, t, :], sg2[:, t, :], ALU.add)
            dve.drain().then_inc(B["x3"], 1)
        dve.wait_ge(B["nf_in"], 16)
        norm_vector(dve, 3 * L2 + 1, n1b)
        dve.drain().then_inc(B["outh"], 1)

    def layer_tensor(pe):
        pe.wait_ge(C["done"], 1)
        with pe.Fori(0, L2) as d:
            def panel(j, k, *terms):
                return pe_panel(pe, Seq(NB + j, (d, LP), *terms), k)

            def used():
                pe.drain().then_inc(s_wdone, 1)

            norm_tensor(pe, d, 0)
            for j in range(NW2):
                wh, wl = panel(j, KT)
                for t in range(NT):
                    v = NT * j + t
                    if v >= 4:
                        pe.wait_ge(B["ze"], lay(d, 10, v - 3))
                    token_major(pe, psum[:, 4 + v % 4, :], act2H, act2L, wh, wl, t, KT).then_inc(B["z"], 1)
                used()
            pe.wait_ge(B["p_in"], lay(d, 16, 16))
            for k in range(2):
                for t in range(NT):
                    i = pe.transpose(psum[:, 3, T * k + P * t:T * k + P * (t + 1)], ptok[:, t, P * k:P * (k + 1)],
                                     ident[:, :])
            i.then_inc(B["pT"], 1)
            pe.wait_ge(B["ze"], lay(d, 10, 10))
            pe.wait_ge(B["pw_in"], lay(d, 96, 96))
            for g in range(4):
                for st in range(NT):
                    i = pe.matmul(psum[64 * (g % 2):64 * (g % 2) + 64, 0, T * (g // 2):T * (g // 2 + 1)],
                                  z2[:, st, HD * g:HD * (g + 1)], band[:, g, st, :], start=(st == 0),
                                  stop=(st == NT - 1))
            i.then_inc(B["py"], 1)
            pe.wait_ge(B["rot"], lay(d, 1, 1))
            pe.wait_ge(B["pL"], lay(d, 1, 1))
            pe.wait_ge(B["pyE"], lay(d, 1, 1))
            for b in range(6):
                for x in range(2):
                    at = PLW + AW * (b // 3) + P * (2 * (b % 3) + x)
                    for t in range(NT):
                        i = pe.transpose(psum[:, 2 + b, T * x + P * t:T * x + P * (t + 1)], z2[:, t, at:at + P],
                                         ident[:, :])
                i.then_inc(s_qT, 1)
            for g in range(4):
                hs = slice(64 * (g % 2), 64 * (g % 2) + 64)
                i = pe.matmul(psum[hs, 1, T * (g // 2):T * (g // 2 + 1)], pw[hs, g // 2, :], yT2[hs, g // 2, :],
                              start=True, stop=True)
            pe.drain().then_inc(B["pfE"], 1)
            for w in range(14):
                if w < 12:
                    t, g, par, hh = heads_of(w)
                    n = P * (t + 1)
                    if w == 0:
                        pe.wait_ge(s_qTe, lay(d, 6, 3 * NT + 6))
                        pe.wait_ge(B["pf"], lay(d, 1, 1))
                    if w >= 2:
                        pe.wait_ge(s_lg, lay(d, 12, NT * H + w - 1))
                    hs = slice(64 * par, 64 * par + 64)
                    for x, h in enumerate(hh):
                        i = pe.matmul(psum[:, w % 2, n * x:n * (x + 1)], qT2[hs, h // 2, P * t:P * (t + 1)],
                                      kT2[hs, h // 2, 0:n], start=True, stop=True)
                    i.then_inc(s_S, 1)
                if 1 <= w <= 12:
                    j = w - 1
                    n = P * (j // 6 + 1)
                    pe.wait_ge(s_ex, lay(d, 12, NT * H + j + 1))
                    if j >= 2:
                        pe.wait_ge(s_pTe, lay(d, 12, NT * H + j - 1))
                    for c in range(2 * n // P):
                        i = pe.transpose(psum[:, 2 + j % 2, P * c:P * (c + 1)], prob2[:, j % 2, P * c:P * (c + 1)],
                                         ident[:, :])
                    i.then_inc(s_pT, 1)
                if w >= 2:
                    j = w - 2
                    t, g, par, hh = heads_of(j)
                    pe.wait_ge(s_pTe, lay(d, 12, NT * H + j + 1))
                    for x, h in enumerate(hh):
                        o = psum[:, 4 + 2 * t + h // 8, HD * (h % 8):HD * (h % 8 + 1)]
                        for k in range(t + 1):
                            at = PLW + 2 * AW + HD * h
                            i = pe.matmul(o, probT2[:, j % 2, (t + 1) * x + k, :], z2[:, k, at:at + HD],
                                          start=(k == 0), stop=(k == t))
                    i.then_inc(s_pv, 1)
            pe.wait_ge(B["ao"], lay(d, 1, 1))
            for b in range(3):
                for x in range(2):
                    at = PLW + P * (2 * b + x)
                    for t in range(NT):
                        i = pe.transpose(psum[:, b, T * x + P * t:T * x + P * (t + 1)], z2[:, t, at:at + P],
                                         ident[:, :])
                i.then_inc(B["cT"], 1)
            pe.wait_ge(B["cL"], lay(d, 4, 4))
            for c in range(2):
                wh, wl = panel(J_OUT + c, KT)
                for t in range(NT):
                    token_major(pe, psum[:, 4 + 2 * c + t, :], act2H, act2L, wh, wl, t, KT).then_inc(B["o"], 1)
                used()
            norm_tensor(pe, d, 1)

            def up(c, *terms):
                pt = [(r, 2 * k) for r, k in terms]
                wh, wl = panel(J_UP0 + (0 if c == 0 else 2 * c - 1), KT, *pt)
                if c >= 2:
                    pe.wait_ge(B["rel"], Seq(c - 1, (d, NQ), *terms).v())
                for j in range(4):
                    o = psum[:, 2 * (c % 2) + j // 2, T * (j % 2):T * (j % 2 + 1)]
                    i = feature_major(pe, o, act2H, act2L, wh, wl, j, KT)
                i.then_inc(B["up"], 1)
                used()

            def down(c, *terms):
                pt = [(r, 2 * k) for r, k in terms]
                wh, wl = panel(J_GATE - 1 if c == NQ - 1 else J_UP0 + 2 * c + 2, 4, *pt)
                pe.wait_ge(B["fL"], Seq(c + 1, (d, NQ), *terms).v())
                for t in range(NT):
                    for half in range(2):
                        i = token_major(pe, psum[:, 4 + 2 * t + half, :], fH, fL, wh, wl, t, 4,
                                        slice(PW * half, PW * (half + 1)), start=(c == 0 and not terms),
                                        stop=(c == NQ - 1))
                i.then_inc(B["dn"], 1)
                used()

            up(0)
            up(1)
            down(0)
            with pe.Fori(0, (NQ - 2) // 2) as i_q:
                for c in range(2):
                    up(2 + c, (i_q, 2))
                    down(1 + c, (i_q, 2))
            down(NQ - 1)
            norm_tensor(pe, d, 2)
            for c in range(2):
                wh, wl = panel(J_GATE + c, KT)
                for t in range(NT):
                    token_major(pe, psum[:, 2 * c + t, :], act2H, act2L, wh, wl, t, KT).then_inc(B["gt"], 1)
                used()
            wh, wl = panel(J_PLE, 4)
            pw_h = WH[(NB + J_PLE) % 2][:, 0:PLW // P * D].rearrange("p (k n) -> p k n", n=D)
            pw_l = WL[(NB + J_PLE) % 2][:, 0:PLW // P * D].rearrange("p (k n) -> p k n", n=D)
            for t in range(NT):
                for half in range(2):
                    i = token_major(pe, psum[:, 4 + 2 * t + half, :], pTH, pTL, pw_h, pw_l, t, PLW // P,
                                    slice(PW * half, PW * (half + 1)))
            i.then_inc(B["pl"], 1)
            used()

    block = ctx.enter_context(nc.Block())

    @block.sync
    def _(sp):
        front_sync(sp)
        merge_sync(sp)
        moe_sync(sp)
        layer_sync(sp)

    @block.gpsimd
    def _(pool):
        front_pool(pool)
        att_pool(pool)
        rwkv_pool(pool)
        merge_pool(pool)
        const2_pool(pool)
        layer_pool(pool)

    @block.scalar
    def _(act):
        front_scalar(act)
        att_scalar(act)
        rwkv_scalar(act)
        merge_scalar(act)
        route_scalar(act)
        const2_scalar(act)
        moe_scalar(act)
        layer_scalar(act)

    @block.vector
    def _(dve):
        front_vector(dve)
        att_vector(dve)
        rwkv_vector(dve)
        merge_vector(dve)
        route_vector(dve)
        const2_vector(dve)
        moe_vector(dve)
        layer_vector(dve)

    @block.tensor
    def _(pe):
        front_tensor(pe)
        att_tensor(pe)
        rwkv_tensor(pe)
        merge_tensor(pe)
        route_tensor(pe)
        moe_tensor(pe)
        layer_tensor(pe)

    ctx.close()


_INS = ("x", "c", "ctx", "c_ctx", "mod_w", "mod_b", "norm1_g", "norm2_g", "w_in", "rw_w0", "rw_w_lora_b", "rw_a0",
        "rw_a_lora_b", "rw_g_lora_b", "rw_k_k", "rw_k_a", "rw_r_k", "rw_ln_g", "rw_ln_b", "na_q_g", "na_k_g",
        "na_rpb", "proj_a", "proj_b", "w_out", "router_w", "router_bias", "moe_w1", "moe_w3", "moe_w2", "p_2",
        "positions_2", "norm1_2", "w_in_2", "pool_w_2", "pool_scale_2", "w_out_2", "norm2_2", "w_up_2",
        "w_down_2", "norm3_2", "w_gate_2", "w_ple_2", "final_norm_2")


def kernel(**inputs):
    import numpy as _np
    import concourse.bacc as _bacc
    from concourse import mybir as _mybir
    from concourse.bass_utils import run_bass_kernel_spmd as _run

    nc = _bacc.Bacc("TRN2", target_bir_lowering=False, num_devices=1)
    arrays, aps = {}, {}
    for name in _INS:
        v = _np.ascontiguousarray(inputs[name])
        arrays[f"in_{name}_dram"] = v
        aps[name] = nc.dram_tensor(f"in_{name}_dram", v.shape, _mybir.dt.from_np(v.dtype),
                                   kind="ExternalInput").ap()
    out = nc.dram_tensor("out_0_dram", inputs["x"].shape, _mybir.dt.from_np(_np.dtype("float32")),
                         kind="ExternalOutput").ap()
    two_block_kernel(nc, aps, out)
    r = _run(nc, [arrays], core_ids=[0])
    return r.results[0]["out_0_dram"]
```

```python
from contextlib import ExitStack

import concourse.bass as bass
from concourse import mybir

F32 = mybir.dt.float32
F32R = mybir.dt.float32r
I32 = mybir.dt.int32
ALU = mybir.AluOpType
ACT = mybir.ActivationFunctionType
AX = mybir.AxisListType.X

P = 128
KB = 1024


def two_block_kernel(nc, a, out):
    T, D = a["x"].shape[1], a["x"].shape[2]
    KT = D // P
    NT = T // P
    DA = a["rw_w0"].shape[2]
    HD = 64
    H = DA // HD
    PW = 512
    E = a["router_w"].shape[1]
    L2 = a["norm1_2"].shape[0]
    EPS = 1e-6
    NEG = -1e30

    ctx = ExitStack()
    base = (nc.sbuf_base + 63) // 64 * 64

    def sb(name, shape, dt, offset):
        return nc.alloc_sbuf_tensor_at(name, shape, dt, offset=offset)

    class Region:

        def __init__(self, start, size):
            self.at, self.end = start, start + size

        def take(self, name, shape, dt=F32):
            size = 4
            for s in shape[1:]:
                size *= s
            t = sb(name, shape, dt, self.at)
            self.at += (size + 31) // 32 * 32
            assert self.at <= self.end, (name, self.at - self.end)
            return t

    def sem(name):
        return ctx.enter_context(nc.semaphore(name))

    def mod_bc(ap, shape):
        return ap.to_broadcast(shape)

    ring = Region(base, 96 * KB)
    RAW = [ring.take(f"raw{i}", [P, 4096]) for i in range(2)]
    WH = [None, None]
    WL = [None, None]
    for i in range(2):
        WH[i] = ring.take(f"w_high{i}", [P, 4096], F32R)
        WL[i] = ring.take(f"w_low{i}", [P, 4096], F32R)
    slot0_off = base + 32 * KB
    act_off = ring.at
    acts = Region(act_off, 32 * KB)
    actH = acts.take("act_high", [P, KT, 2 * T], F32R)
    actL = acts.take("act_low", [P, KT, 2 * T], F32R)
    keep = Region(acts.end, 14 * KB)
    xres = keep.take("xres", [P, NT, D])
    ident = keep.take("ident", [P, P])
    flip = keep.take("flip", [P, P])
    ones = keep.take("ones", [P, P])
    stat = keep.take("stat", [P, 256])
    free_off = keep.end
    FREE = nc.sbuf_usable_end - free_off

    mrow = nc.dram_tensor("mrow", (8, PW), F32, kind="Internal").ap()
    gates_d = nc.dram_tensor("gates_d", (2 * KT, P, T), F32, kind="Internal").ap()

    psum = ctx.enter_context(nc.psum_tensor("psum", [P, 8, 512], F32))

    front = Region(free_off, FREE)
    z_k = front.take("z_k", [P, 2 * NT, DA])
    z_v = front.take("z_v", [P, 2 * NT, DA])
    z_r = front.take("z_r", [P, NT, DA])
    z_lwT = front.take("z_lwT", [P, 2 * T])
    z_laT = front.take("z_laT", [P, 2 * T])
    z_lgT = front.take("z_lgT", [P, T])
    after_front = front.at
    modw = [front.take(f"modw{i}", [P, KT, PW]) for i in range(2)]
    after_modw = front.at
    early = Region(free_off, after_front - free_off)
    ctx_in = early.take("ctx_in", [P, NT, D])
    mbc = early.take("mbc", [P, 4, D])
    tail = Region(after_modw, free_off + FREE - after_modw)
    cc = tail.take("cc", [P, 2, KT])
    ccs = tail.take("ccs", [P, 2, KT])
    macc = tail.take("macc", [P, 2, PW])
    macc_c = Region(slot0_off + 32 * KB, 4 * KB).take("macc_c", [P, 2, PW])
    g1 = Region(slot0_off + 36 * KB, 4 * KB).take("g1", [P, D])
    hbuf = Region(slot0_off + 40 * KB, 8 * KB).take("hbuf", [P, 2, D])
    junk = Region(slot0_off + 48 * KB, 4 * KB).take("junk", [P, D])
    modb = tail.take("modb", [12, PW])
    mstage = tail.take("mstage", [1, PW])
    gstage = Region(acts.end, 8 * KB).take("gstage", [P, 2, 2, 2 * P])

    s_const = sem("const_ready")
    s_cc = sem("c_in")
    s_small = sem("small_in")
    s_x = sem("x_in")
    s_modw = [sem("modw_in0"), sem("modw_in1")]
    s_ccs = sem("silu_ready")
    s_sig = sem("sigmoid_c")
    s_macc = sem("macc_ready")
    s_mread = sem("modw_read")
    s_mps = sem("mod_psum")
    s_mev = sem("mod_evac")
    s_mrow = sem("mrow_out")
    s_ssq = sem("ssq_ready")
    s_var = sem("var_ready")
    s_sqrt = sem("sqrt_ready")
    s_h = sem("h_ready")
    s_hT = sem("hT_psum")
    s_hH = sem("hT_high")
    s_hL = sem("hT_low")
    s_raw = [sem("raw_in0"), sem("raw_in1")]
    s_wh = sem("w_high_ready")
    s_wl = sem("w_low_ready")
    s_wdone = sem("w_used")
    s_unit = sem("win_unit")
    s_uev = sem("win_evac")
    s_gst = [sem("gates_out0"), sem("gates_out1")]

    def full_panel(w, col, width=PW):
        return w[:, col:col + width].rearrange("(k p) n -> p k n", p=P)

    def load_panel(sp, n, par, src, elems=4096):
        if not isinstance(n, int) or n >= 2:
            sp.wait_ge(s_wl, n - 1)
        dst = RAW[par][:, 0:elems]
        if len(src.shape) == 3:
            dst = dst.rearrange("p (k n) -> p k n", n=src.shape[2])
        sp.dma_start(dst, src).then_inc(s_raw[par], 16)

    def panel_arrivals(n):
        return (n // 2) * 16 + 16

    def split_high(act, n, par, arrived, elems=4096):
        act.wait_ge(s_raw[par], arrived)
        if not isinstance(n, int) or n >= 2:
            act.wait_ge(s_wdone, n - 1)
        act.activation(WH[par][:, 0:elems], RAW[par][:, 0:elems], ACT.Copy).then_inc(s_wh, 1)

    def split_low(dve, n, par, elems=4096):
        dve.wait_ge(s_wh, n + 1)
        dve.tensor_tensor(WL[par][:, 0:elems], RAW[par][:, 0:elems],
                          WH[par][:, 0:elems].bitcast(F32), ALU.subtract).then_inc(s_wl, 1)

    def three_pass(pe, o, aH, aL, wH, wL, start, stop):
        pe.matmul(o, aH, wH, start=start, stop=False)
        pe.matmul(o, aH, wL, start=False, stop=False)
        return pe.matmul(o, aL, wH, start=False, stop=stop)

    r0, k0, v0 = 0, DA, 2 * DA
    l0 = 3 * DA
    q0, kb0, vb0 = l0 + 3 * P, l0 + 3 * P + DA, l0 + 3 * P + 2 * DA
    g0 = l0 + 3 * P + 3 * DA
    W_IN = [(k0, PW, "k"), (v0, PW, "v"), (r0, PW, "r"), (l0, 3 * P, "lora")]
    W_IN += [(g0 + PW * i, PW, f"gate{i}") for i in range(4)]
    W_IN += [(q0, PW, "q"), (kb0, PW, "kb"), (vb0, PW, "vb")]
    UNITS = {"k": 4, "v": 4, "kb": 4, "vb": 4, "r": 2, "q": 2, "lora": 3}
    NU_T = 2 * 2 * NT
    RB = 6
    unit0 = []
    u = NU_T
    for _, _, what in W_IN:
        unit0.append(u)
        u += UNITS.get(what, 2)
    NU = u
    N_MOD = 12

    att_in = Region(after_front, free_off + FREE - after_front)
    z_q = att_in.take("z_q", [P, NT, DA])
    z_kb = att_in.take("z_kb", [P, 2 * NT, DA])
    z_vb = att_in.take("z_vb", [P, 2 * NT, DA])

    def mod_load(sp, m):
        if m >= 2:
            sp.wait_ge(s_macc, m - 1)
            sp.wait_ge(s_mread, min(m - 1, 4))
        sp.dma_start(modw[m % 2][:, :, :],
                     a["mod_w"][0][:, PW * m:PW * (m + 1)].rearrange("(p k) n -> p k n", p=P)
                     ).then_inc(s_modw[m % 2], 16)

    def mod_sum(dve, m):
        dve.wait_ge(s_modw[m % 2], 16 * (m // 2 + 1))
        if m >= 2:
            dve.wait_ge(s_mps, m - 1)
        w = modw[m % 2]
        sides = [(0, macc)] + ([(1, macc_c)] if m < 4 else [])
        for side, acc in sides:
            dve.tensor_scalar(acc[:, m % 2, :], w[:, 0, :], ccs[:, side, 0:1], None, ALU.mult)
        for k in range(1, KT):
            dve.drain()
            for side, acc in sides if k < KT // 2 else sides[:1]:
                i = dve.scalar_tensor_tensor(out=acc[:, m % 2, :], in0=w[:, k, :],
                                             scalar=ccs[:, side, k:k + 1], in1=acc[:, m % 2, :],
                                             op0=ALU.mult, op1=ALU.add)
        i.then_inc(s_macc, 1)

    def mod_reduce(pe, m):
        if m >= 1:
            pe.wait_ge(s_mev, m)
        if m < 4:
            pe.wait_ge(s_ccs, 1)
            pe.wait_ge(s_modw[m % 2], 16 * (m // 2 + 1))
            for k in range(KT // 2, KT):
                i = pe.matmul(psum[:, 7, :], mod_bc(ccs[:, 1, k:k + 1], [P, P]), modw[m % 2][:, k, :],
                              start=(k == KT // 2), stop=False)
            i.then_inc(s_mread, 1)
        pe.wait_ge(s_macc, m + 1)
        for side, acc in [(0, macc)] + ([(1, macc_c)] if m < 4 else []):
            pe.matmul(psum[:, 6 + side, :], ones[:, :], acc[:, m % 2, :], start=(side == 0), stop=False)
            i = pe.matmul(psum[:, 6 + side, :], mod_bc(ident[0:N_MOD, m:m + 1], [N_MOD, P]), modb[:, :],
                          start=False, stop=True)
        i.then_inc(s_mps, 1)

    def mod_evac(act, m):
        act.wait_ge(s_mps, m + 1)
        if m < 4:
            dst = slice(PW * (m % 2), PW * (m % 2 + 1))
            act.activation(mbc[:, m // 2, dst], psum[:, 6, :], ACT.Copy)
            act.activation(mbc[:, 2 + m // 2, dst], psum[:, 7, :], ACT.Copy).then_inc(s_mev, 1)
        else:
            if m > 4:
                act.wait_ge(s_mrow, 16 * (m - 4))
            act.activation(mstage[:, :], psum[0:1, 6, :], ACT.Copy).then_inc(s_mev, 1)

    def mod_store(q, m):
        q.wait_ge(s_mev, m + 1)
        q.dma_start(mrow[m - 4:m - 3, :], mstage[:, :]).then_inc(s_mrow, 16)

    def token_tile(t):
        return xres[:, t, :] if t < NT else ctx_in[:, t - NT, :]

    def front_pool(pool):
        pool.memset(ident[:, :], 0.0)
        pool.memset(ones[:, :], 1.0)
        pool.drain()
        pool.affine_select(out=ident[:, :], in_=ident[:, :], compare_op=ALU.not_equal, fill=1.0,
                           base=0, pattern=[[-1, P]], channel_multiplier=1)
        pool.memset(flip[:, :], 0.0)
        pool.drain()
        for half in range(2):
            cs = slice(64 * half, 64 * half + 64)
            pool.affine_select(out=flip[:, cs], in_=flip[:, cs], compare_op=ALU.not_equal, fill=1.0,
                               base=-63 - 64 * half, pattern=[[1, 64]], channel_multiplier=1)
        pool.drain().then_inc(s_const, 1)
        pool.dma_start(g1[:, :], a["norm1_g"][0].partition_broadcast(P)).then_inc(s_small, 16)
        for m in range(4, N_MOD):
            mod_store(pool, m)
        pool.wait_ge(s_mrow, 16 * (N_MOD - 4))

    def front_sync(sp):
        sp.dma_start(modb[:, :], a["mod_b"][0].rearrange("(m n) -> m n", n=PW)).then_inc(s_cc, 16)
        sp.dma_start(cc[:, 0, :], a["c"].rearrange("o (p k) -> (o p) k", p=P)).then_inc(s_cc, 16)
        sp.dma_start(cc[:, 1, :], a["c_ctx"].rearrange("(p k) -> p k", p=P)).then_inc(s_cc, 16)
        for m in range(6):
            mod_load(sp, m)
            if m == 2:
                for dst, src in ((xres, a["x"]), (ctx_in, a["ctx"])):
                    sp.dma_start(dst[:, :, :], src[0].rearrange("(t p) d -> p t d", p=P)).then_inc(s_x, 16)
            if m >= 2 and m < 4:
                load_panel(sp, m - 2, m % 2, full_panel(a["w_in"][0], W_IN[m - 2][0]))
        for n, (col, width, what) in enumerate(W_IN):
            if n >= 2:
                load_panel(sp, n, n % 2, full_panel(a["w_in"][0], col, width), KT * width)
            if n + 4 >= 6 and n + 4 < N_MOD:
                mod_load(sp, n + 4)

    def front_vector(dve):
        dve.wait_ge(s_sig, 1)
        dve.tensor_tensor(ccs[:, :, :], cc[:, :, :], ccs[:, :, :], ALU.mult)
        dve.drain().then_inc(s_ccs, 1)
        for m in range(4):
            mod_sum(dve, m)
            if m == 2:
                dve.drain()
                dve.wait_ge(s_ssq, 1)
                dve.tensor_scalar(stat[:, 4:8], stat[:, 0:4], 1.0 / D, EPS, ALU.mult, ALU.add).then_inc(s_var, 1)
        dve.wait_ge(s_sqrt, 1)
        dve.reciprocal(stat[:, 12:16], stat[:, 8:12])
        dve.wait_ge(s_mev, 4)
        dve.wait_ge(s_small, 16)
        for side in range(2):
            dve.scalar_tensor_tensor(out=mbc[:, 2 * side + 1, :], in0=mbc[:, 2 * side + 1, :], scalar=1.0,
                                     in1=g1[:, :], op0=ALU.add, op1=ALU.mult)
        dve.drain()
        for t in range(2 * NT):
            if t >= 2:
                dve.wait_ge(s_hT, 2 * (t - 1))
            dve.scalar_tensor_tensor(out=hbuf[:, t % 2, :], in0=token_tile(t), scalar=stat[:, 12 + t:13 + t],
                                     in1=mbc[:, 2 * (t // NT) + 1, :], op0=ALU.mult, op1=ALU.mult)
            dve.drain()
            dve.tensor_tensor(hbuf[:, t % 2, :], hbuf[:, t % 2, :], mbc[:, 2 * (t // NT), :],
                              ALU.add).then_inc(s_h, 1)
            if t >= 1:
                front_low(dve, t - 1)
        front_low(dve, 2 * NT - 1)
        for n in range(len(W_IN)):
            if n < 2:
                dve.wait_ge(s_hT, NU_T)
            split_low(dve, n, n % 2, KT * W_IN[n][1])
            if n + 4 < N_MOD:
                mod_sum(dve, n + 4)

    def hT_dst(dst, u):
        t, half = u // 2, u % 2
        return dst[:, 4 * half:4 * half + 4, P * t:P * (t + 1)]

    def front_low(dve, t):
        for u in (2 * t, 2 * t + 1):
            dve.wait_ge(s_hH, u + 1)
            dve.tensor_tensor(hT_dst(actL, u), psum[:, u % RB, :].rearrange("p (k n) -> p k n", n=P),
                              hT_dst(actH, u).bitcast(F32), ALU.subtract).then_inc(s_hL, 1)

    def front_scalar(act):
        act.wait_ge(s_cc, 48)
        act.activation(ccs[:, :, :], cc[:, :, :], ACT.Sigmoid).then_inc(s_sig, 1)
        for m in range(2):
            mod_evac(act, m)
        act.wait_ge(s_x, 32)
        for t in range(2 * NT):
            i = act.activation(junk[:, :], token_tile(t), ACT.Square, accum_out=stat[:, t:t + 1])
            act.drain()
        act.drain().then_inc(s_ssq, 1)
        act.wait_ge(s_var, 1)
        act.activation(stat[:, 8:12], stat[:, 4:8], ACT.Sqrt).then_inc(s_sqrt, 1)
        for m in range(2, 4):
            mod_evac(act, m)
        for u in range(NU_T):
            act.wait_ge(s_hT, u + 1)
            act.activation(hT_dst(actH, u), psum[:, u % RB, :].rearrange("p (k n) -> p k n", n=P),
                           ACT.Copy).then_inc(s_hH, 1)
        split_high(act, 0, 0, 16, KT * W_IN[0][1])
        for n, (col, width, what) in enumerate(W_IN):
            if n + 1 < len(W_IN):
                split_high(act, n + 1, (n + 1) % 2, panel_arrivals(n + 1), KT * W_IN[n + 1][1])
            if n + 4 < N_MOD:
                mod_evac(act, n + 4)
            for j in range(UNITS.get(what, 2)):
                u = unit0[n] + j
                act.wait_ge(s_unit, u - NU_T + 1)
                src = psum[:, u % RB, :]
                if what == "lora":
                    if j == 2:
                        act.activation(z_lgT[:, :], src[:, 0:T], ACT.Sigmoid).then_inc(s_uev, 1)
                    elif j == 1:
                        act.activation(z_laT[:, :], src, ACT.Copy).then_inc(s_uev, 1)
                    else:
                        act.activation(z_lwT[:, :], src, ACT.Tanh).then_inc(s_uev, 1)
                elif what.startswith("gate"):
                    g = 2 * int(what[4:]) + j
                    if g >= 2:
                        act.wait_ge(s_gst[g % 2], 16 * (g // 2))
                    act.activation(gstage[:, g % 2, :, :], src.rearrange("p (c t) -> p c t", c=2),
                                   ACT.Sigmoid).then_inc(s_uev, 1)
                    act.wait_ge(s_uev, u - NU_T + 1)
                    act.dma_start(gates_d[2 * g:2 * g + 2].rearrange("c p t -> p c t"),
                                  gstage[:, g % 2, :, :]).then_inc(s_gst[g % 2], 16)
                else:
                    if what == "q" and j == 0:
                        act.wait_ge(s_macc, N_MOD)
                    dst = {"k": z_k, "v": z_v, "r": z_r, "q": z_q, "kb": z_kb, "vb": z_vb}[what]
                    act.activation(dst[:, j, :], src, ACT.Copy).then_inc(s_uev, 1)

        for i in range(2):
            act.wait_ge(s_gst[i], 64)

    def wait_bank(pe, u):
        if u - RB < 0:
            return
        if u - RB < NU_T:
            pe.wait_ge(s_hL, u - RB + 1)
        else:
            pe.wait_ge(s_uev, u - RB - NU_T + 1)

    def front_tensor(pe):
        pe.wait_ge(s_const, 1)
        pe.wait_ge(s_cc, 48)
        for m in range(4):
            mod_reduce(pe, m)
        for u in range(NU_T):
            t, half = u // 2, u % 2
            pe.wait_ge(s_h, t + 1)
            wait_bank(pe, u)
            for j in range(4):
                c = 4 * half + j
                i = pe.transpose(psum[:, u % RB, P * j:P * (j + 1)], hbuf[:, t % 2, P * c:P * (c + 1)],
                                 ident[:, :])
            i.then_inc(s_hT, 1)
        pe.wait_ge(s_hL, NU_T)
        for n, (col, width, what) in enumerate(W_IN):
            pe.wait_ge(s_wl, n + 1)
            wh = WH[n % 2][:, 0:KT * width].rearrange("p (k n) -> p k n", k=KT)
            wl = WL[n % 2][:, 0:KT * width].rearrange("p (k n) -> p k n", k=KT)
            for j in range(UNITS.get(what, 2)):
                u = unit0[n] + j
                wait_bank(pe, u)
                bank = psum[:, u % RB, :]
                if what == "lora" or what.startswith("gate"):
                    toks = 2 * T if what == "lora" and j < 2 else T
                    chunks = [j] if what == "lora" else [2 * j, 2 * j + 1]
                    for ci, c in enumerate(chunks):
                        o = bank[:, T * ci:T * ci + toks]
                        for k in range(KT):
                            cs = slice(P * c, P * (c + 1))
                            i = three_pass(pe, o, wh[:, k, cs], wl[:, k, cs], actH[:, k, 0:toks],
                                           actL[:, k, 0:toks], k == 0, k == KT - 1)
                else:
                    for k in range(KT):
                        ts = slice(P * j, P * (j + 1))
                        i = three_pass(pe, bank, actH[:, k, ts], actL[:, k, ts], wh[:, k, :], wl[:, k, :],
                                       k == 0, k == KT - 1)
                i.then_inc(s_unit, 1)
            pe.drain().then_inc(s_wdone, 1)
            if n + 4 < N_MOD:
                mod_reduce(pe, n + 4)

    NW = NU - NU_T
    BW = PW // 2
    attw = Region(act_off, 32 * KB)
    qT = [attw.take(f"qT{i}", [P, H // 2, T]) for i in range(2)]
    kT = attw.take("kT", [P, H // 2, 2 * T])
    logit = attw.take("logit", [P, 2, BW])
    prob = attw.take("prob", [P, 2, 2 * T])
    probT = attw.take("probT", [P, 2, 4, P])
    sq = keep.take("sq", [P, 2 * T])
    qg = keep.take("qg", [P, 2, HD])
    rtab = keep.take("rtab", [15 * H, P])
    attf = Region(att_in.at, free_off + FREE - att_in.at)
    bias = attf.take("bias", [P, NT, H, BW])
    yb = attf.take("yb", [P, NT, DA])
    rtab_d = nc.dram_tensor("rtab_d", (15 * H, P), F32, kind="Internal").ap()
    qk_ss = stat[:, 16:64]
    qk_rs = stat[:, 64:112]
    lsum = stat[:, 112:144].rearrange("p (s i) -> p s i", s=2)
    nmax = stat[:, 144:160]
    mx = stat[:, 160:192].rearrange("p (s i) -> p s i", s=2)

    s_qg = sem("qk_gains_in")
    s_rt = sem("rpb_in")
    s_rz = sem("rpb_zeroed")
    s_rtd = sem("rpb_table_out")
    s_bias = [sem("bias_in0"), sem("bias_in1")]
    s_mask = sem("bias_masked")
    s_qss = sem("qk_squares")
    s_qsq = sem("qk_sqrt")
    s_qn = sem("qk_normed")
    s_qT = sem("qkT_psum")
    s_qTe = sem("qkT_ready")
    s_S = sem("logits")
    s_lg = sem("logits_biased")
    s_ex = sem("exp_done")
    s_pT = sem("probT_psum")
    s_pTe = sem("probT_ready")
    s_pv = sem("pv_done")
    s_yb = sem("yb_ready")

    def bias_rows(q, t):
        for i in range(2 * t, 2 * t + 2):
            for h in range(H):
                src = bass.AP(rtab_d.tensor, (h * 15 + 7 - i) * P, [[1, 64], [P, 4], [1, 64]])
                q.dma_start(bias[64 * (i % 2):64 * (i % 2) + 64, t, h, :]
                            .rearrange("p (a k) -> p a k", a=4), src).then_inc(s_bias[t], 16)

    def att_sync(sp):
        sp.wait_ge(s_rtd, 16)
        bias_rows(sp, 0)

    def att_pool(pool):
        pool.wait_ge(s_macc, N_MOD)
        pool.wait_ge(s_mps, N_MOD)
        pool.dma_start(qg[:, 0, :], a["na_q_g"][0].partition_broadcast(P)).then_inc(s_qg, 16)
        pool.dma_start(qg[:, 1, :], a["na_k_g"][0].partition_broadcast(P)).then_inc(s_qg, 16)
        pool.memset(rtab[:, :], 0.0).then_inc(s_rz, 1)
        pool.wait_ge(s_rz, 1)
        pool.dma_start(rtab[:, 48:48 + 31], a["na_rpb"][0].rearrange("h r c -> (h r) c")).then_inc(s_rt, 16)
        pool.wait_ge(s_rt, 16)
        pool.dma_start(rtab_d, rtab[:, :]).then_inc(s_rtd, 16)
        pool.wait_ge(s_rtd, 16)
        bias_rows(pool, 1)
        pool.wait_ge(s_unit, NW)
        for par in range(2):
            hs = slice(64, 128) if par == 0 else slice(0, 64)
            pool.memset(qT[par][hs, :, :], 0.0)
            pool.drain().then_inc(s_const, 1)
        for t in range(NT):
            pool.wait_ge(s_bias[t], 16 * 2 * H)
            for half in range(2):
                b = bias[64 * half:64 * half + 64, t, :, :].rearrange("p h (a k) -> p (h a) k", a=4)
                pool.affine_select(out=b[:, :, 0:48], in_=b[:, :, 0:48], compare_op=ALU.is_ge, fill=NEG,
                                   base=8 - 63, pattern=[[0, 32], [1, 48]], channel_multiplier=1)
                pool.drain()
                pool.affine_select(out=b[:, :, 16:64], in_=b[:, :, 16:64], compare_op=ALU.is_ge, fill=NEG,
                                   base=63 + 7 - 16, pattern=[[0, 32], [-1, 48]], channel_multiplier=-1)
                pool.drain().then_inc(s_mask, 1)

    def heads(ap):
        return ap.rearrange("p t (h d) -> p (t h) d", d=HD)

    def bc(ap, n):
        return ap.unsqueeze(2).to_broadcast([ap.shape[0], ap.shape[1], n])

    def att_vector(dve):
        dve.wait_ge(s_uev, NW - 2 * NT)
        parts = [(z_q, t, t) for t in range(NT)] + [(z_kb, t, NT + t) for t in range(2 * NT)]
        for z, t, c in parts:
            dve.tensor_tensor(sq[:, :], z[:, t, :], z[:, t, :], ALU.mult)
            dve.drain()
            i = dve.tensor_reduce(qk_ss[:, H * c:H * c + H], sq[:, :].rearrange("p (h d) -> p h d", d=HD),
                                  AX, ALU.add)
            dve.drain()
        dve.tensor_scalar(qk_ss, qk_ss, 1.0 / HD, EPS, ALU.mult, ALU.add).then_inc(s_qss, 1)
        dve.wait_ge(s_qsq, 1)
        dve.reciprocal(qk_rs, qk_rs)
        dve.wait_ge(s_qg, 32)
        dve.tensor_scalar(qg[:, 0, :], qg[:, 0, :], HD ** -0.5, None, ALU.mult)
        dve.drain()
        for z, t, c in parts:
            zt = z[:, t, :].rearrange("p (h d) -> p h d", d=HD)
            dve.tensor_tensor(zt, zt, bc(qk_rs[:, H * c:H * c + H], HD), ALU.mult)
            dve.drain()
            g = qg[:, 0 if c < NT else 1, :].unsqueeze(1).to_broadcast([P, H, HD])
            dve.tensor_tensor(zt, zt, g, ALU.mult).then_inc(s_qn, 1)
        for i in range(NT * H + 1):
            if i < NT * H:
                t, h = i // H, i % H
                dve.wait_ge(s_S, i + 1)
                if h == 0:
                    dve.wait_ge(s_mask, 2 * (t + 1))
                dve.tensor_tensor_reduce(out=logit[:, i % 2, :], in0=psum[:, i % 2, 0:BW],
                                         in1=bias[:, t, h, :], scale=1.0, scalar=NEG, op0=ALU.add,
                                         op1=ALU.max, accum_out=mx[:, 0, i:i + 1])
                dve.tensor_reduce(mx[:, 1, i:i + 1], psum[:, i % 2, BW:2 * BW], AX, ALU.max)
                dve.drain()
                dve.tensor_scalar(nmax[:, i:i + 1], mx[:, 0, i:i + 1], mx[:, 1, i:i + 1], -1.0, ALU.max,
                                  ALU.mult).then_inc(s_lg, 1)
            if i >= 1:
                j = i - 1
                dve.wait_ge(s_pT, j + 1)
                if j >= 2:
                    dve.wait_ge(s_pv, j - 1)
                dve.tensor_copy(probT[:, j % 2, :, :],
                                psum[:, 2 + j % 2, :].rearrange("p (c n) -> p c n", c=4)).then_inc(s_pTe, 1)
        dve.wait_ge(s_ex, NT * H)
        dve.tensor_tensor(lsum[:, 0, :], lsum[:, 0, :], lsum[:, 1, :], ALU.add)
        dve.drain()
        dve.reciprocal(lsum[:, 0, :], lsum[:, 0, :])
        dve.wait_ge(s_pv, NT * H)
        dve.drain()
        for t in range(NT):
            dve.tensor_tensor(yb[:, t, :].rearrange("p (h d) -> p h d", d=HD),
                              psum[:, 4 + t, :].rearrange("p (h d) -> p h d", d=HD),
                              bc(lsum[:, 0, H * t:H * t + H], HD), ALU.mult).then_inc(s_yb, 1)

    def att_scalar(act):
        act.wait_ge(s_qss, 1)
        act.activation(qk_rs, qk_ss, ACT.Sqrt).then_inc(s_qsq, 1)
        for b in range(3 * NT):
            act.wait_ge(s_qT, b + 1)
            src = psum[:, b, :].rearrange("p (c n) -> p c n", c=4)
            if b < NT:
                for par in range(2):
                    hs = slice(64 * par, 64 * par + 64)
                    act.activation(qT[par][hs, :, P * b:P * b + P], src[hs], ACT.Copy)
                act.drain().then_inc(s_qTe, 1)
            else:
                act.activation(kT[:, :, P * (b - NT):P * (b - NT) + P], src, ACT.Copy).then_inc(s_qTe, 1)
        for i in range(NT * H):
            act.wait_ge(s_lg, i + 1)
            if i >= 2:
                act.wait_ge(s_pT, i - 1)
            act.activation(prob[:, i % 2, 0:BW], logit[:, i % 2, :], ACT.Exp, bias=nmax[:, i:i + 1],
                           accum_out=lsum[:, 0, i:i + 1])
            act.activation(prob[:, i % 2, BW:2 * BW], psum[:, i % 2, BW:2 * BW], ACT.Exp,
                           bias=nmax[:, i:i + 1], accum_out=lsum[:, 1, i:i + 1])
            act.drain().then_inc(s_ex, 1)

    def att_tensor(pe):
        pe.wait_ge(s_uev, NW)
        for b in range(3 * NT):
            pe.wait_ge(s_qn, b + 1)
            z, t = (z_q, b) if b < NT else (z_kb, b - NT)
            for j in range(4):
                i = pe.matmul(psum[:, b, P * j:P * (j + 1)], z[:, t, P * j:P * (j + 1)],
                              (flip if b < NT else ident)[:, :], start=True, stop=True)
            i.then_inc(s_qT, 1)
        for i in range(NT * H + 2):
            if i < NT * H:
                t, h = i // H, i % H
                if i == 0:
                    pe.wait_ge(s_qTe, 3 * NT)
                    pe.wait_ge(s_const, 3)
                if i >= 2:
                    pe.wait_ge(s_ex, i - 1)
                pe.matmul(psum[:, i % 2, :], qT[h % 2][:, h // 2, P * t:P * (t + 1)], kT[:, h // 2, :],
                          start=True, stop=True).then_inc(s_S, 1)
            if 1 <= i <= NT * H:
                j = i - 1
                pe.wait_ge(s_ex, j + 1)
                if j >= 2:
                    pe.wait_ge(s_pTe, j - 1)
                for c in range(4):
                    ins = pe.transpose(psum[:, 2 + j % 2, P * c:P * (c + 1)], prob[:, j % 2, P * c:P * (c + 1)],
                                       ident[:, :])
                ins.then_inc(s_pT, 1)
            if i >= 2:
                j = i - 2
                t, h = j // H, j % H
                pe.wait_ge(s_pTe, j + 1)
                for c in range(4):
                    ins = pe.matmul(psum[:, 4 + t, HD * h:HD * (h + 1)], probT[:, j % 2, c, :],
                                    z_vb[:, c, HD * h:HD * (h + 1)], start=(c == 0), stop=(c == 3))
                ins.then_inc(s_pv, 1)

    STEPS = [(0, 2), (1, 3), (0, 3), (1, 2), (0, 0), (1, 1), (0, 1), (1, 0)]
    NS = len(STEPS)
    LV = 7
    C0 = float(2.718281828459045 ** -0.5)

    rk = Region(slot0_off, 32 * KB)
    maskF = rk.take("maskF", [P, LV, P])
    maskR = rk.take("maskR", [P, LV, P])
    tri2 = rk.take("tri2", [P, 2, 2, P])
    cumT = rk.take("cumT", [P, 2, P])
    colm = rk.take("colm", [P, 2, 2])
    w0b_off = rk.at
    w0b = rk.take("w0b", [P, 2, DA])
    a0b = rk.take("a0b", [P, 2, DA])
    kkb = rk.take("kkb", [P, DA])
    kab = rk.take("kab", [P, DA])
    alb = rk.take("alb", [P, 2, DA])
    xr = Region(acts.end, 8 * KB)
    wlb = xr.take("wlb", [P, 2, DA])
    KRT1 = xr.take("KRT1", [P, H // 2, 2, P])

    rf = Region(after_front, 36 * KB)
    ew = rf.take("ew", [P, DA])
    ea = rf.take("ea", [P, DA])
    kkn = rf.take("kkn", [P, DA])
    Ktk = rf.take("Ktk", [P, DA])
    Rtk = rf.take("Rtk", [P, DA])
    epos = rf.take("epos", [P, DA])
    kdir = rf.take("kdir", [P, DA])
    Kb = rf.take("Kb", [P, 2, DA])
    Bb = rf.take("Bb", [P, 2, DA])
    KRT = [rf.take("KRT0", [P, H // 2, 2, P]), KRT1]
    KbT = rf.take("KbT", [P, H // 2, P])
    BbT = rf.take("BbT", [P, H // 2, P])
    CD = rf.take("CD", [P, 2, 2, P])
    Mst = rf.take("Mst", [P, 2, H // 2, HD])
    Mp = rf.take("Mp", [P, 2, H // 2, HD])
    ra = Region(act_off, 32 * KB)
    AtE = ra.take("AtE", [P, H, 2, P])
    Tm = ra.take("Tm", [P, H, P])
    Tt = ra.take("Tt", [P, H, P])
    M1s = ra.take("M1s", [P, H, P])
    Xs = ra.take("Xs", [P, DA])
    yacc = ra.take("yacc", [P, NT, DA])
    nU = ra.take("nU", [P, DA])
    Yps_off = rk.at
    Yps = rk.take("Yps", [P, DA])
    fin = Region(w0b_off, 8 * KB)
    glb = fin.take("glb", [P, DA])
    rkb = fin.take("rkb", [P, DA])
    lngb = fin.take("lngb", [P, DA])
    lnbb = fin.take("lnbb", [P, DA])
    idx = Region(Yps_off, 2 * KB)
    ixor = idx.take("ixor", [P, P], I32)
    ixp = idx.take("ixp", [P, P], I32)
    ixs = idx.take("ixs", [P, P], I32)
    krs = stat[:, 192:224]
    facs = stat[:, 224:240].rearrange("p (s c) -> p s c", s=2)
    kq = stat[:, 0:32]
    gst = stat[:, 32:64]

    HO = [h for par in range(2) for h in range(par, H, 2)]

    R = {name: sem("rk_" + name) for name in (
        "iota", "tri", "vec", "vec2", "krs", "kd", "p1", "e1", "a1", "p2", "e3", "a2", "ks",
        "tr", "trE", "gram", "gev", "Ap", "T0", "tmu", "xyh", "xy", "xyE", "mp", "m1", "m1e",
        "y", "upd", "U", "nU", "EU", "yf", "dM", "Mu", "gmm", "done")}

    def tr_before(s):
        return 3 * s if s <= 4 else 12 + 4 * (s - 4)

    def is_x(s):
        return s >= 4

    def rwkv_pool(pool):
        pool.wait_ge(s_gst[0], 64)
        pool.wait_ge(s_gst[1], 64)
        pool.iota(ixp[:, :], pattern=[[0, P]], base=0, channel_multiplier=1)
        pool.iota(ixor[:, :], pattern=[[1, P]], base=0, channel_multiplier=0)
        pool.drain().then_inc(R["iota"], 1)
        for d in range(2):
            for dst, src in [(w0b[:, d, :], a["rw_w0"][0, d].partition_broadcast(P)),
                             (a0b[:, d, :], a["rw_a0"][0, d].partition_broadcast(P))]:
                pool.dma_start(dst, src).then_inc(R["vec"], 16)
        for dst, src in [(kkb[:, :], a["rw_k_k"][0].partition_broadcast(P)),
                         (kab[:, :], a["rw_k_a"][0].partition_broadcast(P)),
                         (wlb[0:64, 0, :], a["rw_w_lora_b"][0, 0]), (wlb[64:128, 1, :], a["rw_w_lora_b"][0, 1]),
                         (alb[0:64, 0, :], a["rw_a_lora_b"][0, 0]), (alb[64:128, 1, :], a["rw_a_lora_b"][0, 1])]:
            pool.dma_start(dst, src).then_inc(R["vec"], 16)
        pool.memset(tri2[:, :, :, :], 1.0)
        pool.memset(cumT[:, :, :], 1.0)
        pool.memset(colm[:, :, :], 0.0)
        for d in range(2):
            hs = slice(64, 128) if d == 0 else slice(0, 64)
            pool.drain()
            pool.memset(wlb[hs, d, :], 0.0)
            pool.memset(alb[hs, d, :], 0.0)
            if d == 1:
                pool.memset(KRT[d][hs, :, :, :], 0.0)
        pool.drain()
        for d, sgn in ((0, 1), (1, -1)):
            for incl in range(2):
                pool.affine_select(out=tri2[:, d, incl, :], in_=tri2[:, d, incl, :], compare_op=ALU.is_ge,
                                   fill=0.0, base=incl - 1, pattern=[[sgn, P]], channel_multiplier=-sgn)
                pool.drain()
            pool.affine_select(out=cumT[:, d, :], in_=cumT[:, d, :], compare_op=ALU.is_ge,
                               fill=0.0, base=0, pattern=[[sgn, P]], channel_multiplier=-sgn)
        pool.drain()
        pool.memset(colm[0:64, 0, 0:1], 1.0)
        pool.drain()
        pool.memset(colm[64:128, 0, 1:2], 1.0)
        pool.drain()
        pool.memset(colm[64:128, 1, 0:1], 1.0)
        pool.drain()
        pool.memset(colm[0:64, 1, 1:2], 1.0)
        pool.drain()
        for d in range(2):
            half = slice(0, 64) if d == 0 else slice(64, 128)
            pool.tensor_scalar(cumT[half, d, :], cumT[half, d, :], -1.0, None, ALU.add)
            pool.drain()
        pool.drain().then_inc(R["tri"], 1)
        pool.wait_ge(s_pv, NT * H)
        pool.wait_ge(s_yb, NT)
        pool.memset(KRT[0][64:128, :, :, :], 0.0)
        pool.drain().then_inc(s_const, 1)
        pool.wait_ge(R["krs"], 1)
        for s in range(NS):
            prep_on_pool(pool, s)
        pool.wait_ge(R["e1"], NS)
        for dst, src in [(glb[:, :], a["rw_g_lora_b"][0]),
                         (rkb[:, :], a["rw_r_k"][0].rearrange("h d -> (h d)").partition_broadcast(P)),
                         (lngb[:, :], a["rw_ln_g"][0].partition_broadcast(P)),
                         (lnbb[:, :], a["rw_ln_b"][0].partition_broadcast(P))]:
            pool.dma_start(dst, src).then_inc(R["vec2"], 16)

    def prep_on_pool(pool, s):
        tt = STEPS[s][1]
        pool.tensor_tensor(kkn[:, :], z_k[:, tt, :], kkb[:, :], ALU.mult)
        pool.drain()
        pool.tensor_tensor(hv(kkn[:, :]), hv(kkn[:, :]), bc(krs[:, H * tt:H * tt + H], HD), ALU.mult)
        pool.drain()
        pool.wait_ge(R["kd"], s + 1)
        pool.tensor_tensor(ea[:, :], ea[:, :], kkn[:, :], ALU.mult)
        pool.drain()
        pool.wait_ge(R["a2"], s + 1)
        if s >= 2:
            pool.wait_ge(R["dM"], s - 1)
        pool.tensor_tensor(Kb[:, s % 2, :], kdir[:, :], epos[:, :], ALU.mult)
        pool.tensor_tensor(Bb[:, s % 2, :], ea[:, :], epos[:, :], ALU.mult)
        pool.tensor_tensor(Ktk[:, :], Ktk[:, :], kkn[:, :], ALU.mult)
        if is_x(s):
            pool.tensor_tensor(Rtk[:, :], Rtk[:, :], z_r[:, tt, :], ALU.mult)
        pool.drain().then_inc(R["ks"], 1)

    def mb(m):
        return m.unsqueeze(1).to_broadcast([P, 4, P])

    def hv(ap):
        return ap.rearrange("p (h d) -> p h d", d=HD)

    def prep_vector(dve, s, part):
        d, tt = STEPS[s]
        if part == 1:
            dve.wait_ge(R["p1"], s + 1)
            if s > 0:
                dve.wait_ge(R["p2"], s)
                dve.wait_ge(R["ks"], s)
            dve.tensor_tensor(ew[:, :], psum[:, 6, :], w0b[:, d, :], ALU.add)
            dve.tensor_tensor(ea[:, :], psum[:, 7, :], a0b[:, d, :], ALU.add)
            dve.drain().then_inc(R["e1"], 1)
        elif part == 3:
            dve.wait_ge(R["p2"], s + 1)
            if s > 0:
                dve.wait_ge(R["tr"], tr_before(s))
            dve.tensor_tensor(Ktk[:, :], psum[:, 6, :], ew[:, :], ALU.subtract)
            dve.wait_ge(R["a1"], s + 1)
            dve.scalar_tensor_tensor(out=kdir[:, :], in0=ea[:, :], scalar=-1.0, in1=kab[:, :],
                                     op0=ALU.add, op1=ALU.mult)
            dve.drain().then_inc(R["e3"], 1)
        elif part == 4:
            dve.scalar_tensor_tensor(out=kdir[:, :], in0=kdir[:, :], scalar=1.0, in1=z_k[:, tt, :],
                                     op0=ALU.add, op1=ALU.mult).then_inc(R["kd"], 1)

    def post_vector(dve, t, part):
        sums, var = gst[:, H * t:H * t + H], gst[:, 16 + H * t:16 + H * t + H]
        y = yacc[:, t, :]
        if part == 1:
            dve.wait_ge(R["vec2"], 16 * 4)
            dve.wait_ge(R["ks"], NS)
            dve.tensor_reduce(sums, hv(y), AX, ALU.add)
            dve.tensor_tensor(kdir[:, :], z_r[:, t, :], z_k[:, t, :], ALU.mult)
            dve.drain()
        elif part == 2:
            dve.tensor_scalar(sums, sums, 1.0 / HD, None, ALU.mult)
            dve.tensor_tensor(kdir[:, :], kdir[:, :], rkb[:, :], ALU.mult)
            dve.drain()
            dve.tensor_tensor(hv(y), hv(y), bc(sums, HD), ALU.subtract)
            dve.tensor_reduce(krs[:, H * t:H * t + H], hv(kdir[:, :]), AX, ALU.add)
            dve.drain()
        elif part == 3:
            dve.wait_ge(R["p2"], NS)
            dve.tensor_tensor(ew[:, :], y, y, ALU.mult)
            dve.drain()
            dve.tensor_reduce(var, hv(ew[:, :]), AX, ALU.add)
            dve.drain()
            dve.tensor_scalar(var, var, 1.0 / HD, 64e-5, ALU.mult, ALU.add).then_inc(s_qss, 1)
        elif part == 4:
            dve.wait_ge(s_qsq, 4 - t)
            dve.reciprocal(var, var)
            dve.drain()
            dve.tensor_tensor(hv(y), hv(y), bc(var, HD), ALU.mult)
            dve.tensor_tensor(hv(kdir[:, :]), hv(z_v[:, t, :]), bc(krs[:, H * t:H * t + H], HD), ALU.mult)
            dve.drain()
        elif part == 5:
            dve.tensor_tensor(y, y, lngb[:, :], ALU.mult)
            dve.tensor_tensor(kdir[:, :], kdir[:, :], lnbb[:, :], ALU.add)
            dve.drain()
            dve.tensor_tensor(y, y, kdir[:, :], ALU.add)
            dve.wait_ge(R["gmm"], 1)
            dve.drain()
            dve.tensor_tensor(y, y, psum[:, 6 + t, :], ALU.mult)
            dve.drain()

    def rwkv_vector(dve):
        split_low(dve, len(W_IN), 1)
        dve.wait_ge(R["vec"], 16 * 10)
        for tt in range(2 * NT):
            dve.tensor_tensor(ew[:, :], z_k[:, tt, :], kkb[:, :], ALU.mult)
            dve.drain()
            dve.tensor_tensor(ea[:, :], ew[:, :], ew[:, :], ALU.mult)
            dve.drain()
            dve.tensor_reduce(kq[:, H * tt:H * tt + H], hv(ea[:, :]), AX, ALU.add)
            dve.drain()
        dve.tensor_scalar(kq, kq, 1e-12, None, ALU.max).then_inc(s_qss, 1)
        dve.wait_ge(s_qsq, 2)
        dve.reciprocal(krs, krs).then_inc(R["krs"], 1)
        for part in (1, 3, 4):
            prep_vector(dve, 0, part)
        dve.wait_ge(R["iota"], 1)
        dve.tensor_tensor(ixor[:, :], ixor[:, :], ixp[:, :], ALU.bitwise_xor)
        dve.wait_ge(R["tri"], 1)
        dve.drain()
        for l in range(LV):
            dve.tensor_scalar(ixs[:, :], ixor[:, :], l, None, ALU.logical_shift_right)
            dve.drain()
            dve.tensor_scalar(maskF[:, l, :], ixs[:, :], 1, None, ALU.is_equal)
            dve.drain()
            dve.tensor_tensor(maskR[:, l, :], maskF[:, l, :], tri2[:, 1, 0, :], ALU.mult)
            dve.drain()
            dve.tensor_tensor(maskF[:, l, :], maskF[:, l, :], tri2[:, 0, 0, :], ALU.mult)
            dve.drain()
        dve.drain()
        for s in range(NS):
            d, tt = STEPS[s]
            mk, mt = (maskR, maskF) if d == 0 else (maskF, maskR)
            if s >= 2:
                dve.tensor_tensor(Mp[:, d, :, :], Mst[:, d, :, :],
                                  bc(facs[:, s % 2, 0:8:2], HD), ALU.mult).then_inc(R["mp"], 1)
            for h in range(H):
                dve.wait_ge(R["gram"], H * s + h + 1)
                if h == 0 and s > 0:
                    dve.wait_ge(R["m1"], 12 * s)
                    dve.wait_ge(R["EU"], s)
                n = 2 if is_x(s) else 1
                m = tri2[:, d, 0:n, :]
                pb = psum[:, 4 + h % 2, :].rearrange("p (s c n) -> p s c n", s=2, c=2)
                dve.tensor_tensor(AtE[:, h, 0:n, :], pb[:, 0, 0:n, :], m, ALU.mult)
                if s > 0 or h >= 2:
                    dve.wait_ge(R["xyh"], H * s + h - 1)
                dve.tensor_tensor(CD[:, h % 2, 0:n, :], pb[:, 1, 0:n, :], m, ALU.mult)
                dve.drain().then_inc(R["gev"], 1)
                if h % 4 == 3:
                    g = h // 4
                    hs = slice(4 * g, 4 * g + 4)
                    dve.wait_ge(R["Ap"], 2 * s + g + 1)
                    if s > 0 and g == 0:
                        dve.wait_ge(R["y"], 12 * s)
                        dve.wait_ge(R["U"], s)
                    dve.tensor_tensor(Tm[:, hs, :], psum[:, g, :].rearrange("p (h n) -> p h n", n=P),
                                      mb(mk[:, 0, :]), ALU.mult)
                    dve.tensor_tensor(Tt[:, hs, :], AtE[:, hs, 0, :], mb(mt[:, 0, :]), ALU.mult)
                    dve.drain()
                    dve.tensor_tensor(Tm[:, hs, :], mb(ident[:, :]), Tm[:, hs, :], ALU.subtract)
                    dve.tensor_tensor(Tt[:, hs, :], mb(ident[:, :]), Tt[:, hs, :], ALU.subtract)
                    dve.drain().then_inc(R["T0"], 1)
            def minus(T_, g, b):
                hs = slice(4 * g, 4 * g + 4)
                return dve.tensor_tensor(T_[:, hs, :], T_[:, hs, :],
                                         psum[:, b, :].rearrange("p (h n) -> p h n", n=P), ALU.subtract)

            for l in range(1, LV):
                dve.wait_ge(R["m1"], 12 * s + 2 * l - 1)
                dve.tensor_tensor(M1s[:, 0:4, :], psum[:, 4, :].rearrange("p (h n) -> p h n", n=P),
                                  mb(mk[:, l, :]), ALU.mult).then_inc(R["m1e"], 1)
                if l > 1:
                    minus(Tt, 1, 3).then_inc(R["upd"], 1)
                dve.wait_ge(R["m1"], 12 * s + 2 * l)
                dve.tensor_tensor(M1s[:, 4:8, :], psum[:, 5, :].rearrange("p (h n) -> p h n", n=P),
                                  mb(mk[:, l, :]), ALU.mult).then_inc(R["m1e"], 1)
                if s + 1 < NS:
                    prep_vector(dve, s + 1, l)
                else:
                    post_vector(dve, 1, l)
                    if l == 5:
                        dve.drain().then_inc(R["done"], 1)
                for g in range(2):
                    dve.wait_ge(R["y"], 12 * s + 2 * (l - 1) + g + 1)
                    if l < LV - 1:
                        minus(Tm, g, g).then_inc(R["tmu"], 1)
                    if g == 0 or l == LV - 1:
                        minus(Tt, g, 2 + g).then_inc(R["upd"], 1)
                dve.drain()
            if is_x(s):
                dve.wait_ge(R["EU"], s + 1)
                first = s < 6
                dst = yacc[:, tt, :] if first else Yps[:, :]
                dve.tensor_tensor(dst, Yps[:, :], psum[:, 5, :], ALU.add)
                if not first:
                    dve.drain()
                    dve.tensor_tensor(yacc[:, tt, :], yacc[:, tt, :], Yps[:, :], ALU.add)
                dve.drain().then_inc(R["yf"], 1)
            if s < NS - 2:
                dve.wait_ge(R["dM"], s + 1)
                src = psum[:, 4, 0:4 * HD].rearrange("p (c v) -> p c v", c=4)
                fl = bc(facs[:, s % 2, 1:8:2], HD)
                if s < 2:
                    dve.tensor_tensor(Mst[:, d, :, :], src, fl, ALU.mult)
                else:
                    dve.tensor_tensor(Mst[:, d, :, :], Mp[:, d, :, :], src, ALU.add)
                    dve.drain()
                    dve.tensor_tensor(Mst[:, d, :, :], Mst[:, d, :, :], fl, ALU.mult)
                dve.drain().then_inc(R["Mu"], 1)
        for part in range(1, 6):
            post_vector(dve, 0, part)
        dve.drain().then_inc(R["done"], 1)

    def prep_scalar(act, s, part):
        if part == 1:
            act.wait_ge(R["e1"], s + 1)
            act.activation(ew[:, :], ew[:, :], ACT.Sigmoid)
            act.activation(ea[:, :], ea[:, :], ACT.Sigmoid)
            act.drain().then_inc(R["a1"], 1)
        else:
            act.wait_ge(R["e3"], s + 1)
            act.wait_ge(R["p2"], s + 1)
            if s > 0:
                act.wait_ge(R["ks"], s)
                act.wait_ge(R["tr"], tr_before(s))
            act.activation(Ktk[:, :], Ktk[:, :], ACT.Exp, scale=-C0)
            act.activation(epos[:, :], psum[:, 6, :], ACT.Exp, scale=C0)
            if is_x(s):
                act.activation(Rtk[:, :], psum[:, 6, :], ACT.Exp, scale=-C0)
            if s >= 2 and s - 2 < NS - 2:
                act.wait_ge(R["Mu"], s - 1)
            act.activation(facs[:, s % 2, :], psum[:, 7, 0:8], ACT.Exp, scale=-C0)
            act.drain().then_inc(R["a2"], 1)

    def post_scalar(act, t):
        act.wait_ge(s_qss, 4 - t)
        var = gst[:, 16 + H * t:16 + H * t + H]
        act.activation(var, var, ACT.Sqrt).then_inc(s_qsq, 1)

    def rwkv_scalar(act):
        split_high(act, len(W_IN), 1, panel_arrivals(len(W_IN)))
        act.wait_ge(s_qss, 2)
        act.activation(krs, kq, ACT.Sqrt).then_inc(s_qsq, 1)
        prep_scalar(act, 0, 1)
        prep_scalar(act, 0, 2)
        for s in range(NS):
            d, tt = STEPS[s]
            names = [((0, 0), 0), (KbT[:, :, :], 2), (BbT[:, :, :], 3)]
            if is_x(s):
                names.append(((1, 1), 1))
            if s > 0:
                act.wait_ge(R["xy"], s)
            for j, (dst, b) in enumerate(names):
                act.wait_ge(R["tr"], tr_before(s) + j + 1)
                src = psum[:, b, :].rearrange("p (c n) -> p c n", c=4)
                if j in (0, 3):
                    q = j // 3
                    act.activation(KRT[0][0:64, :, q, :], src[0:64], ACT.Copy)
                    act.activation(KRT[1][64:128, :, q, :], src[64:128], ACT.Copy)
                    act.drain().then_inc(R["trE"], 1)
                else:
                    act.activation(dst, src, ACT.Copy).then_inc(R["trE"], 1)
            act.wait_ge(R["xy"], s + 1)
            if s > 0:
                act.wait_ge(R["U"], s)
            act.activation(Xs[:, :], psum[:, 2, :], ACT.Copy)
            if is_x(s):
                if s > 4:
                    act.wait_ge(R["yf"], s - 4)
                act.activation(Yps[:, :], psum[:, 3, :], ACT.Copy)
            act.drain().then_inc(R["xyE"], 1)
            if s + 1 < NS:
                prep_scalar(act, s + 1, 1)
                prep_scalar(act, s + 1, 2)
            else:
                post_scalar(act, 1)
            act.wait_ge(R["U"], s + 1)
            if s > 0:
                act.wait_ge(R["EU"], s)
                act.wait_ge(R["dM"], min(s, NS - 2))
            act.activation(nU[:, :], psum[:, 4, :], ACT.Copy, scale=-1.0).then_inc(R["nU"], 1)
        post_scalar(act, 0)

    def prep_tensor(pe, s, part):
        d, tt = STEPS[s]
        ts = slice(P * tt, P * (tt + 1))
        if part == 1:
            if s > 0:
                pe.wait_ge(R["a2"], s)
            pe.matmul(psum[:, 6, :], z_lwT[:, ts], wlb[:, d, :], start=True, stop=True)
            pe.matmul(psum[:, 7, :], z_laT[:, ts], alb[:, d, :], start=True, stop=True).then_inc(R["p1"], 1)
        else:
            pe.wait_ge(R["a1"], s + 1)
            pe.matmul(psum[:, 6, :], cumT[:, d, :], ew[:, :], start=True, stop=True)
            for c in range(4):
                i = pe.matmul(psum[:, 7, 2 * c:2 * c + 2], ew[:, P * c:P * (c + 1)], colm[:, d, :],
                              start=True, stop=True)
            i.then_inc(R["p2"], 1)

    def transposes_tensor(pe, s):
        pe.wait_ge(R["ks"], s + 1)
        names = [(Ktk[:, :], 0), (Kb[:, s % 2, :], 2), (Bb[:, s % 2, :], 3)]
        if is_x(s):
            names.append((Rtk[:, :], 1))
        for src, b in names:
            for c in range(4):
                i = pe.transpose(psum[:, b, P * c:P * (c + 1)], src[:, P * c:P * (c + 1)], ident[:, :])
            i.then_inc(R["tr"], 1)

    def rwkv_tensor(pe):
        pe.wait_ge(R["vec"], 16 * 10)
        pe.wait_ge(R["tri"], 1)
        pe.wait_ge(s_const, 4)
        prep_tensor(pe, 0, 1)
        prep_tensor(pe, 0, 2)
        transposes_tensor(pe, 0)
        for s in range(NS):
            d, tt = STEPS[s]
            if s > 0:
                pe.wait_ge(R["nU"], s)
                pe.wait_ge(R["Mu"], min(s, NS - 2))
                if s > 4:
                    pe.wait_ge(R["yf"], s - 4)
            pe.wait_ge(R["trE"], tr_before(s + 1))
            if s >= 2:
                pe.wait_ge(R["mp"], s - 1)
            n = 2 if is_x(s) else 1

            def xy(i_h):
                h = HO[i_h]
                c = h // 2
                vs = slice(HD * h, HD * (h + 1))
                pe.wait_ge(R["gev"], H * s + i_h + 1)
                for q in range(n):
                    o = psum[:, 2 + q, vs]
                    if s >= 2:
                        pe.matmul(o, KRT[h % 2][:, c, q, :], Mp[:, d, c, :], start=True, stop=False)
                    i = pe.matmul(o, CD[:, i_h % 2, q, :], z_v[:, tt, vs], start=(s < 2), stop=True)
                i.then_inc(R["xyh"], 1)

            for i_h, h in enumerate(HO):
                c = h // 2
                if i_h >= 2:
                    pe.wait_ge(R["gev"], H * s + i_h - 1)
                b = psum[:, 4 + i_h % 2, :].rearrange("p (s n) -> p s n", s=2)
                rhs = KRT[h % 2][:, c, 0:n, :].rearrange("p c n -> p (c n)")
                pe.matmul(b[:, 0, 0:P * n], BbT[:, c, :], rhs, start=True, stop=True)
                pe.matmul(b[:, 1, 0:P * n], KbT[:, c, :], rhs, start=True, stop=True).then_inc(R["gram"], 1)
                i = pe.matmul(psum[:, i_h // 4, P * (i_h % 4):P * (i_h % 4 + 1)], KRT[h % 2][:, c, 0, :], BbT[:, c, :],
                              start=True, stop=True)
                if i_h % 4 == 3:
                    i.then_inc(R["Ap"], 1)
                if i_h >= 1:
                    xy(i_h - 1)
            xy(H - 1)
            pe.drain().then_inc(R["xy"], 1)
            if s + 1 < NS:
                prep_tensor(pe, s + 1, 1)
            else:
                pe.wait_ge(R["a2"], NS)
                pe.wait_ge(R["vec2"], 16 * 4)
                for t in range(NT):
                    i = pe.matmul(psum[:, 6 + t, :], z_lgT[:, P * t:P * (t + 1)], glb[:, :], start=True, stop=True)
                i.then_inc(R["gmm"], 1)
            for l in range(1, LV):
                for g in range(2):
                    i0 = 12 * s + 2 * (l - 1) + g
                    if l == 1:
                        pe.wait_ge(R["T0"], 2 * s + g + 1)
                    else:
                        pe.wait_ge(R["tmu"], 2 * (LV - 2) * s + 2 * (l - 2) + g + 1)
                    for h in range(4 * g, 4 * g + 4):
                        i = pe.matmul(psum[:, 4 + g, P * (h % 4):P * (h % 4 + 1)], AtE[:, h, 0, :], Tm[:, h, :],
                                      start=True, stop=True)
                    i.then_inc(R["m1"], 1)
                for g in range(2):
                    i0 = 12 * s + 2 * (l - 1) + g
                    pe.wait_ge(R["m1e"], i0 + 1)
                    if l > 1:
                        pe.wait_ge(R["upd"], i0 - 1)
                    else:
                        pe.wait_ge(R["xyE"], s + 1)
                    for h in range(4 * g, 4 * g + 4):
                        cs = slice(P * (h % 4), P * (h % 4 + 1))
                        if l < LV - 1:
                            pe.matmul(psum[:, g, cs], Tt[:, h, :], M1s[:, h, :], start=True, stop=True)
                        i = pe.matmul(psum[:, 2 + g, cs], M1s[:, h, :], Tt[:, h, :], start=True, stop=True)
                    i.then_inc(R["y"], 1)
                if s + 1 < NS and l == 2:
                    prep_tensor(pe, s + 1, 2)
            pe.wait_ge(R["upd"], 12 * (s + 1))
            for i_h, h in enumerate(HO):
                vs = slice(HD * h, HD * (h + 1))
                i = pe.matmul(psum[:, 4, vs], Tt[:, i_h, :], Xs[:, vs], start=True, stop=True)
            i.then_inc(R["U"], 1)
            if s + 1 < NS:
                transposes_tensor(pe, s + 1)
            pe.wait_ge(R["nU"], s + 1)
            if is_x(s):
                for i_h, h in enumerate(HO):
                    vs = slice(HD * h, HD * (h + 1))
                    pe.matmul(psum[:, 5, vs], AtE[:, i_h, 1, :], nU[:, vs], start=True, stop=True)
            pe.drain().then_inc(R["EU"], 1)
            if s < NS - 2:
                for h in HO:
                    hs, c = slice(64 * (h % 2), 64 * (h % 2) + 64), h // 2
                    vs = slice(HD * h, HD * (h + 1))
                    o = psum[hs, 4, HD * c:HD * (c + 1)]
                    pe.matmul(o, Kb[:, s % 2, vs], z_v[:, tt, vs], start=True, stop=False)
                    i = pe.matmul(o, Bb[:, s % 2, vs], nU[:, vs], start=False, stop=True)
                i.then_inc(R["dM"], 1)

    class Seq:

        def __init__(self, c, *terms):
            self.c, self.terms = c, terms

        def v(self, off=0, mul=1):
            x = (self.c + off) * mul
            for reg, k in self.terms:
                x = reg * (k * mul) + x
            return x

        def plus(self, off):
            return Seq(self.c + off, *self.terms)

        def par(self):
            return self.c % 2

        def arrivals(self):
            x = (self.c // 2) * 16 + 16
            for reg, k in self.terms:
                x = reg * (k * 8) + x
            return x

    def sp_panel(sp, n, src):
        sp.wait_ge(s_wl, n.v(-1))
        size = src.shape[-1] * src.shape[-2]
        dst = RAW[n.par()][:, 0:size].rearrange("p (k n) -> p k n", n=src.shape[-1])
        sp.dma_start(dst, src).then_inc(s_raw[n.par()], 16)

    def act_panel(act, n, elems=4096):
        act.wait_ge(s_raw[n.par()], n.arrivals())
        act.wait_ge(s_wdone, n.v(-1))
        act.activation(WH[n.par()][:, 0:elems], RAW[n.par()][:, 0:elems], ACT.Copy).then_inc(s_wh, 1)

    def dve_panel(dve, n, elems=4096):
        dve.wait_ge(s_wh, n.v(1))
        dve.tensor_tensor(WL[n.par()][:, 0:elems], RAW[n.par()][:, 0:elems],
                          WH[n.par()][:, 0:elems].bitcast(F32), ALU.subtract).then_inc(s_wl, 1)

    def pe_panel(pe, n, k):
        pe.wait_ge(s_wl, n.v(1))
        return tuple(w[n.par()][:, :].rearrange("p (k n) -> p k n", k=k) for w in (WH, WL))

    NP0 = len(W_IN)
    act2H = Region(act_off, 8 * KB).take("act2_high", [P, KT, T], F32R)
    act2L = Region(act_off + 16 * KB, 8 * KB).take("act2_low", [P, KT, T], F32R)
    gap1 = act_off + 8 * KB
    gap2 = act_off + 24 * KB
    me = Region(free_off, 25 * KB)
    pg = me.take("pg", [P, KT, T])
    msum = me.take("msum", [P, KT, T])
    mg2 = me.take("mg2", [P, D])
    sh2 = me.take("sh2", [P, D])
    me2 = Region(after_front, 36 * KB)
    yTH = me2.take("yT_high", [P, 2, H // 2, T], F32R)
    yTL = me2.take("yT_low", [P, 2, H // 2, T], F32R)
    gt = me2.take("gates", [P, 2, KT, T])
    sc2 = me2.take("sc2", [P, D])
    n2g = Region(free_off, 4 * KB).take("n2g", [P, D])
    mg5 = Region(free_off + 4 * KB, 4 * KB).take("mg5", [P, D])
    htok = Region(free_off + 8 * KB, 8 * KB).take("htok", [P, NT, D])
    mo = Region(after_front, FREE - (after_front - free_off))
    accm = mo.take("accm", [P, NT, D])
    sg = mo.take("sg", [P, 4, T])
    hidf = mo.take("hidf", [P, 4, T])
    hidH = mo.take("hid_high", [P, 4, T], F32R)
    hidL = mo.take("hid_low", [P, 4, T], F32R)
    rwf = mo.take("rwf", [P, KT, E])
    rwH = mo.take("rw_high", [P, KT, E], F32R)
    rwL = mo.take("rw_low", [P, KT, E], F32R)
    rbias = mo.take("rbias", [P, E])
    junk2 = Region(gap1, 4 * KB).take("junk2", [P, D])
    rt_off = gap1 + 4 * KB
    rtr = Region(rt_off, 4 * KB)
    NG = 4
    GE = E // NG
    sco = rtr.take("sco", [P, NT, E])
    sel = rtr.take("sel", [P, NT, E])
    pair = rtr.take("pair", [P, NT * NG, 6])
    gs4 = rtr.take("gs4", [P, NT, NG])
    gmask = rtr.take("gmask", [P, NT, NG])
    rank4 = rtr.take("rank4", [P, NT, NG])
    rank16 = rtr.take("rank16", [P, NT, E])
    tmpr = rtr.take("tmpr", [P, NT, E])
    oh = rtr.take("oh", [P, 2, NT, E])
    mx1 = rtr.take("mx1", [P, NT])
    gate = rtr.take("gate", [P, NT, E])
    n2st = stat[:, 64:80]

    M = {name: sem("mg_" + name) for name in (
        "x_in", "gt_in", "vec_in", "yT", "yH", "yL", "pa", "pb", "ga", "gb", "mH", "mL", "wo", "x1", "v2_in",
        "rw_in", "rH", "rL", "logit", "sig", 
        "rank", "g", "silu", "hid", "hH2", "hL2", "acc", "x2")}

    def merge_sync(sp):
        load_panel(sp, NP0, 1, a["proj_a"][0].rearrange("(k p) n -> p k n", p=P))
        load_panel(sp, NP0 + 1, 0, a["proj_b"][0].rearrange("(k p) n -> p k n", p=P))
        for c in range(2):
            load_panel(sp, NP0 + 2 + c, (NP0 + c) % 2, full_panel(a["w_out"][0], PW * c))

    def merge_pool(pool):
        pool.wait_ge(R["done"], 2)
        pool.dma_start(xres[:, :, :], a["x"][0].rearrange("(t p) d -> p t d", p=P)).then_inc(M["x_in"], 16)
        for c in range(2):
            pool.dma_start(gt[:, c, :, :], gates_d[KT * c:KT * (c + 1)].rearrange("c p t -> p c t")
                           ).then_inc(M["gt_in"], 16)
        rows = mrow.rearrange("(v h) n -> v (h n)", h=2)
        for dst, v in ((mg2, 0), (sh2, 1), (sc2, 2)):
            pool.dma_start(dst[:, :], rows[v].partition_broadcast(P)).then_inc(M["vec_in"], 16)
        pool.wait_ge(M["yT"], 4)
        pool.iota(rank4[:, :, :], pattern=[[0, NT], [-1, NG]], base=NG, channel_multiplier=0,
                  allow_small_or_imprecise_dtypes=True)
        pool.iota(rank16[:, :, :], pattern=[[0, NT], [-1, E]], base=E, channel_multiplier=0,
                  allow_small_or_imprecise_dtypes=True).then_inc(M["rank"], 1)
        pool.wait_ge(M["mH"], 4)
        pool.wait_ge(M["mL"], 4)
        pool.dma_start(n2g[:, :], a["norm2_g"][0].partition_broadcast(P)).then_inc(M["v2_in"], 16)
        pool.dma_start(mg5[:, :], rows[3].partition_broadcast(P)).then_inc(M["v2_in"], 16)
        pool.dma_start(rwf[:, :, :], a["router_w"].rearrange("(k p) e -> p k e", p=P)).then_inc(M["rw_in"], 16)
        pool.dma_start(rbias[:, :], a["router_bias"].partition_broadcast(P)).then_inc(M["rw_in"], 16)

    def bank3(b, n=P):
        return psum[:, b, :].rearrange("p (c n) -> p c n", n=n)

    YJ = (2, 3, 1, 0)

    def merge_scalar(act):
        act.wait_ge(R["done"], 2)
        for i, j in enumerate(YJ):
            act.wait_ge(M["yT"], i + 1)
            act.activation(yTH[:, j // 2, :, P * (j % 2):P * (j % 2 + 1)], bank3(j), ACT.Copy
                           ).then_inc(M["yH"], 1)
        act_panel(act, Seq(NP0 + 1))
        act_panel(act, Seq(NP0 + 2))
        for b in range(4):
            act.wait_ge(M["gb"], b + 1)
            act.activation(act2H[:, 2 * b:2 * b + 2, :], msum[:, 2 * b:2 * b + 2, :], ACT.Copy
                           ).then_inc(M["mH"], 1)
        act_panel(act, Seq(NP0 + 3))
        act_panel(act, Seq(NP0 + 4))

    def merge_vector(dve):
        for i, j in enumerate(YJ):
            dve.wait_ge(M["yH"], i + 1)
            ts = slice(P * (j % 2), P * (j % 2 + 1))
            dve.tensor_tensor(yTL[:, j // 2, :, ts], bank3(j), yTH[:, j // 2, :, ts].bitcast(F32),
                              ALU.subtract).then_inc(M["yL"], 1)
        dve_panel(dve, Seq(NP0 + 1))
        dve.wait_ge(M["gt_in"], 32)
        for b in range(4):
            dve.wait_ge(M["pa"], b + 1)
            dve.tensor_tensor(pg[:, 2 * b:2 * b + 2, :], bank3(4 + b, T), gt[:, 0, 2 * b:2 * b + 2, :],
                              ALU.mult).then_inc(M["ga"], 1)
        dve_panel(dve, Seq(NP0 + 2))
        for b in range(5):
            if b < 4:
                dve.wait_ge(M["pb"], b + 1)
                cs = slice(2 * b, 2 * b + 2)
                dve.tensor_tensor(msum[:, cs, :], bank3(b, T), gt[:, 1, cs, :], ALU.mult)
                dve.drain()
                dve.tensor_tensor(msum[:, cs, :], msum[:, cs, :], pg[:, cs, :], ALU.add).then_inc(M["gb"], 1)
            if b >= 1:
                cs = slice(2 * b - 2, 2 * b)
                dve.wait_ge(M["mH"], b)
                dve.tensor_tensor(act2L[:, cs, :], msum[:, cs, :], act2H[:, cs, :].bitcast(F32), ALU.subtract
                                  ).then_inc(M["mL"], 1)
        dve_panel(dve, Seq(NP0 + 3))
        dve.wait_ge(M["x_in"], 16)
        dve.wait_ge(M["vec_in"], 48)
        for c in range(2):
            cs = slice(PW * c, PW * (c + 1))
            if c == 1:
                dve_panel(dve, Seq(NP0 + 4))
            for t in range(NT):
                dve.wait_ge(M["wo"], NT * c + t + 1)
                b = psum[:, 4 + 2 * c + t, :]
                dve.tensor_tensor(junk2[:, cs], b, mg2[:, cs], ALU.mult)
                dve.drain()
                dve.tensor_tensor(xres[:, t, cs], xres[:, t, cs], junk2[:, cs], ALU.add)
                dve.drain().then_inc(M["x1"], 1)

    def merge_tensor(pe):
        for j in YJ:
            if j < 2:
                pe.wait_ge(R["done"], 2 - j)
            src = yacc[:, j, :] if j < 2 else yb[:, j - 2, :]
            for c in range(4):
                i = pe.matmul(psum[:, j, P * c:P * (c + 1)], src[:, P * c:P * (c + 1)],
                              (ident if j < 2 else flip)[:, :], start=True, stop=True)
            i.then_inc(M["yT"], 1)
        for side in range(2):
            wh, wl = pe_panel(pe, Seq(NP0 + side), 4)
            if side == 0:
                pe.wait_ge(M["yL"], 4)
            for c in range(KT):
                b = (4 if side == 0 else 0) + c // 2
                for k in range(4):
                    i = three_pass(pe, psum[:, b, T * (c % 2):T * (c % 2 + 1)], wh[:, k, P * c:P * (c + 1)],
                                   wl[:, k, P * c:P * (c + 1)], yTH[:, side, k, :], yTL[:, side, k, :],
                                   k == 0, k == 3)
                if c % 2 == 1:
                    i.then_inc(M["pa" if side == 0 else "pb"], 1)
            pe.drain().then_inc(s_wdone, 1)
        pe.wait_ge(M["mL"], 4)
        pe.wait_ge(M["ga"], 4)
        for c in range(2):
            wh, wl = pe_panel(pe, Seq(NP0 + 2 + c), KT)
            for t in range(NT):
                i = token_major(pe, psum[:, 4 + 2 * c + t, :], act2H, act2L, wh, wl, t, KT)
                i.then_inc(M["wo"], 1)
            pe.drain().then_inc(s_wdone, 1)

    def token_major(pe, o, xH, xL, wh, wl, t, kt, cols=slice(None), start=True, stop=True):
        ts = slice(P * t, P * (t + 1))
        for k in range(kt):
            i = three_pass(pe, o, xH[:, k, ts], xL[:, k, ts], wh[:, k, cols], wl[:, k, cols],
                           start and k == 0, stop and k == kt - 1)
        return i

    def feature_major(pe, o, xH, xL, wh, wl, c, kt):
        cs = slice(P * c, P * (c + 1))
        for k in range(kt):
            i = three_pass(pe, o, wh[:, k, cs], wl[:, k, cs], xH[:, k, :], xL[:, k, :], k == 0, k == kt - 1)
        return i

    NM = NP0 + 4

    def route_scalar(act):
        act.wait_ge(M["x1"], 2 * NT)
        for t in range(NT):
            act.activation(htok[:, t, :], xres[:, t, :], ACT.Square, accum_out=n2st[:, t:t + 1])
        act.drain().then_inc(s_ssq, 1)
        act.wait_ge(s_var, 2)
        act.activation(n2st[:, 4:6], n2st[:, 2:4], ACT.Sqrt).then_inc(s_sqrt, 1)
        act.wait_ge(M["rw_in"], 32)
        act.activation(rwH[:, :, :], rwf[:, :, :], ACT.Copy).then_inc(M["rH"], 1)
        for j in range(4):
            act.wait_ge(s_hT, NU_T + j + 1)
            act.activation(hdst(act2H, j), bank3(j), ACT.Copy).then_inc(s_hH, 1)
        act.wait_ge(M["logit"], 1)
        act.activation(sco[:, :, :], psum[:, 4, 0:NT * E].rearrange("p (t e) -> p t e", t=NT), ACT.Sigmoid
                       ).then_inc(M["sig"], 1)

    def hdst(x, j):
        return x[:, 4 * (j % 2):4 * (j % 2) + 4, P * (j // 2):P * (j // 2 + 1)]

    def route_vector(dve):
        dve.wait_ge(s_ssq, 2)
        dve.tensor_scalar(n2st[:, 2:4], n2st[:, 0:2], 1.0 / D, EPS, ALU.mult, ALU.add).then_inc(s_var, 1)
        dve.wait_ge(M["v2_in"], 32)
        dve.scalar_tensor_tensor(out=sc2[:, :], in0=sc2[:, :], scalar=1.0, in1=n2g[:, :], op0=ALU.add,
                                 op1=ALU.mult)
        dve.wait_ge(s_sqrt, 2)
        dve.reciprocal(n2st[:, 6:8], n2st[:, 4:6])
        dve.drain()
        for t in range(NT):
            dve.scalar_tensor_tensor(out=htok[:, t, :], in0=xres[:, t, :], scalar=n2st[:, 6 + t:7 + t],
                                     in1=sc2[:, :], op0=ALU.mult, op1=ALU.mult)
            dve.drain()
            dve.tensor_tensor(htok[:, t, :], htok[:, t, :], sh2[:, :], ALU.add).then_inc(s_h, 1)
        dve.wait_ge(M["rH"], 1)
        dve.tensor_tensor(rwL[:, :, :], rwf[:, :, :], rwH[:, :, :].bitcast(F32), ALU.subtract
                          ).then_inc(M["rL"], 1)
        for j in range(4):
            dve.wait_ge(s_hH, NU_T + j + 1)
            dve.tensor_tensor(hdst(act2L, j), bank3(j), hdst(act2H, j).bitcast(F32), ALU.subtract
                              ).then_inc(s_hL, 1)
        dve.memset(accm[:, :, :], 0.0).then_inc(M["acc"], 1)
        dve.wait_ge(M["sig"], 1)
        dve.wait_ge(M["rank"], 1)
        step = lambda i: dve.drain()
        step(dve.tensor_tensor(sel[:, :, :], sco[:, :, :], rbias[:, :].unsqueeze(1).to_broadcast([P, NT, E]),
                               ALU.add))
        s4 = sel[:, :, :].rearrange("p t (g e) -> p (t g) e", e=GE)
        dve.tensor_tensor(pair[:, :, 0:3], s4[:, :, 0:3], s4[:, :, 1:4], ALU.add)
        dve.tensor_tensor(pair[:, :, 3:5], s4[:, :, 0:2], s4[:, :, 2:4], ALU.add)
        step(dve.tensor_tensor(pair[:, :, 5:6], s4[:, :, 0:1], s4[:, :, 3:4], ALU.add))
        step(dve.tensor_reduce(gs4[:, :, :].rearrange("p t g -> p (t g)"), pair[:, :, :], AX, ALU.max))

        def first_max(mask, vals, ranks, n):
            tmp = tmpr[:, :, 0:n]
            step(dve.tensor_reduce(mx1[:, :], vals, AX, ALU.max))
            step(dve.tensor_tensor(tmp, vals, bc(mx1[:, :], n), ALU.is_equal))
            step(dve.tensor_tensor(tmp, tmp, ranks, ALU.mult))
            step(dve.tensor_reduce(mx1[:, :], tmp, AX, ALU.max))
            step(dve.tensor_tensor(mask, ranks, bc(mx1[:, :], n), ALU.is_equal))

        first_max(gmask[:, :, :], gs4[:, :, :], rank4[:, :, :], NG)
        g16 = gmask[:, :, :].rearrange("p t g -> p (t g)")
        s16 = s4
        step(dve.tensor_tensor(s16, s16, bc(g16, GE), ALU.mult))
        step(dve.tensor_scalar(g16, g16, -NEG, NEG, ALU.mult, ALU.add))
        step(dve.tensor_tensor(s16, s16, bc(g16, GE), ALU.add))
        first_max(oh[:, 0, :, :], sel[:, :, :], rank16[:, :, :], E)
        step(dve.scalar_tensor_tensor(out=sel[:, :, :].rearrange("p t e -> p (t e)"),
                                      in0=oh[:, 0, :, :].rearrange("p t e -> p (t e)"), scalar=4 * NEG,
                                      in1=sel[:, :, :].rearrange("p t e -> p (t e)"),
                                      op0=ALU.mult, op1=ALU.add))
        first_max(oh[:, 1, :, :], sel[:, :, :], rank16[:, :, :], E)
        step(dve.tensor_tensor(gate[:, :, :], oh[:, 0, :, :], oh[:, 1, :, :], ALU.add))
        step(dve.tensor_tensor(gate[:, :, :], gate[:, :, :], sco[:, :, :], ALU.mult))
        step(dve.tensor_reduce(mx1[:, :], gate[:, :, :], AX, ALU.add))
        step(dve.reciprocal(mx1[:, :], mx1[:, :]))
        step(dve.tensor_tensor(gate[:, :, :], gate[:, :, :], bc(mx1[:, :], E), ALU.mult))

    def route_tensor(pe):
        for j in range(4):
            t, half = j // 2, j % 2
            pe.wait_ge(s_h, NU_T // 2 + t + 1)
            for c in range(4):
                i = pe.transpose(psum[:, j, P * c:P * (c + 1)],
                                 htok[:, t, P * (4 * half + c):P * (4 * half + c + 1)], ident[:, :])
            i.then_inc(s_hT, 1)
        pe.wait_ge(s_hL, NU_T + 4)
        pe.wait_ge(M["rL"], 1)
        for t in range(NT):
            i = token_major(pe, psum[:, 4, E * t:E * (t + 1)], act2H, act2L, rwH, rwL, t, KT)
        i.then_inc(M["logit"], 1)


    PLW = 256
    WINS = (2, 4, 8, 16)
    AW = D - PLW
    H2 = AW // HD
    DIL = (1, 4, 16)
    STEPS_BACK = 128
    ZW = PLW + 3 * AW
    RH = HD // 4 // 2
    c2 = Region(free_off + 51 * KB + 512, FREE - 51 * KB - 512)
    band = c2.take("band", [P, 4, NT, T])
    cmask = c2.take("cmask", [P, 3, 3 * P])
    cs_t = c2.take("cs_t", [P, 2, NT, RH])
    invf = c2.take("invf", [P, RH])
    posi = c2.take("posi", [P, NT], I32)
    posf = c2.take("posf", [P, NT])
    ang = c2.take("ang", [P, NT, RH])
    kint = c2.take("kint", [P, NT, RH], I32)
    kflt = c2.take("kflt", [P, NT, RH])
    g2r = Region(gap2, 8 * KB)
    cnt = g2r.take("cnt", [P, 4, T])
    dint = g2r.take("dint", [P, 3 * P], I32)
    dand = g2r.take("dand", [P, 3 * P], I32)

    C = {name: sem("c2_" + name) for name in ("vec", "done", "sin", "pos_in", "ang")}

    def const2_pool(pool):
        pool.wait_ge(M["logit"], 1)
        pool.wait_ge(s_hL, NU_T + 4)
        pool.iota(cnt[:, :, :], pattern=[[0, 4], [1, T]], base=1, channel_multiplier=0,
                  allow_small_or_imprecise_dtypes=True)
        pool.iota(dint[:, 0:P], pattern=[[-1, P]], base=2 * T, channel_multiplier=1)
        pool.iota(dint[:, P:3 * P], pattern=[[-1, 2 * P]], base=2 * T + P, channel_multiplier=1)
        for i in range(RH):
            pool.memset(invf[:, i:i + 1], float(500000.0 ** (-2.0 * i / (2 * RH))))
        pool.drain().then_inc(R["iota"], 1)
        for t in range(NT):
            pool.dma_start(posi[:, t:t + 1], a["positions_2"][0, P * t:P * (t + 1)].unsqueeze(1)
                           ).then_inc(C["pos_in"], 16)
        pool.wait_ge(C["vec"], 1)
        for g, w in enumerate(WINS):
            for st in range(NT):
                b = band[:, g, st, :]
                pool.tensor_copy(b, cnt[:, g, :])
                pool.drain()
                pool.affine_select(out=b, in_=b, compare_op=ALU.is_ge, fill=0.0, base=-P * st,
                                   pattern=[[1, T]], channel_multiplier=-1)
                pool.drain()
                pool.affine_select(out=b, in_=b, compare_op=ALU.is_ge, fill=0.0, base=P * st + w - 1,
                                   pattern=[[-1, T]], channel_multiplier=1)
                pool.drain()
                pool.tensor_tensor(b[:, P * st:P * (st + 1)], b[:, P * st:P * (st + 1)], ident[:, :],
                                   ALU.subtract)
        for g in range(3):
            for t, k in ((0, slice(0, P)), (1, slice(P, 3 * P))):
                m = cmask[:, g, k]
                n = P * (t + 1)
                pool.affine_select(out=m, in_=m, compare_op=ALU.is_ge, fill=NEG, base=P * t,
                                   pattern=[[-1, n]], channel_multiplier=1)
                pool.drain()
                pool.affine_select(out=m, in_=m, compare_op=ALU.is_ge, fill=NEG,
                                   base=STEPS_BACK * DIL[g] - P * t, pattern=[[1, n]], channel_multiplier=-1)
                pool.drain()
        pool.drain().then_inc(C["done"], 1)

    def const2_vector(dve):
        dve.wait_ge(R["iota"], 2)
        for g, w in enumerate(WINS):
            dve.tensor_scalar(cnt[:, g, :], cnt[:, g, :], float(w), None, ALU.min)
        dve.drain()
        dve.reciprocal(cnt[:, :, :], cnt[:, :, :])
        for g in range(3):
            dve.drain()
            dve.tensor_scalar(dand[:, :], dint[:, :], DIL[g] - 1, None, ALU.bitwise_and)
            dve.drain()
            dve.tensor_scalar(cmask[:, g, :], dand[:, :], 0, None, ALU.is_equal)
            dve.drain()
            dve.tensor_scalar(cmask[:, g, :], cmask[:, g, :], -NEG, NEG, ALU.mult, ALU.add)
        dve.drain().then_inc(C["vec"], 1)
        dve.wait_ge(C["pos_in"], 32)
        dve.tensor_copy(posf[:, :], posi[:, :])
        dve.drain()
        for t in range(NT):
            dve.tensor_scalar(ang[:, t, :], invf[:, :], posf[:, t:t + 1], None, ALU.mult)
        dve.drain()
        dve.tensor_scalar(kint[:, :, :], ang[:, :, :], 0.15915494309189535, None, ALU.mult)
        dve.drain()
        dve.tensor_copy(kflt[:, :, :], kint[:, :, :])
        dve.drain()
        af = ang[:, :, :].rearrange("p t r -> p (t r)")
        kf = kflt[:, :, :].rearrange("p t r -> p (t r)")
        for part in (6.28125, 0.0019350051879882812, 3.019915981956753e-07):
            dve.scalar_tensor_tensor(out=af, in0=kf, scalar=-part, in1=af, op0=ALU.mult, op1=ALU.add)
            dve.drain()
        dve.tensor_scalar(af, af, 3.1415925, -3.1415925, ALU.min, ALU.max)
        dve.drain().then_inc(C["ang"], 1)
        dve.wait_ge(C["sin"], 1)
        dve.tensor_tensor(cs_t[:, 0, :, :], cs_t[:, 0, :, :], cs_t[:, 0, :, :], ALU.mult)
        dve.drain()
        dve.tensor_scalar(cs_t[:, 0, :, :], cs_t[:, 0, :, :], -2.0, 1.0, ALU.mult, ALU.add)

    def const2_scalar(act):
        act.wait_ge(C["ang"], 1)
        act.activation(cs_t[:, 0, :, :], ang[:, :, :], ACT.Sin, scale=0.5)
        act.activation(cs_t[:, 1, :, :], ang[:, :, :], ACT.Sin)
        act.drain().then_inc(C["sin"], 1)

    class Expert:

        def __init__(self, c, i=None):
            self.c, self.i = c, i

        def count(self, mul, off):
            return Seq(self.c * mul + off, *([(self.i, 2 * mul)] if self.i is not None else []))

        def index(self):
            return self.c if self.i is None else self.i * 2 + self.c

    def expert_loop(eng, body):
        with eng.Fori(0, (E - 2) // 2) as i:
            for c in range(2):
                body(eng, Expert(c, i), False)
        body(eng, Expert(E - 2), False)
        body(eng, Expert(E - 1), True)

    def moe_src(name, e, kt):
        w = a[name][0]
        idx = e.index()
        w = w[idx] if isinstance(idx, int) else w[bass.ds(idx, 1)].rearrange("a k n -> (a k) n")
        return w.rearrange("(k p) n -> p k n", p=P)

    def moe_sync_body(sp, e, last):
        sp_panel(sp, e.count(3, NM + 1), moe_src("moe_w3", e, KT))
        if not last:
            sp_panel(sp, e.count(3, NM + 2), moe_src("moe_w1", Expert(e.c + 1, e.i), KT))
        sp_panel(sp, e.count(3, NM + (2 if last else 3)), moe_src("moe_w2", e, 4))

    def moe_sync(sp):
        sp_panel(sp, Seq(NM), moe_src("moe_w1", Expert(0), KT))
        expert_loop(sp, moe_sync_body)

    def moe_scalar_body(act, e, last):
        act.wait_ge(M["g"], e.count(1, 1).v())
        act.activation(sg[:, :, :], psum[:, 0:2, :].rearrange("p b (c n) -> p (b c) n", n=T), ACT.Silu
                       ).then_inc(M["silu"], 1)
        act_panel(act, e.count(3, NM + 2))
        act.wait_ge(M["hid"], e.count(1, 1).v())
        act.activation(hidH[:, :, :], hidf[:, :, :], ACT.Copy).then_inc(M["hH2"], 1)
        if not last:
            act_panel(act, e.count(3, NM + 3))
            act_panel(act, e.count(3, NM + 4))

    def moe_scalar(act):
        act_panel(act, Seq(NM + 1))
        expert_loop(act, moe_scalar_body)

    def moe_vector_acc(dve, e, last):
        dve.wait_ge(s_wdone, e.count(3, NM + (3 if last else 4)).v())
        for t in range(NT):
            g = (gate[:, t, e.c:e.c + 1] if e.i is None else gate[:, t, bass.ds(e.i * 2 + e.c, 1)])
            dve.scalar_tensor_tensor(out=accm[:, t, :],
                                     in0=psum[:, 4 + 2 * t:6 + 2 * t, :].rearrange("p b n -> p (b n)"),
                                     scalar=g, in1=accm[:, t, :], op0=ALU.mult, op1=ALU.add)
        dve.drain().then_inc(M["acc"], 1)

    def moe_vector_body(dve, e, last):
        dve_panel(dve, e.count(3, NM + 2))
        dve.wait_ge(s_wdone, e.count(3, NM + 2).v())
        dve.wait_ge(M["silu"], e.count(1, 1).v())
        dve.tensor_tensor(hidf[:, :, :], psum[:, 2:4, :].rearrange("p b (c n) -> p (b c) n", n=T),
                          sg[:, :, :], ALU.mult).then_inc(M["hid"], 1)
        dve.wait_ge(M["hH2"], e.count(1, 1).v())
        dve.tensor_tensor(hidL[:, :, :], hidf[:, :, :], hidH[:, :, :].bitcast(F32), ALU.subtract
                          ).then_inc(M["hL2"], 1)
        if not last:
            dve_panel(dve, e.count(3, NM + 3))
            dve_panel(dve, e.count(3, NM + 4))
        moe_vector_acc(dve, e, last)

    def moe_vector(dve):
        dve_panel(dve, Seq(NM + 1))
        expert_loop(dve, moe_vector_body)
        dve.wait_ge(M["v2_in"], 32)
        for t in range(NT):
            dve.tensor_tensor(accm[:, t, :], accm[:, t, :], mg5[:, :], ALU.mult)
            dve.drain()
            dve.tensor_tensor(xres[:, t, :], xres[:, t, :], accm[:, t, :], ALU.add)
        dve.drain().then_inc(M["x2"], 1)

    def moe_w1(pe, n, e_next):
        wh, wl = pe_panel(pe, n, KT)
        for c in range(4):
            i = feature_major(pe, psum[:, c // 2, T * (c % 2):T * (c % 2 + 1)], act2H, act2L, wh, wl, c, KT)
        i.then_inc(M["g"], 1)
        pe.drain().then_inc(s_wdone, 1)

    def moe_tensor_body(pe, e, last):
        wh, wl = pe_panel(pe, e.count(3, NM + 1), KT)
        for c in range(4):
            i = feature_major(pe, psum[:, 2 + c // 2, T * (c % 2):T * (c % 2 + 1)], act2H, act2L, wh, wl, c, KT)
        i.then_inc(s_wdone, 1)
        if not last:
            pe.wait_ge(M["silu"], e.count(1, 1).v())
            moe_w1(pe, e.count(3, NM + 2), e)
        wh, wl = pe_panel(pe, e.count(3, NM + (2 if last else 3)), 4)
        pe.wait_ge(M["hL2"], e.count(1, 1).v())
        pe.wait_ge(M["acc"], e.count(1, 1).v())
        for t in range(NT):
            for half in range(2):
                i = token_major(pe, psum[:, 4 + 2 * t + half, :], hidH, hidL, wh, wl, t, 4,
                                slice(PW * half, PW * (half + 1)))
        i.then_inc(s_wdone, 1)

    def moe_tensor(pe):
        moe_w1(pe, Seq(NM), None)
        expert_loop(pe, moe_tensor_body)

    NB = NM + 3 * E
    FF = a["w_up_2"].shape[2]
    NQ = FF // PW
    NW2 = ZW // PW
    J_OUT = NW2
    J_UP0 = J_OUT + 2
    J_GATE = J_UP0 + 2 * NQ
    J_PLE = J_GATE + 2
    LP = J_PLE + 1
    assert LP % 2 == 0 and NQ % 2 == 0
    z2 = Region(free_off, 20 * KB).take("z2", [P, NT, ZW])
    n3b = Region(free_off + 4 * KB, 4 * KB).take("n3b", [P, D])
    n2b = Region(free_off + 14 * KB, 4 * KB).take("n2b", [P, D])
    v2 = Region(free_off + 20 * KB, 5 * KB)
    n1b = v2.take("n1b", [P, D])
    pw = v2.take("pw", [P, 2, HD])
    psc = v2.take("psc", [P, 2])
    r1 = Region(free_off + 25 * KB, 24 * KB)
    qT2 = [r1.take("qT2_0", [P, H2 // 2, T]), Region(gap1, 8 * KB).take("qT2_1", [P, H2 // 2, T])]
    kT2 = r1.take("kT2", [P, H2 // 2, T])
    logit2 = r1.take("logit2", [P, 2, 2 * T])
    prob2 = r1.take("prob2", [P, 2, 2 * T])
    probT2 = r1.take("probT2", [P, 2, 4, P])
    r2 = Region(free_off + 25 * KB, 24 * KB)
    rel = r2.take("rel", [P, 4, T])
    sqf = r2.take("sqf", [P, 4, T])
    fH = r2.take("ff_high", [P, 4, T], F32R)
    fL = r2.take("ff_low", [P, 4, T], F32R)
    sg2 = r2.take("sg2", [P, NT, D])
    htok2 = Region(gap1, 8 * KB).take("htok2", [P, NT, D])
    g2 = Region(gap2, 8 * KB)
    ptok = g2.take("ptok", [P, NT, PLW])
    pTH = g2.take("pT_high", [P, 2, T], F32R)
    pTL = g2.take("pT_low", [P, 2, T], F32R)
    yT2 = g2.take("yT2", [P, 2, T])
    negm = stat[:, 0:24]
    mcol = stat[:, 24:48]
    l2 = stat[:, 48:72]
    lse = stat[:, 72:96]
    mx3 = stat[:, 96:104]
    e3 = stat[:, 104:128]
    sw = stat[:, 128:136]
    fac = stat[:, 136:160]
    n3st = stat[:, 160:176]

    B = {name: sem("b2_" + name) for name in (
        "n1_in", "n2_in", "n3_in", "pw_in", "p_in", "nf_in", 
        "z", "ze", "pT", "pH", "pL", "py", "pyE", "pf", "pfE", "rot", 
        "ln", "fmax", "fexp", "ao", "cT", "cH", "cL", "o", "oe", "rel", "sq", "fH",
        "fL", "ffe", "gt", "gs", "x3", "outh", "store")}

    def up_panel(d, c, *terms):
        return Seq(NB + J_UP0 + (0 if c == 0 else 2 * c - 1), (d, LP), *[(r, 2 * k) for r, k in terms])

    def down_panel(d, c, *terms):
        return Seq(NB + J_UP0 + 2 * c + 2, (d, LP), *[(r, 2 * k) for r, k in terms])

    def done(eng, d, name, count, j, c, t):
        if t == NT - 1:
            eng.wait_ge(s_wdone, Seq(NB + j + c + 1, (d, LP)).v())
        else:
            eng.wait_ge(B[name], lay(d, count, c + 1))

    def lay(d, k, c):
        return Seq(c, (d, k)).v()

    def row(name, d):
        return a[name][bass.ds(d, 1)].rearrange("a n -> (a n)").partition_broadcast(P)

    def layer_sync(sp):
        with sp.Fori(0, L2) as d:
            def src(name, rows=slice(None), cols=slice(None)):
                w = a[name][bass.ds(d, 1)].rearrange("a k n -> (a k) n")
                return w[rows, cols].rearrange("(k p) n -> p k n", p=P)

            def panel(j, s, *terms):
                sp_panel(sp, Seq(NB + j, (d, LP), *terms), s)

            for j in range(NW2):
                panel(j, src("w_in_2", cols=slice(PW * j, PW * (j + 1))))
            for j in range(2):
                panel(J_OUT + j, src("w_out_2", cols=slice(PW * j, PW * (j + 1))))

            def up(j, q, *terms):
                panel(j, src("w_up_2", cols=bass.ds(q * PW, PW)), *terms)

            def down(j, q, *terms):
                panel(j, src("w_down_2", rows=bass.ds(q * PW, PW)), *terms)

            up(J_UP0, 0)
            sp.wait_ge(B["cL"], lay(d, 4, 4))
            sp.dma_start(n2b[:, :], row("norm2_2", d)).then_inc(B["n2_in"], 16)
            sp.dma_start(n3b[:, :], row("norm3_2", d)).then_inc(B["n3_in"], 16)
            up(J_UP0 + 1, 1)
            down(J_UP0 + 2, 0)
            with sp.Fori(0, (NQ - 2) // 2) as i:
                for c in range(2):
                    up(J_UP0 + 3 + 2 * c, i * 2 + (2 + c), (i, 4))
                    down(J_UP0 + 4 + 2 * c, i * 2 + (1 + c), (i, 4))
            down(J_GATE - 1, NQ - 1)
            for j in range(2):
                panel(J_GATE + j, src("w_gate_2", cols=slice(PW * j, PW * (j + 1))))
            panel(J_PLE, src("w_ple_2"))
        sp.wait_ge(B["outh"], 1)
        sp.dma_start(out[0].rearrange("(t p) d -> p t d", p=P), htok2[:, :, :]).then_inc(B["store"], 16)
        sp.wait_ge(B["store"], 16)

    def layer_pool(pool):
        pool.wait_ge(M["x2"], 1)
        with pool.Fori(0, L2) as d:
            pool.dma_start(n1b[:, :], row("norm1_2", d)).then_inc(B["n1_in"], 16)
            for par in range(2):
                hs = slice(64 * par, 64 * par + 64)
                w = a["pool_w_2"][bass.ds(d, 1)].rearrange("a (h g) c n -> g c (a h) n", g=2)
                s = a["pool_scale_2"][bass.ds(d, 1)].rearrange("a (h g c n) -> g c (a h) n", g=2, h=2, n=1)
                pool.dma_start(pw[hs, :, :], w[par]).then_inc(B["pw_in"], 16)
                for c in range(2):
                    pool.dma_start(psc[hs, c:c + 1], s[par, :, c, :]).then_inc(B["pw_in"], 16)
            pool.dma_start(ptok[:, :, :], a["p_2"][bass.ds(d, 1)].rearrange("a o (t p) n -> p (a o t) n", p=P)
                           ).then_inc(B["p_in"], 16)
            pool.wait_ge(B["x3"], lay(d, 1, 1))
        pool.dma_start(n1b[:, :], a["final_norm_2"].partition_broadcast(P)).then_inc(B["nf_in"], 16)

    def norm_scalar(act, cnt1):
        for t in range(NT):
            act.activation(htok2[:, t, :], xres[:, t, :], ACT.Square, accum_out=n3st[:, t:t + 1])
        act.drain().then_inc(s_ssq, 1)
        act.wait_ge(s_var, 2 + cnt1)
        act.activation(n3st[:, 4:6], n3st[:, 2:4], ACT.Sqrt).then_inc(s_sqrt, 1)

    def norm_vector(dve, cnt1, gain):
        dve.wait_ge(s_ssq, 2 + cnt1)
        dve.tensor_scalar(n3st[:, 2:4], n3st[:, 0:2], 1.0 / D, EPS, ALU.mult, ALU.add).then_inc(s_var, 1)
        dve.wait_ge(s_sqrt, 2 + cnt1)
        dve.reciprocal(n3st[:, 6:8], n3st[:, 4:6])
        dve.drain()
        for t in range(NT):
            dve.scalar_tensor_tensor(out=htok2[:, t, :], in0=xres[:, t, :], scalar=n3st[:, 6 + t:7 + t],
                                     in1=gain[:, :], op0=ALU.mult, op1=ALU.mult).then_inc(s_h, 1)

    def split_scalar(act, d, k):
        for j in range(4):
            act.wait_ge(s_hT, lay(d, 12, NU_T + 4 + 4 * k + j + 1))
            act.activation(hdst(act2H, j), bank3(j), ACT.Copy).then_inc(s_hH, 1)

    def split_vector(dve, d, k):
        for j in range(4):
            dve.wait_ge(s_hH, lay(d, 12, NU_T + 4 + 4 * k + j + 1))
            dve.tensor_tensor(hdst(act2L, j), bank3(j), hdst(act2H, j).bitcast(F32), ALU.subtract
                              ).then_inc(s_hL, 1)

    def norm_tensor(pe, d, k):
        for j in range(4):
            t, half = j // 2, j % 2
            pe.wait_ge(s_h, lay(d, 6, NU_T // 2 + 2 + 2 * k + t + 1))
            for c in range(4):
                i = pe.transpose(psum[:, j, P * c:P * (c + 1)],
                                 htok2[:, t, P * (4 * half + c):P * (4 * half + c + 1)], ident[:, :])
            i.then_inc(s_hT, 1)
        pe.wait_ge(s_hL, lay(d, 12, NU_T + 4 + 4 * k + 4))

    def heads_of(w):
        t, g, par = w // 6, w % 6 // 2, w % 2
        return t, g, par, (4 * g + par, 4 * g + par + 2)

    def two(col, t, g, par):
        at = H2 * t + 4 * g + par
        return col[:, at:at + 3:2]

    def layer_scalar(act):
        act.wait_ge(M["x2"], 1)
        with act.Fori(0, L2) as d:
            def panel(j, *terms, elems=4096):
                act_panel(act, Seq(NB + j, (d, LP), *terms), elems)

            panel(0)
            norm_scalar(act, lay(d, 3, 1))
            split_scalar(act, d, 0)
            for j in range(NW2):
                panel(j + 1)
                for t in range(NT):
                    v = NT * j + t
                    done(act, d, "z", NW2, 0, j, t)
                    act.activation(z2[:, t, PW * j:PW * (j + 1)], psum[:, 4 + v % 4, :], ACT.Copy
                                   ).then_inc(B["ze"], 1)
            act.wait_ge(B["pT"], lay(d, 1, 1))
            act.activation(pTH[:, :, :], bank3(3, T), ACT.Copy).then_inc(B["pH"], 1)
            act.wait_ge(B["py"], lay(d, 1, 1))
            act.activation(yT2[:, :, :], bank3(0, T), ACT.Copy).then_inc(B["pyE"], 1)
            for b in range(6):
                act.wait_ge(s_qT, lay(d, 6, 3 * NT + b + 1))
                cs = slice(2 * (b % 3), 2 * (b % 3) + 2)
                if b < 3:
                    for par in range(2):
                        hs = slice(64 * par, 64 * par + 64)
                        act.activation(qT2[par][hs, cs, :], bank3(2 + b, T)[hs], ACT.Copy)
                    act.drain().then_inc(s_qTe, 1)
                else:
                    act.activation(kT2[:, cs, :], bank3(2 + b, T), ACT.Copy).then_inc(s_qTe, 1)
            for w in range(12):
                t, g, par, hh = heads_of(w)
                act.wait_ge(s_lg, lay(d, 12, NT * H + w + 1))
                if w >= 2:
                    act.wait_ge(s_pT, lay(d, 12, NT * H + w - 1))
                n = P * (t + 1)
                for x, h in enumerate(hh):
                    c = H2 * t + h
                    act.activation(prob2[:, w % 2, n * x:n * (x + 1)], logit2[:, w % 2, n * x:n * (x + 1)],
                                   ACT.Exp, bias=negm[:, c:c + 1], accum_out=l2[:, c:c + 1])
                act.drain().then_inc(s_ex, 1)
            act.activation(lse, l2, ACT.Ln).then_inc(B["ln"], 1)
            act.wait_ge(B["fmax"], lay(d, 1, 1))
            act.activation(e3, e3, ACT.Exp).then_inc(B["fexp"], 1)
            act.wait_ge(B["pf"], lay(d, 1, 1))
            act.activation(act2H[:, 0:2, :], z2[:, :, 0:PLW], ACT.Copy).then_inc(B["cH"], 1)
            for b in range(3):
                act.wait_ge(B["cT"], lay(d, 3, b + 1))
                act.activation(act2H[:, 2 + 2 * b:4 + 2 * b, :], bank3(b, T), ACT.Copy).then_inc(B["cH"], 1)
            panel(J_OUT + 1)
            panel(J_UP0)
            act.wait_ge(B["oe"], lay(d, 4, 4))
            norm_scalar(act, lay(d, 3, 2))
            panel(J_UP0 + 1)
            split_scalar(act, d, 1)

            def relu(c, *terms):
                act.wait_ge(s_wdone, up_panel(d, c, *terms).v(1))
                b = 2 * (c % 2)
                act.activation(rel[:, :, :], psum[:, b:b + 2, :].rearrange("p b (c n) -> p (b c) n", n=T),
                               ACT.Relu).then_inc(B["rel"], 1)

            def high(c, *terms, first=False):
                act.wait_ge(B["sq"], Seq(c + 1, (d, NQ), *terms).v())
                if not first:
                    act.wait_ge(s_wdone, down_panel(d, c - 1, *terms).v(1))
                act.activation(fH[:, :, :], sqf[:, :, :], ACT.Copy).then_inc(B["fH"], 1)

            relu(0)
            high(0, first=True)
            panel(J_UP0 + 2)
            relu(1)
            panel(J_UP0 + 3)
            with act.Fori(0, (NQ - 2) // 2) as i:
                for c in range(2):
                    high(1 + c, (i, 2))
                    panel(J_UP0 + 4 + 2 * c, (i, 4))
                    relu(2 + c, (i, 2))
                    panel(J_UP0 + 5 + 2 * c, (i, 4))
            high(NQ - 1)
            panel(J_GATE)
            act.wait_ge(B["ffe"], lay(d, 1, 1))
            norm_scalar(act, lay(d, 3, 3))
            split_scalar(act, d, 2)
            panel(J_GATE + 1)
            for c in range(2):
                for t in range(NT):
                    done(act, d, "gt", 2, J_GATE, c, t)
                    act.activation(sg2[:, t, PW * c:PW * (c + 1)], psum[:, 2 * c + t, :], ACT.Sigmoid
                                   ).then_inc(B["gs"], 1)
                if c == 0:
                    panel(J_PLE, elems=PLW // P * D)
            act.wait_ge(B["x3"], lay(d, 1, 1))
        norm_scalar(act, 3 * L2 + 1)

    def layer_vector(dve):
        dve.wait_ge(C["done"], 1)
        with dve.Fori(0, L2) as d:
            def panel(j, *terms, elems=4096):
                dve_panel(dve, Seq(NB + j, (d, LP), *terms), elems)

            panel(0)
            dve.wait_ge(B["n1_in"], lay(d, 16, 16))
            norm_vector(dve, lay(d, 3, 1), n1b)
            split_vector(dve, d, 0)
            for j in range(NW2):
                panel(j + 1)
            dve.wait_ge(B["ze"], lay(d, 10, 10))
            dve.wait_ge(B["pH"], lay(d, 1, 1))
            dve.tensor_tensor(pTL[:, :, :], bank3(3, T), pTH[:, :, :].bitcast(F32), ALU.subtract
                              ).then_inc(B["pL"], 1)
            for t in range(NT):
                qk = z2[:, t, PLW:PLW + 2 * AW].rearrange("p (h d) -> p h d", d=HD)
                x1, x2 = qk[:, :, 0:RH], qk[:, :, RH:2 * RH]
                co, si = (cs_t[:, i, t, :].unsqueeze(1).to_broadcast([P, 2 * H2, RH]) for i in range(2))
                tmp = [htok2[:, t, 2 * H2 * RH * i:2 * H2 * RH * (i + 1)].rearrange("p (h r) -> p h r", r=RH)
                       for i in range(4)]
                dve.tensor_tensor(tmp[0], x1, co, ALU.mult)
                dve.tensor_tensor(tmp[1], x2, si, ALU.mult)
                dve.tensor_tensor(tmp[2], x2, co, ALU.mult)
                dve.tensor_tensor(tmp[3], x1, si, ALU.mult)
                dve.drain()
                dve.tensor_tensor(x1, tmp[0], tmp[1], ALU.subtract)
                dve.tensor_tensor(x2, tmp[2], tmp[3], ALU.add)
            dve.drain().then_inc(B["rot"], 1)
            dve.memset(qT2[0][64:128, :, :], 0.0)
            dve.memset(qT2[1][0:64, :, :], 0.0)
            dve.wait_ge(B["pfE"], lay(d, 1, 1))
            for c in range(2):
                dve.tensor_scalar(z2[:, c, 0:PLW], psum[:, 1, T * c:T * (c + 1)], psc[:, c:c + 1], None, ALU.mult)
            dve.drain().then_inc(B["pf"], 1)
            for w in range(13):
                if w < 12:
                    t, g, par, hh = heads_of(w)
                    n = P * (t + 1)
                    dve.wait_ge(s_S, lay(d, 12, NT * H + w + 1))
                    lg = logit2[:, w % 2, 0:2 * n].rearrange("p (h n) -> p h n", h=2)
                    k = slice(0, P) if t == 0 else slice(P, 3 * P)
                    dve.scalar_tensor_tensor(out=lg,
                                             in0=psum[:, w % 2, 0:2 * n].rearrange("p (h n) -> p h n", h=2),
                                             scalar=HD ** -0.5,
                                             in1=cmask[:, g, k].unsqueeze(1).to_broadcast([P, 2, n]),
                                             op0=ALU.mult, op1=ALU.add)
                    dve.drain()
                    dve.tensor_reduce(two(mcol, t, g, par), lg, AX, ALU.max)
                    dve.drain()
                    dve.tensor_scalar(two(negm, t, g, par), two(mcol, t, g, par), -1.0, None, ALU.mult)
                    dve.drain().then_inc(s_lg, 1)
                if w >= 1:
                    j = w - 1
                    n = P * (j // 6 + 1)
                    dve.wait_ge(s_pT, lay(d, 12, NT * H + j + 1))
                    if j >= 2:
                        dve.wait_ge(s_pv, lay(d, 12, NT * H + j - 1))
                    dve.tensor_copy(probT2[:, j % 2, 0:2 * n // P, :], bank3(2 + j % 2)[:, 0:2 * n // P, :]
                                    ).then_inc(s_pTe, 1)
            dve.wait_ge(B["ln"], lay(d, 1, 1))
            dve.tensor_tensor(lse, lse, mcol, ALU.add)
            dve.reciprocal(l2, l2)
            dve.drain()
            by_g = lambda x: x.rearrange("p (t g j) -> p t j g", t=NT, g=3)
            view = lambda x: x.rearrange("p (t j) -> p t j", t=NT)
            dve.tensor_reduce(view(mx3), by_g(lse), AX, ALU.max)
            dve.drain()
            for t in range(NT):
                dve.tensor_tensor(e3[:, H2 * t:H2 * (t + 1)].rearrange("p (g j) -> p g j", g=3),
                                  lse[:, H2 * t:H2 * (t + 1)].rearrange("p (g j) -> p g j", g=3),
                                  mx3[:, 4 * t:4 * t + 4].unsqueeze(1).to_broadcast([P, 3, 4]), ALU.subtract)
            dve.drain().then_inc(B["fmax"], 1)
            dve.wait_ge(B["fexp"], lay(d, 1, 1))
            dve.tensor_reduce(view(sw), by_g(e3), AX, ALU.add)
            dve.drain()
            dve.tensor_tensor(e3, e3, l2, ALU.mult)
            dve.drain()
            dve.reciprocal(sw, sw)
            dve.drain()
            for t in range(NT):
                dve.tensor_tensor(fac[:, H2 * t:H2 * (t + 1)].rearrange("p (g j) -> p g j", g=3),
                                  e3[:, H2 * t:H2 * (t + 1)].rearrange("p (g j) -> p g j", g=3),
                                  sw[:, 4 * t:4 * t + 4].unsqueeze(1).to_broadcast([P, 3, 4]), ALU.mult)
            dve.drain()
            dve.wait_ge(s_pv, lay(d, 12, NT * H + 12))
            for t in range(NT):
                ao = z2[:, t, PLW:PLW + AW].rearrange("p (h d) -> p h d", d=HD)
                dve.tensor_tensor(ao[:, 0:8, :], bank3(4 + 2 * t, HD), bc(fac[:, H2 * t:H2 * t + 8], HD), ALU.mult)
                dve.tensor_tensor(ao[:, 8:12, :], bank3(5 + 2 * t, HD)[:, 0:4, :],
                                  bc(fac[:, H2 * t + 8:H2 * t + 12], HD), ALU.mult)
            dve.drain().then_inc(B["ao"], 1)
            dve.wait_ge(B["cH"], lay(d, 4, 1))
            dve.tensor_tensor(act2L[:, 0:2, :], z2[:, :, 0:PLW], act2H[:, 0:2, :].bitcast(F32), ALU.subtract
                              ).then_inc(B["cL"], 1)
            for b in range(3):
                dve.wait_ge(B["cH"], lay(d, 4, b + 2))
                cs = slice(2 + 2 * b, 4 + 2 * b)
                dve.tensor_tensor(act2L[:, cs, :], bank3(b, T), act2H[:, cs, :].bitcast(F32), ALU.subtract
                                  ).then_inc(B["cL"], 1)
            panel(J_OUT + 1)
            for c in range(2):
                if c == 1:
                    panel(J_UP0)
                for t in range(NT):
                    done(dve, d, "o", 2, J_OUT, c, t)
                    cs = slice(PW * c, PW * (c + 1))
                    dve.tensor_tensor(xres[:, t, cs], xres[:, t, cs], psum[:, 4 + 2 * c + t, :], ALU.add)
                    dve.drain().then_inc(B["oe"], 1)
            dve.wait_ge(B["n2_in"], lay(d, 16, 16))
            norm_vector(dve, lay(d, 3, 2), n2b)
            panel(J_UP0 + 1)
            split_vector(dve, d, 1)

            def square(c, *terms):
                dve.wait_ge(B["rel"], Seq(c + 1, (d, NQ), *terms).v())
                dve.tensor_tensor(sqf[:, :, :], rel[:, :, :], rel[:, :, :], ALU.mult).then_inc(B["sq"], 1)

            def low(c, *terms):
                dve.wait_ge(B["fH"], Seq(c + 1, (d, NQ), *terms).v())
                dve.tensor_tensor(fL[:, :, :], sqf[:, :, :], fH[:, :, :].bitcast(F32), ALU.subtract
                                  ).then_inc(B["fL"], 1)
                dve.drain()

            square(0)
            low(0)
            panel(J_UP0 + 2)
            square(1)
            panel(J_UP0 + 3)
            with dve.Fori(0, (NQ - 2) // 2) as i:
                for c in range(2):
                    low(1 + c, (i, 2))
                    panel(J_UP0 + 4 + 2 * c, (i, 4))
                    square(2 + c, (i, 2))
                    panel(J_UP0 + 5 + 2 * c, (i, 4))
            low(NQ - 1)
            panel(J_GATE)
            dve.wait_ge(s_wdone, Seq(NB + J_GATE, (d, LP)).v())
            for t in range(NT):
                dve.tensor_tensor(xres[:, t, :], xres[:, t, :],
                                  psum[:, 4 + 2 * t:6 + 2 * t, :].rearrange("p b n -> p (b n)"), ALU.add)
            dve.drain().then_inc(B["ffe"], 1)
            dve.wait_ge(B["n3_in"], lay(d, 16, 16))
            norm_vector(dve, lay(d, 3, 3), n3b)
            split_vector(dve, d, 2)
            panel(J_GATE + 1)
            panel(J_PLE, elems=PLW // P * D)
            dve.wait_ge(B["gs"], lay(d, 4, 4))
            dve.wait_ge(s_wdone, Seq(NB + J_PLE + 1, (d, LP)).v())
            for t in range(NT):
                dve.tensor_tensor(sg2[:, t, :], psum[:, 4 + 2 * t:6 + 2 * t, :].rearrange("p b n -> p (b n)"),
                                  sg2[:, t, :], ALU.mult)
            dve.drain()
            for t in range(NT):
                dve.tensor_tensor(xres[:, t, :], xres[:, t, :], sg2[:, t, :], ALU.add)
            dve.drain().then_inc(B["x3"], 1)
        dve.wait_ge(B["nf_in"], 16)
        norm_vector(dve, 3 * L2 + 1, n1b)
        dve.drain().then_inc(B["outh"], 1)

    def layer_tensor(pe):
        pe.wait_ge(C["done"], 1)
        with pe.Fori(0, L2) as d:
            def panel(j, k, *terms):
                return pe_panel(pe, Seq(NB + j, (d, LP), *terms), k)

            def signal(name, t):
                return s_wdone if t == NT - 1 else B[name]

            norm_tensor(pe, d, 0)
            for j in range(NW2):
                wh, wl = panel(j, KT)
                for t in range(NT):
                    v = NT * j + t
                    if v >= 4:
                        pe.wait_ge(B["ze"], lay(d, 10, v - 3))
                    token_major(pe, psum[:, 4 + v % 4, :], act2H, act2L, wh, wl, t, KT).then_inc(signal("z", t), 1)
            pe.wait_ge(B["p_in"], lay(d, 16, 16))
            for k in range(2):
                for t in range(NT):
                    i = pe.transpose(psum[:, 3, T * k + P * t:T * k + P * (t + 1)], ptok[:, t, P * k:P * (k + 1)],
                                     ident[:, :])
            i.then_inc(B["pT"], 1)
            pe.wait_ge(B["ze"], lay(d, 10, 10))
            pe.wait_ge(B["pw_in"], lay(d, 96, 96))
            for g in range(4):
                for st in range(NT):
                    i = pe.matmul(psum[64 * (g % 2):64 * (g % 2) + 64, 0, T * (g // 2):T * (g // 2 + 1)],
                                  z2[:, st, HD * g:HD * (g + 1)], band[:, g, st, :], start=(st == 0),
                                  stop=(st == NT - 1))
            i.then_inc(B["py"], 1)
            pe.wait_ge(B["rot"], lay(d, 1, 1))
            pe.wait_ge(B["pL"], lay(d, 1, 1))
            pe.wait_ge(B["pyE"], lay(d, 1, 1))
            for b in range(6):
                for x in range(2):
                    at = PLW + AW * (b // 3) + P * (2 * (b % 3) + x)
                    for t in range(NT):
                        i = pe.transpose(psum[:, 2 + b, T * x + P * t:T * x + P * (t + 1)], z2[:, t, at:at + P],
                                         ident[:, :])
                i.then_inc(s_qT, 1)
            for g in range(4):
                hs = slice(64 * (g % 2), 64 * (g % 2) + 64)
                i = pe.matmul(psum[hs, 1, T * (g // 2):T * (g // 2 + 1)], pw[hs, g // 2, :], yT2[hs, g // 2, :],
                              start=True, stop=True)
            pe.drain().then_inc(B["pfE"], 1)
            for w in range(14):
                if w < 12:
                    t, g, par, hh = heads_of(w)
                    n = P * (t + 1)
                    if w == 0:
                        pe.wait_ge(s_qTe, lay(d, 6, 3 * NT + 6))
                        pe.wait_ge(B["pf"], lay(d, 1, 1))
                    if w >= 2:
                        pe.wait_ge(s_lg, lay(d, 12, NT * H + w - 1))
                    for x, h in enumerate(hh):
                        i = pe.matmul(psum[:, w % 2, n * x:n * (x + 1)], qT2[par][:, h // 2, P * t:P * (t + 1)],
                                      kT2[:, h // 2, 0:n], start=True, stop=True)
                    i.then_inc(s_S, 1)
                if 1 <= w <= 12:
                    j = w - 1
                    n = P * (j // 6 + 1)
                    pe.wait_ge(s_ex, lay(d, 12, NT * H + j + 1))
                    if j >= 2:
                        pe.wait_ge(s_pTe, lay(d, 12, NT * H + j - 1))
                    for c in range(2 * n // P):
                        i = pe.transpose(psum[:, 2 + j % 2, P * c:P * (c + 1)], prob2[:, j % 2, P * c:P * (c + 1)],
                                         ident[:, :])
                    i.then_inc(s_pT, 1)
                if w >= 2:
                    j = w - 2
                    t, g, par, hh = heads_of(j)
                    pe.wait_ge(s_pTe, lay(d, 12, NT * H + j + 1))
                    for x, h in enumerate(hh):
                        o = psum[:, 4 + 2 * t + h // 8, HD * (h % 8):HD * (h % 8 + 1)]
                        for k in range(t + 1):
                            at = PLW + 2 * AW + HD * h
                            i = pe.matmul(o, probT2[:, j % 2, (t + 1) * x + k, :], z2[:, k, at:at + HD],
                                          start=(k == 0), stop=(k == t))
                    i.then_inc(s_pv, 1)
            pe.wait_ge(B["ao"], lay(d, 1, 1))
            for b in range(3):
                for x in range(2):
                    at = PLW + P * (2 * b + x)
                    for t in range(NT):
                        i = pe.transpose(psum[:, b, T * x + P * t:T * x + P * (t + 1)], z2[:, t, at:at + P],
                                         ident[:, :])
                i.then_inc(B["cT"], 1)
            pe.wait_ge(B["cL"], lay(d, 4, 4))
            for c in range(2):
                wh, wl = panel(J_OUT + c, KT)
                for t in range(NT):
                    token_major(pe, psum[:, 4 + 2 * c + t, :], act2H, act2L, wh, wl, t, KT
                                ).then_inc(signal("o", t), 1)
            norm_tensor(pe, d, 1)

            def up(c, *terms):
                pt = [(r, 2 * k) for r, k in terms]
                wh, wl = panel(J_UP0 + (0 if c == 0 else 2 * c - 1), KT, *pt)
                if c >= 2:
                    pe.wait_ge(B["rel"], Seq(c - 1, (d, NQ), *terms).v())
                for j in range(4):
                    o = psum[:, 2 * (c % 2) + j // 2, T * (j % 2):T * (j % 2 + 1)]
                    i = feature_major(pe, o, act2H, act2L, wh, wl, j, KT)
                i.then_inc(s_wdone, 1)

            def down(c, *terms):
                pt = [(r, 2 * k) for r, k in terms]
                wh, wl = panel(J_GATE - 1 if c == NQ - 1 else J_UP0 + 2 * c + 2, 4, *pt)
                pe.wait_ge(B["fL"], Seq(c + 1, (d, NQ), *terms).v())
                for t in range(NT):
                    for half in range(2):
                        i = token_major(pe, psum[:, 4 + 2 * t + half, :], fH, fL, wh, wl, t, 4,
                                        slice(PW * half, PW * (half + 1)), start=(c == 0 and not terms),
                                        stop=(c == NQ - 1))
                i.then_inc(s_wdone, 1)

            up(0)
            up(1)
            down(0)
            with pe.Fori(0, (NQ - 2) // 2) as i_q:
                for c in range(2):
                    up(2 + c, (i_q, 2))
                    down(1 + c, (i_q, 2))
            down(NQ - 1)
            norm_tensor(pe, d, 2)
            for c in range(2):
                wh, wl = panel(J_GATE + c, KT)
                for t in range(NT):
                    token_major(pe, psum[:, 2 * c + t, :], act2H, act2L, wh, wl, t, KT
                                ).then_inc(signal("gt", t), 1)
            wh, wl = panel(J_PLE, 4)
            pw_h = WH[(NB + J_PLE) % 2][:, 0:PLW // P * D].rearrange("p (k n) -> p k n", n=D)
            pw_l = WL[(NB + J_PLE) % 2][:, 0:PLW // P * D].rearrange("p (k n) -> p k n", n=D)
            for t in range(NT):
                for half in range(2):
                    i = token_major(pe, psum[:, 4 + 2 * t + half, :], pTH, pTL, pw_h, pw_l, t, PLW // P,
                                    slice(PW * half, PW * (half + 1)))
            i.then_inc(s_wdone, 1)

    block = ctx.enter_context(nc.Block())

    @block.sync
    def _(sp):
        front_sync(sp)
        att_sync(sp)
        merge_sync(sp)
        moe_sync(sp)
        layer_sync(sp)

    @block.gpsimd
    def _(pool):
        front_pool(pool)
        att_pool(pool)
        rwkv_pool(pool)
        merge_pool(pool)
        const2_pool(pool)
        layer_pool(pool)

    @block.scalar
    def _(act):
        front_scalar(act)
        att_scalar(act)
        rwkv_scalar(act)
        merge_scalar(act)
        route_scalar(act)
        const2_scalar(act)
        moe_scalar(act)
        layer_scalar(act)

    @block.vector
    def _(dve):
        front_vector(dve)
        att_vector(dve)
        rwkv_vector(dve)
        merge_vector(dve)
        route_vector(dve)
        const2_vector(dve)
        moe_vector(dve)
        layer_vector(dve)

    @block.tensor
    def _(pe):
        front_tensor(pe)
        att_tensor(pe)
        rwkv_tensor(pe)
        merge_tensor(pe)
        route_tensor(pe)
        moe_tensor(pe)
        layer_tensor(pe)

    ctx.close()


_INS = ("x", "c", "ctx", "c_ctx", "mod_w", "mod_b", "norm1_g", "norm2_g", "w_in", "rw_w0", "rw_w_lora_b", "rw_a0",
        "rw_a_lora_b", "rw_g_lora_b", "rw_k_k", "rw_k_a", "rw_r_k", "rw_ln_g", "rw_ln_b", "na_q_g", "na_k_g",
        "na_rpb", "proj_a", "proj_b", "w_out", "router_w", "router_bias", "moe_w1", "moe_w3", "moe_w2", "p_2",
        "positions_2", "norm1_2", "w_in_2", "pool_w_2", "pool_scale_2", "w_out_2", "norm2_2", "w_up_2",
        "w_down_2", "norm3_2", "w_gate_2", "w_ple_2", "final_norm_2")


def kernel(**inputs):
    import numpy as _np
    import concourse.bacc as _bacc
    from concourse import mybir as _mybir
    from concourse.bass_utils import run_bass_kernel_spmd as _run

    nc = _bacc.Bacc("TRN2", target_bir_lowering=False, num_devices=1)
    arrays, aps = {}, {}
    for name in _INS:
        v = _np.ascontiguousarray(inputs[name])
        arrays[f"in_{name}_dram"] = v
        aps[name] = nc.dram_tensor(f"in_{name}_dram", v.shape, _mybir.dt.from_np(v.dtype),
                                   kind="ExternalInput").ap()
    out = nc.dram_tensor("out_0_dram", inputs["x"].shape, _mybir.dt.from_np(_np.dtype("float32")),
                         kind="ExternalOutput").ap()
    two_block_kernel(nc, aps, out)
    r = _run(nc, [arrays], core_ids=[0])
    return r.results[0]["out_0_dram"]
```
